# Optimizing a Trainium2 kernel written in Bass

```python
import math
import jax, jax.numpy as jnp
from jax import lax
import numpy as np

D_MODEL = 1024
BATCH = 1
SEQ = 256
DEPTH = 2

N_MIXERS = 2
N_POOL_LAYERS = (DEPTH + 1) // 2
N_GDN_LAYERS = DEPTH // 2
PLE_DIM = 256
D_FF = 4 * D_MODEL
POOL_WINDOWS = (2, 4, 8, 16)
N_POOL_GROUPS = len(POOL_WINDOWS)
POOL_GROUP = D_MODEL // N_POOL_GROUPS
GDN_HEADS = 8
GDN_HEAD_DIM = 128
GDN_KEY_DIM = GDN_HEADS * GDN_HEAD_DIM
GDN_VAL_DIM = GDN_HEADS * GDN_HEAD_DIM
GDN_CONV_DIM = 2 * GDN_KEY_DIM + GDN_VAL_DIM
GDN_IN_DIM = GDN_CONV_DIM + GDN_VAL_DIM + 2 * GDN_HEADS
CONV_WIDTH = 4
CHUNK = 64
DEEPNORM_ALPHA = (2.0 * DEPTH) ** 0.25
DEEPNORM_BETA = (8.0 * DEPTH) ** -0.25
LN_EPS = 1e-5
RMS_EPS = 1e-6
L2_EPS = 1e-6


def layer_norm(x, g, b):
    xf = x.astype(jnp.float32)
    mu = jnp.mean(xf, axis=-1, keepdims=True)
    var = jnp.mean(jnp.square(xf - mu), axis=-1, keepdims=True)
    return ((xf - mu) * lax.rsqrt(var + LN_EPS) * g + b).astype(x.dtype)

def pool_mixer(x, w_grp, b_grp, scale):
    B, S, _ = x.shape
    xg = x.astype(jnp.float32).reshape(B, S, N_POOL_GROUPS, POOL_GROUP)
    cs = jnp.cumsum(xg, axis=1)
    pos = jnp.arange(1, S + 1, dtype=jnp.float32)[None, :, None]
    outs = []
    for gi, w in enumerate(POOL_WINDOWS):
        c = cs[:, :, gi]
        c_prev = jnp.pad(c, ((0, 0), (w, 0), (0, 0)))[:, :S]
        mean = (c - c_prev) / jnp.minimum(pos, float(w))
        outs.append(mean - xg[:, :, gi])
    pooled = jnp.stack(outs, axis=2).astype(x.dtype)
    y = jnp.einsum('bsgc,gcd->bsgd', pooled, w_grp) + b_grp
    return y.reshape(B, S, D_MODEL) * scale

def causal_depthwise_conv(x, w):
    C = x.shape[-1]
    return lax.conv_general_dilated(
        x, w[:, None, :].astype(x.dtype), window_strides=(1,),
        padding=[(CONV_WIDTH - 1, 0)], dimension_numbers=('NWC', 'WIO', 'NWC'),
        feature_group_count=C)

def l2_normalize(t):
    return t * lax.rsqrt(jnp.sum(jnp.square(t), axis=-1, keepdims=True) + L2_EPS)

def chunk_gated_delta_rule(q, k, v, g, beta):
    B, S, H, Dk = q.shape
    Dv = v.shape[-1]
    N = S // CHUNK

    def to_chunks(t):
        return t.reshape(B, N, CHUNK, H, -1).transpose(0, 3, 1, 2, 4)

    q, k, v = to_chunks(q), to_chunks(k), to_chunks(v)
    g = g.reshape(B, N, CHUNK, H).transpose(0, 3, 1, 2)
    beta = beta.reshape(B, N, CHUNK, H).transpose(0, 3, 1, 2)
    g = jnp.cumsum(g, axis=-1)

    idx = jnp.arange(CHUNK)
    causal = idx[:, None] >= idx[None, :]
    strict = idx[:, None] > idx[None, :]
    decay = jnp.exp(jnp.where(causal, g[..., :, None] - g[..., None, :], -jnp.inf))

    k_beta = k * beta[..., None]
    a = jnp.einsum('bhncd,bhnmd->bhncm', k_beta, k) * decay
    m = jnp.where(strict, a, 0.0) + jnp.eye(CHUNK, dtype=jnp.float32)
    rhs = jnp.concatenate([v * beta[..., None], k_beta * jnp.exp(g)[..., None]], axis=-1)
    sol = lax.linalg.triangular_solve(m, rhs, left_side=True, lower=True, unit_diagonal=True)
    u, w = sol[..., :Dv], sol[..., Dv:]

    qk = jnp.einsum('bhncd,bhnmd->bhncm', q, k) * decay
    q_dec = q * jnp.exp(g)[..., None]
    k_dec = k * jnp.exp(g[..., -1:] - g)[..., None]
    g_last = jnp.exp(g[..., -1])

    def step(state, xs):
        u_c, w_c, qk_c, qd_c, kd_c, gl_c = xs
        v_new = u_c - jnp.einsum('bhcd,bhde->bhce', w_c, state)
        o_c = (jnp.einsum('bhcd,bhde->bhce', qd_c, state)
               + jnp.einsum('bhcm,bhme->bhce', qk_c, v_new))
        state = state * gl_c[..., None, None] + jnp.einsum('bhcd,bhce->bhde', kd_c, v_new)
        return state, o_c

    xs = tuple(jnp.moveaxis(t, 2, 0) for t in (u, w, qk, q_dec, k_dec, g_last))
    s0 = jnp.zeros((B, H, Dk, Dv), jnp.float32)
    _, o = lax.scan(step, s0, xs)
    return o.transpose(1, 0, 3, 2, 4).reshape(B, S, H, Dv)

def gated_deltanet(x, w_in, conv_w, a_log, dt_bias, norm_w, w_out):
    B, S, _ = x.shape
    H, Dh = GDN_HEADS, GDN_HEAD_DIM
    proj = x @ w_in
    qkv, z, b_logit, a_logit = jnp.split(
        proj, [GDN_CONV_DIM, GDN_CONV_DIM + GDN_VAL_DIM, GDN_CONV_DIM + GDN_VAL_DIM + H], axis=-1)
    qkv = jax.nn.silu(causal_depthwise_conv(qkv, conv_w))
    q, k, v = jnp.split(qkv, [GDN_KEY_DIM, 2 * GDN_KEY_DIM], axis=-1)
    q = l2_normalize(q.reshape(B, S, H, Dh).astype(jnp.float32)) * (Dh ** -0.5)
    k = l2_normalize(k.reshape(B, S, H, Dh).astype(jnp.float32))
    v = v.reshape(B, S, H, Dh).astype(jnp.float32)
    beta = jax.nn.sigmoid(b_logit.astype(jnp.float32))
    g = -jnp.exp(a_log.astype(jnp.float32)) * jax.nn.softplus(
        a_logit.astype(jnp.float32) + dt_bias.astype(jnp.float32))
    o = chunk_gated_delta_rule(q, k, v, g, beta)
    zf = z.reshape(B, S, H, Dh).astype(jnp.float32)
    o = o * lax.rsqrt(jnp.mean(jnp.square(o), axis=-1, keepdims=True) + RMS_EPS) * norm_w * jax.nn.silu(zf)
    return o.reshape(B, S, GDN_VAL_DIM).astype(x.dtype) @ w_out

def squared_relu_mlp(x, w1, w2):
    return jnp.square(jax.nn.relu(x @ w1)) @ w2

def first_inputs(seed: int = 0) -> dict:
    key = jax.random.key(seed)
    ks = jax.random.split(key, 20)
    f32 = jnp.float32
    nrm = lambda k, s: jax.random.normal(k, s, f32)
    dt = jnp.exp(jax.random.uniform(ks[9], (N_GDN_LAYERS, GDN_HEADS), f32,
                                    math.log(1e-3), math.log(1e-1)))
    return {
        "x": nrm(ks[0], (BATCH, SEQ, D_MODEL)),
        "p": nrm(ks[1], (DEPTH, BATCH, SEQ, PLE_DIM)),
        "ln_gain": 1.0 + 0.02 * nrm(ks[2], (DEPTH, 2, D_MODEL)),
        "ln_bias": 0.02 * nrm(ks[3], (DEPTH, 2, D_MODEL)),
        "pool_w": nrm(ks[4], (N_POOL_LAYERS, N_POOL_GROUPS, POOL_GROUP, POOL_GROUP)) * (POOL_GROUP ** -0.5) * DEEPNORM_BETA,
        "pool_b": 0.02 * nrm(ks[5], (N_POOL_LAYERS, N_POOL_GROUPS, POOL_GROUP)),
        "pool_scale": 1.0 + 0.1 * nrm(ks[6], (N_POOL_LAYERS, D_MODEL)),
        "gdn_w_in": nrm(ks[7], (N_GDN_LAYERS, D_MODEL, GDN_IN_DIM)) * (D_MODEL ** -0.5),
        "gdn_conv": nrm(ks[8], (N_GDN_LAYERS, CONV_WIDTH, GDN_CONV_DIM)) * (CONV_WIDTH ** -0.5),
        "gdn_a_log": jnp.log(jax.random.uniform(ks[10], (N_GDN_LAYERS, GDN_HEADS), f32, 1.0, 16.0)),
        "gdn_dt_bias": dt + jnp.log(-jnp.expm1(-dt)),
        "gdn_norm_w": 1.0 + 0.02 * nrm(ks[11], (N_GDN_LAYERS, GDN_HEAD_DIM)),
        "gdn_w_out": nrm(ks[12], (N_GDN_LAYERS, GDN_VAL_DIM, D_MODEL)) * (GDN_VAL_DIM ** -0.5) * DEEPNORM_BETA,
        "mlp_w1": nrm(ks[13], (DEPTH, D_MODEL, D_FF)) * (D_MODEL ** -0.5),
        "mlp_w2": nrm(ks[14], (DEPTH, D_FF, D_MODEL)) * (D_FF ** -0.5) * DEEPNORM_BETA,
        "ple_gate_w": nrm(ks[15], (DEPTH, D_MODEL, D_MODEL)) * (D_MODEL ** -0.5),
        "ple_gate_b": 0.02 * nrm(ks[16], (DEPTH, D_MODEL)),
        "ple_proj": nrm(ks[17], (DEPTH, PLE_DIM, D_MODEL)) * (PLE_DIM ** -0.5),
    }

def first_block(x, p, ln_gain, ln_bias, pool_w, pool_b, pool_scale, gdn_w_in, gdn_conv,
              gdn_a_log, gdn_dt_bias, gdn_norm_w, gdn_w_out, mlp_w1, mlp_w2,
              ple_gate_w, ple_gate_b, ple_proj):
    for i in range(DEPTH):
        j = i // N_MIXERS
        if i % N_MIXERS == 0:
            mix = pool_mixer(x, pool_w[j], pool_b[j], pool_scale[j])
        else:
            mix = gated_deltanet(x, gdn_w_in[j], gdn_conv[j], gdn_a_log[j], gdn_dt_bias[j],
                                 gdn_norm_w[j], gdn_w_out[j])
        x = layer_norm(DEEPNORM_ALPHA * x + mix, ln_gain[i, 0], ln_bias[i, 0])
        ff = squared_relu_mlp(x, mlp_w1[i], mlp_w2[i])
        pe = jax.nn.sigmoid(x @ ple_gate_w[i] + ple_gate_b[i]) * (p[i] @ ple_proj[i])
        x = layer_norm(DEEPNORM_ALPHA * x + ff + pe, ln_gain[i, 1], ln_bias[i, 1])
    return x


DEPTH_2 = 1

HEAD_DIM = 64
N_NSA_HEADS = 8
N_NSA_KV = 2
NSA_GROUP = N_NSA_HEADS // N_NSA_KV
N_FOX_HEADS = 8
D_NSA = N_NSA_HEADS * HEAD_DIM
D_FOX = N_FOX_HEADS * HEAD_DIM
D_MIX = D_NSA + D_FOX
D_KV = N_NSA_KV * HEAD_DIM
D_PROJ = D_NSA + 6 * D_KV + 3 * N_NSA_HEADS + 3 * D_FOX + N_FOX_HEADS
CMP_BLOCK = 32
CMP_STRIDE = 16
CMP_HIDDEN = 128
SEL_BLOCK = 64
SEL_TOPK = 16
WINDOW = 512
Q_BLOCK = 128
N_EXPERTS = 32
TOP_K = 4
D_FF_2 = D_MODEL
SWIGLU_LIMIT = 7.0
SWIGLU_ALPHA = 1.702
EPS = 1e-6
NEG = -1e30
FORCED_SCORE = 1e9


def rmsnorm(x, g):
    xf = x.astype(jnp.float32)
    y = xf * lax.rsqrt(jnp.mean(xf * xf, axis=-1, keepdims=True) + EPS)
    return (y * g.astype(jnp.float32)).astype(x.dtype)

def masked_softmax(logits, mask):
    logits = jnp.where(mask, logits.astype(jnp.float32), NEG)
    m = jnp.max(logits, axis=-1, keepdims=True)
    e = jnp.exp(logits - m) * mask
    return e / jnp.maximum(jnp.sum(e, axis=-1, keepdims=True), 1e-30)

def alibi_slopes(n):
    return jnp.exp2(-8.0 * jnp.arange(1, n + 1, dtype=jnp.float32) / n)

def proj_split_points():
    sizes = [D_NSA, D_KV, D_KV, D_KV, D_KV, D_KV, D_KV, 3 * N_NSA_HEADS,
             D_FOX, D_FOX, D_FOX, N_FOX_HEADS]
    pts, acc = [], 0
    for s in sizes[:-1]:
        acc += s
        pts.append(acc)
    return pts

def compress(kv, w1, w2, pe):
    B, T, G, Dh = kv.shape
    nc = (T - CMP_BLOCK) // CMP_STRIDE + 1
    idx = jnp.arange(nc)[:, None] * CMP_STRIDE + jnp.arange(CMP_BLOCK)[None, :]
    blocks = kv[:, idx] + pe[None, None, :, None, :]
    blocks = jnp.swapaxes(blocks, 2, 3).reshape(B, nc, G, CMP_BLOCK * Dh)
    return jax.nn.gelu(blocks @ w1) @ w2

def nsa_attention(q, k_c, v_c, k_s, v_s, k_w, v_w, gate_logits, slopes):
    B, T, H, Dh = q.shape
    G = k_s.shape[2]
    R = H // G
    scale = Dh ** -0.5
    nc = k_c.shape[1]
    ns = T // SEL_BLOCK
    topk = min(SEL_TOPK, ns)
    cmp_start = jnp.arange(nc) * CMP_STRIDE
    cmp_end = cmp_start + CMP_BLOCK - 1
    sel_start = jnp.arange(ns) * SEL_BLOCK
    overlap = ((cmp_start[:, None] < sel_start[None, :] + SEL_BLOCK)
               & (cmp_end[:, None] >= sel_start[None, :])).astype(jnp.float32)
    ks_blocks = k_s.reshape(B, ns, SEL_BLOCK, G, Dh).transpose(0, 3, 1, 2, 4)
    vs_blocks = v_s.reshape(B, ns, SEL_BLOCK, G, Dh).transpose(0, 3, 1, 2, 4)
    pad = jnp.zeros((B, WINDOW, G, Dh), k_w.dtype)
    kw_pad = jnp.concatenate([pad, k_w], axis=1)
    vw_pad = jnp.concatenate([pad, v_w], axis=1)
    qg = q.reshape(B, T, G, R, Dh)
    gates = jax.nn.sigmoid(gate_logits.reshape(B, T, G, R, 3))
    sl = slopes.reshape(G, R)
    b_ix = jnp.arange(B)[:, None, None, None]
    g_ix = jnp.arange(G)[None, None, :, None]
    j_sel = jnp.arange(ns)
    l_sel = jnp.arange(SEL_BLOCK)

    def block(start):
        qb = lax.dynamic_slice_in_dim(qg, start, Q_BLOCK, 1)
        gb = lax.dynamic_slice_in_dim(gates, start, Q_BLOCK, 1)
        t = start + jnp.arange(Q_BLOCK)
        lc = jnp.einsum('bqgrd,bcgd->bqgrc', qb, k_c).astype(jnp.float32) * scale
        dist_c = (t[:, None] - cmp_end[None, :]).astype(jnp.float32)
        lc = lc - sl[None, None, :, :, None] * dist_c[None, :, None, None, :]
        mask_c = (cmp_end[None, :] <= t[:, None])[None, :, None, None, :]
        p_c = masked_softmax(lc, mask_c)
        o_c = jnp.einsum('bqgrc,bcgd->bqgrd', p_c.astype(v_c.dtype), v_c)
        imp = jnp.einsum('bqgrc,cn->bqgn', p_c, overlap)
        cur = t // SEL_BLOCK
        valid = j_sel[None, :] <= cur[:, None]
        forced = valid & ((j_sel[None, :] == 0) | (j_sel[None, :] == cur[:, None])
                          | (j_sel[None, :] == cur[:, None] - 1))
        score = jnp.where(forced[None, :, None, :], FORCED_SCORE,
                          jnp.where(valid[None, :, None, :], imp, -1.0))
        _, idx = lax.top_k(score, topk)
        ks = ks_blocks[b_ix, g_ix, idx]
        vs = vs_blocks[b_ix, g_ix, idx]
        ls = jnp.einsum('bqgrd,bqgkld->bqgrkl', qb, ks).astype(jnp.float32) * scale
        pos = idx[..., None] * SEL_BLOCK + l_sel
        dist_s = (t[None, :, None, None, None] - pos)[:, :, :, None]
        ls = ls - sl[None, None, :, :, None, None] * dist_s.astype(jnp.float32)
        mask_s = jnp.broadcast_to(dist_s >= 0, ls.shape)
        flat = (B, Q_BLOCK, G, R, topk * SEL_BLOCK)
        p_s = masked_softmax(ls.reshape(flat), mask_s.reshape(flat)).reshape(ls.shape)
        o_s = jnp.einsum('bqgrkl,bqgkld->bqgrd', p_s.astype(vs.dtype), vs)
        kw = lax.dynamic_slice_in_dim(kw_pad, start, Q_BLOCK + WINDOW, 1)
        vw = lax.dynamic_slice_in_dim(vw_pad, start, Q_BLOCK + WINDOW, 1)
        s = start - WINDOW + jnp.arange(Q_BLOCK + WINDOW)
        dist_w = t[:, None] - s[None, :]
        lw = jnp.einsum('bqgrd,bsgd->bqgrs', qb, kw).astype(jnp.float32) * scale
        lw = lw - sl[None, None, :, :, None] * dist_w.astype(jnp.float32)[None, :, None, None, :]
        mask_w = ((dist_w >= 0) & (dist_w < WINDOW) & (s[None, :] >= 0))[None, :, None, None, :]
        p_w = masked_softmax(lw, mask_w)
        o_w = jnp.einsum('bqgrs,bsgd->bqgrd', p_w.astype(vw.dtype), vw)
        o = gb[..., 0:1] * o_c + gb[..., 1:2] * o_s + gb[..., 2:3] * o_w
        return o.reshape(B, Q_BLOCK, H * Dh)

    starts = jnp.arange(T // Q_BLOCK) * Q_BLOCK
    out = lax.map(block, starts)
    return out.transpose(1, 0, 2, 3).reshape(B, T, H * Dh)

def fox_attention(q, k, v, f_logit):
    B, T, H, Dh = q.shape
    scale = Dh ** -0.5
    c = jnp.cumsum(jax.nn.log_sigmoid(f_logit.astype(jnp.float32)), axis=1).transpose(0, 2, 1)
    kpos = jnp.arange(T)

    def block(start):
        qb = lax.dynamic_slice_in_dim(q, start, Q_BLOCK, 1)
        cb = lax.dynamic_slice_in_dim(c, start, Q_BLOCK, 2)
        t = start + jnp.arange(Q_BLOCK)
        l = jnp.einsum('bqhd,bshd->bhqs', qb, k).astype(jnp.float32) * scale
        l = l + (cb[..., None] - c[:, :, None, :])
        mask = (kpos[None, :] <= t[:, None])[None, None]
        pr = masked_softmax(l, mask)
        o = jnp.einsum('bhqs,bshd->bqhd', pr.astype(v.dtype), v)
        return o.reshape(B, Q_BLOCK, H * Dh)

    starts = jnp.arange(T // Q_BLOCK) * Q_BLOCK
    out = lax.map(block, starts)
    return out.transpose(1, 0, 2, 3).reshape(B, T, H * Dh)

def moe(x, w_router, b_router, w_up, b_up, w_down, b_down):
    B, T, D = x.shape
    xf = x.reshape(-1, D)
    n = xf.shape[0]
    logits = (xf @ w_router + b_router).astype(jnp.float32)
    top_v, top_i = lax.top_k(logits, TOP_K)
    w = jax.nn.softmax(top_v, axis=-1)
    flat_e = top_i.reshape(-1)
    order = jnp.argsort(flat_e)
    sorted_e = flat_e[order]
    tok = order // TOP_K
    sizes = jnp.bincount(flat_e, length=N_EXPERTS).astype(jnp.int32)
    xs = xf[tok]
    h = lax.ragged_dot(xs, w_up, sizes) + b_up[sorted_e]
    g, lin = jnp.split(h, 2, axis=-1)
    g = jnp.minimum(g, SWIGLU_LIMIT)
    lin = jnp.clip(lin, -SWIGLU_LIMIT, SWIGLU_LIMIT)
    act = g * jax.nn.sigmoid(SWIGLU_ALPHA * g) * (lin + 1.0)
    y = lax.ragged_dot(act, w_down, sizes) + b_down[sorted_e]
    y = y * w.reshape(-1)[order][:, None].astype(y.dtype)
    return jax.ops.segment_sum(y, tok, num_segments=n).reshape(B, T, D)

def second_inputs(seed: int = 0) -> dict:
    key = jax.random.key(seed)
    ks = jax.random.split(key, 32)
    L, D, E, F = DEPTH_2, D_MODEL, N_EXPERTS, D_FF_2
    nrm = lambda k, shape, fan: jax.random.normal(k, shape, jnp.float32) * (fan ** -0.5)
    gain = lambda k, shape: 1.0 + 0.02 * jax.random.normal(k, shape, jnp.float32)
    small = lambda k, shape, s: s * jax.random.normal(k, shape, jnp.float32)
    return {
        "x": jax.random.normal(ks[0], (BATCH, SEQ, D), jnp.float32),
        "p": jax.random.normal(ks[1], (L, BATCH, SEQ, PLE_DIM), jnp.float32),
        "ln1": gain(ks[2], (L, D)),
        "w_in": nrm(ks[3], (L, D, D_PROJ), D),
        "b_fg": jax.random.uniform(ks[4], (L, N_FOX_HEADS), jnp.float32, 1.0, 5.0),
        "w_cmp1_k": nrm(ks[5], (L, CMP_BLOCK * HEAD_DIM, CMP_HIDDEN), CMP_BLOCK * HEAD_DIM),
        "w_cmp2_k": nrm(ks[6], (L, CMP_HIDDEN, HEAD_DIM), CMP_HIDDEN),
        "pe_cmp_k": small(ks[7], (L, CMP_BLOCK, HEAD_DIM), 0.1),
        "w_cmp1_v": nrm(ks[8], (L, CMP_BLOCK * HEAD_DIM, CMP_HIDDEN), CMP_BLOCK * HEAD_DIM),
        "w_cmp2_v": nrm(ks[9], (L, CMP_HIDDEN, HEAD_DIM), CMP_HIDDEN),
        "pe_cmp_v": small(ks[10], (L, CMP_BLOCK, HEAD_DIM), 0.1),
        "gn_nsa": gain(ks[11], (L, D_NSA)),
        "gn_fox": gain(ks[12], (L, D_FOX)),
        "w_out": nrm(ks[13], (L, D_MIX, D), D_MIX),
        "ln2": gain(ks[14], (L, D)),
        "w_router": nrm(ks[15], (L, D, E), D),
        "b_router": small(ks[16], (L, E), 0.01),
        "w_up": nrm(ks[17], (L, E, D, 2 * F), D),
        "b_up": small(ks[18], (L, E, 2 * F), 0.01),
        "w_down": nrm(ks[19], (L, E, F, D), F),
        "b_down": small(ks[20], (L, E, D), 0.01),
        "ln_ple": gain(ks[21], (L, D)),
        "w_ple": nrm(ks[22], (L, PLE_DIM, D), PLE_DIM),
        "w_ple_gate": nrm(ks[23], (L, D, D), D),
        "ln_f": gain(ks[24], (D,)),
    }

def second_block(x, p, ln1, w_in, b_fg, w_cmp1_k, w_cmp2_k, pe_cmp_k, w_cmp1_v, w_cmp2_v,
              pe_cmp_v, gn_nsa, gn_fox, w_out, ln2, w_router, b_router, w_up, b_up,
              w_down, b_down, ln_ple, w_ple, w_ple_gate, ln_f):
    B, T, _ = x.shape
    G, Dh = N_NSA_KV, HEAD_DIM
    slopes = alibi_slopes(N_NSA_HEADS)
    pts = proj_split_points()
    h = x
    for i in range(DEPTH_2):
        u = rmsnorm(h, ln1[i])
        proj = u @ w_in[i]
        (q_n, k_c, v_c, k_s, v_s, k_w, v_w, g_n,
         q_f, k_f, v_f, f_f) = jnp.split(proj, pts, axis=-1)
        kc = compress(k_c.reshape(B, T, G, Dh), w_cmp1_k[i], w_cmp2_k[i], pe_cmp_k[i])
        vc = compress(v_c.reshape(B, T, G, Dh), w_cmp1_v[i], w_cmp2_v[i], pe_cmp_v[i])
        o_nsa = nsa_attention(q_n.reshape(B, T, N_NSA_HEADS, Dh), kc, vc,
                              k_s.reshape(B, T, G, Dh), v_s.reshape(B, T, G, Dh),
                              k_w.reshape(B, T, G, Dh), v_w.reshape(B, T, G, Dh),
                              g_n.reshape(B, T, N_NSA_HEADS, 3), slopes)
        o_fox = fox_attention(q_f.reshape(B, T, N_FOX_HEADS, Dh),
                              k_f.reshape(B, T, N_FOX_HEADS, Dh),
                              v_f.reshape(B, T, N_FOX_HEADS, Dh),
                              f_f + b_fg[i])
        mix = jnp.concatenate([rmsnorm(o_nsa, gn_nsa[i]), rmsnorm(o_fox, gn_fox[i])], axis=-1)
        h = h + mix @ w_out[i]
        h = h + moe(rmsnorm(h, ln2[i]), w_router[i], b_router[i], w_up[i], b_up[i],
                    w_down[i], b_down[i])
        h = h + (p[i] @ w_ple[i]) * jax.nn.sigmoid(rmsnorm(h, ln_ple[i]) @ w_ple_gate[i])
    return rmsnorm(h, ln_f)


def setup_inputs(seed=0):
    out = dict(first_inputs(seed))
    for name, value in second_inputs(seed + 1).items():
        if name != "x":
            out[name + "_2"] = value
    return out


def reference(
    x, p, ln_gain, ln_bias, pool_w, pool_b, pool_scale, gdn_w_in, gdn_conv, gdn_a_log,
    gdn_dt_bias, gdn_norm_w, gdn_w_out, mlp_w1, mlp_w2, ple_gate_w, ple_gate_b, ple_proj, p_2,
    ln1_2, w_in_2, b_fg_2, w_cmp1_k_2, w_cmp2_k_2, pe_cmp_k_2, w_cmp1_v_2, w_cmp2_v_2,
    pe_cmp_v_2, gn_nsa_2, gn_fox_2, w_out_2, ln2_2, w_router_2, b_router_2, w_up_2, b_up_2,
    w_down_2, b_down_2, ln_ple_2, w_ple_2, w_ple_gate_2, ln_f_2,
):
    x = first_block(
        x, p, ln_gain, ln_bias, pool_w, pool_b, pool_scale, gdn_w_in, gdn_conv, gdn_a_log,
        gdn_dt_bias, gdn_norm_w, gdn_w_out, mlp_w1, mlp_w2, ple_gate_w, ple_gate_b, ple_proj,
    )
    return second_block(
        x, p_2, ln1_2, w_in_2, b_fg_2, w_cmp1_k_2, w_cmp2_k_2, pe_cmp_k_2, w_cmp1_v_2,
        w_cmp2_v_2, pe_cmp_v_2, gn_nsa_2, gn_fox_2, w_out_2, ln2_2, w_router_2, b_router_2,
        w_up_2, b_up_2, w_down_2, b_down_2, ln_ple_2, w_ple_2, w_ple_gate_2, ln_f_2,
    )


_drawn_inputs = setup_inputs


def setup_inputs(seed=0):
    import zlib

    import numpy as np

    out = dict(_drawn_inputs(seed))
    spreads = {}
    factors = {'gdn_norm_w': 4.139,
     'ple_gate_b': 6.258,
     'pe_cmp_k_2': 5.227,
     'b_router_2': 2.832,
     'b_up_2': 8.0,
     'b_down_2': 8.0,
     'ln_ple_2': 139.926,
     'ln_f_2': 22.457}
    for name, (base, spread) in spreads.items():
        noise = np.random.default_rng([zlib.crc32(name.encode()), seed]).standard_normal(out[name].shape)
        drawn = base * np.exp(spread * noise) if base else spread * noise
        out[name] = __import__('jax').numpy.asarray(drawn.astype(out[name].dtype))
    for name, factor in factors.items():
        out[name] = (out[name] * factor).astype(out[name].dtype)
    return out
```

```python
from contextlib import ExitStack

import numpy as np

import concourse.bass as bass
from concourse import mybir

F32 = mybir.dt.float32
F32R = mybir.dt.float32r
I32 = mybir.dt.int32
ALU = mybir.AluOpType
ACT = mybir.ActivationFunctionType
AX = mybir.AxisListType

P = 128
SEQ = 256
TILES = SEQ // P
D = 1024
KT = D // P
HEADS = 8
DFF = 4096
STEP = 512
MLP_STEPS = DFF // STEP
UNIT = 4096
SLOTS = 6
ALPHA = 4.0 ** 0.25
WINDOWS = (2, 4, 8, 16)
NCMP = (SEQ - 32) // 16 + 1
EXPERTS = 32
TOP_K = 4
BIG = 1e30
LIMIT = 7.0

FLAGS = {
    "tensor": (
        "gdn_ba_psum", "gdn_rows_psum", "gdn_KK_psum", "gdn_QK_psum", "gdn_k_psum", "gdn_v_psum",
        "gdn_u0_psum", "gdn_wT_psum", "gdn_state_psum", "gdn_o0_psum", "gdn_vnew_psum", "gdn_os_psum",
        "gdn_o1_psum", "att_kv_psum", "att_nat_psum", "att_qf_psum", "fox_cum_psum", "fox_rows_psum",
        "cmp_hid_psum", "cmp_kv_psum", "cmp_score_psum", "cmp_pT_psum", "cmp_o_psum", "router_psum",
        "router_rank_psum", "router_wT_psum", "router_bias_psum", "ple2_psum",
    ),
    "vector": (
        "gdn_ba", "gdn_g_in", "gdn_g", "gdn_diff", "gdn_DB", "gdn_LT", "gdn_QKT", "gdn_k_ready",
        "gdn_v_ready", "gdn_wT", "gdn_o_ss", "att_kv", "att_nat", "cmp_in", "fox_f", "att_kf", "fox_lf",
        "fox_bias", "cmp_clear", "cmp_hv4", "cmp_kcc", "cmp_vblk", "cmp_diff", "cmp_prob", "cmp_pT", "cmp_o",
        "router_top", "router_chosen", "router_weight", "router_rank", "router_count", "router_wT",
        "router_x", "ple2_copied", "moe_end",
    ),
    "scalar": (
        "gdn_beta", "gdn_log", "gdn_exp_gc", "gdn_z", "gdn_exp", "gdn_u0", "gdn_state", "gdn_vnew",
        "gdn_o_sq", "gdn_o_rms", "att_qn", "att_gates", "fox_log", "att_qf", "att_vf", "cmp_exp", "att_rms",
        "ple2_side",
    ),
}


def shape_tables():
    p = np.arange(P)[:, None]
    c = np.arange(P)[None, :]
    t = {}
    t["ident"] = (p == c)
    t["upto"] = (p <= c)
    t["ones"] = np.ones((P, P))
    t["strict"] = (p < c)
    for level in range(7):
        b = 1 << level
        t[f"level{level}"] = (c // (2 * b) == p // (2 * b)) & ((c // b) % 2 == 1) & ((p // b) % 2 == 0)
    sel = np.zeros((P, HEADS, P))
    for h in range(HEADS):
        sel[h, h] = 1
    t["pick_head"] = sel.reshape(P, -1)
    dist = np.concatenate([p - c, p + P - np.arange(SEQ)[None, :]], 1).astype(np.float64)
    t["neg_dist"] = np.where(dist >= 0, -dist, -1e32)
    t["mask_neg"] = np.where(dist >= 0, 0.0, -BIG)
    j = np.arange(16)[None, :]
    d = np.concatenate([p - (16 * j + 31), p + P - (16 * j + 31)], 1).astype(np.float64)
    ok = (d >= 0) & (np.tile(j, (1, 2)) < NCMP)
    slopes = 2.0 ** -(np.arange(HEADS) + 1.0)
    bias = np.where(ok, -d, 0.0).reshape(P, 1, 2, 1, 16) * slopes.reshape(1, 2, 1, 4, 1)
    valid = np.broadcast_to(ok.reshape(P, 1, 2, 1, 16), bias.shape)
    t["cmp_bias"] = np.where(valid, bias, -BIG).reshape(P, -1)
    t["cmp_mask"] = valid.reshape(P, -1)
    t["slopes"] = np.broadcast_to(slopes.reshape(2, 4).T.reshape(1, 4, 2, 1), (P, 4, 2, 2)).reshape(P, -1)
    t["own_row"] = (p // 32 == np.arange(4)[None, :])
    t["slot_no"] = np.broadcast_to(np.arange(P)[None, :], (P, P))
    t["slot_no2"] = t["slot_no"] + P
    t["eps"] = np.broadcast_to(np.array([1e-5, 1e-6, 128e-6, 1.0, 4.0])[None, :], (P, 5))
    return {k: np.asarray(v, np.float32) for k, v in t.items()}


def band_tables():
    s = np.arange(SEQ)[:, None]
    t = np.arange(SEQ)[None, :]
    bands = []
    for w in WINDOWS:
        mean = ((s <= t) & (s > t - w)) / np.minimum(t + 1.0, w)
        bands.append(mean - (s == t))
    b = np.stack(bands, 1).astype(np.float32)
    return np.concatenate([b[:P].reshape(P, -1), b[P:, :, P:].reshape(P, -1)], 1)


def column_layout(parts):
    at, where = 0, {}
    for name, a in parts.items():
        where[name] = (at, a.shape[1])
        at += a.shape[1]
    return where, at


def unit(w, k0, kn, c0, cn):
    return w[k0 * P:(k0 + kn) * P, c0:c0 + cn].reshape(kn, P, cn).transpose(1, 0, 2).reshape(P, kn * cn)


def padded(a, n):
    return np.concatenate([a, np.zeros((a.shape[0], n - a.shape[1]), a.dtype)], 1)


def weight_units(i):
    u = {}
    pool = np.concatenate([unit(i["pool_w"][0, g], 0, 2, 0, 256) for g in range(4)], 1)
    u["pool_proj0"] = np.concatenate([pool, unit(i["ple_proj"][0], 0, 2, 0, D)], 1)
    for l in range(2):
        for h in range(2):
            u[f"gate{l}{h}"] = unit(i["ple_gate_w"][l], 4 * h, 4, 0, D)
        for s in range(MLP_STEPS):
            u[f"mlp{l}_up{s}"] = unit(i["mlp_w1"][l], 0, KT, s * STEP, STEP)
            u[f"mlp{l}_down{s}"] = unit(i["mlp_w2"][l], 4 * s, 4, 0, D)
    for n in range(8):
        u[f"gdn_in{n}"] = unit(i["gdn_w_in"][0], 0, KT, n * STEP, STEP)
    for h in range(2):
        u[f"gdn_out{h}"] = unit(i["gdn_w_out"][0], 4 * h, 4, 0, D)
    u["proj1"] = padded(unit(i["ple_proj"][1], 0, 2, 0, D), UNIT)
    w = i["w_in_2"][0]
    w = np.concatenate([w[:, 0:512].reshape(D, 2, 4, 64).transpose(0, 2, 1, 3).reshape(D, 512),
                        w[:, 512:768].reshape(D, 2, 2, 64).transpose(0, 2, 1, 3).reshape(D, 256), w[:, 768:]], 1)
    for n, (c0, cn) in enumerate(ATT_COLS):
        u[f"att_in{n}"] = padded(unit(w, 0, KT, c0, cn), UNIT)
    cmp = [i[k][0].reshape(32, 64, 128).transpose(1, 0, 2).reshape(64, UNIT) for k in ("w_cmp1_k_2", "w_cmp1_v_2")]
    u["cmp"] = np.concatenate(cmp, 0)
    for h in range(2):
        u[f"att_out{h}"] = unit(i["w_out_2"][0], 4 * h, 4, 0, D)
    u["ple2"] = padded(unit(i["w_ple_2"][0], 0, 2, 0, D), UNIT)
    for h in range(2):
        u[f"gate2{h}"] = unit(i["w_ple_gate_2"][0], 4 * h, 4, 0, D)
    return u


ATT_COLS = ((0, 512), (512, 512), (1024, 280), (1304, 512), (1816, 512), (2328, 512))


def row_vectors(i):
    r = {"pool_b": i["pool_b"][0].reshape(-1), "pool_scale": i["pool_scale"][0]}
    for l in range(2):
        r[f"gain{l}0"], r[f"bias{l}0"] = i["ln_gain"][l, 0], i["ln_bias"][l, 0]
        r[f"gate_b{l}"] = i["ple_gate_b"][l]
        r[f"gain{l}1"], r[f"bias{l}1"] = i["ln_gain"][l, 1], i["ln_bias"][l, 1]
    r["ln1"] = i["ln1_2"][0]
    r["gn"] = np.concatenate([i["gn_nsa_2"][0], i["gn_fox_2"][0]])
    r["ln2"] = i["ln2_2"][0]
    r["ln_ple"] = i["ln_ple_2"][0]
    r["ln_f"] = i["ln_f_2"]
    return r


def small_params(i):
    s = {}

    def every(a):
        return np.broadcast_to(a.reshape(1, -1), (P, a.size))

    s["conv"] = i["gdn_conv"][0].reshape(4, 24, P).transpose(2, 1, 0).reshape(P, 96)
    s["a_log"] = every(i["gdn_a_log"])
    s["dt_bias"] = every(i["gdn_dt_bias"])
    s["norm_w"] = every(i["gdn_norm_w"])
    s["w_ba"] = unit(i["gdn_w_in"][0], 0, KT, 4096, 16)
    s["b_fg"] = every(i["b_fg_2"])
    s["w_fg"] = unit(i["w_in_2"][0], 0, KT, 2840, 8)
    s["w_router"] = unit(i["w_router_2"][0], 0, KT, 0, EXPERTS)
    s["b_router"] = every(i["b_router_2"])
    s["pe"] = np.concatenate([i["pe_cmp_k_2"][0].T, i["pe_cmp_v_2"][0].T], 0)
    s["cmp2_k"] = i["w_cmp2_k_2"][0]
    s["cmp2_v"] = i["w_cmp2_v_2"][0]
    return s


def lay_out(inputs):
    i = {k: np.asarray(v) for k, v in inputs.items()}
    units = weight_units(i)
    rows = row_vectors(i)
    tables, small = shape_tables(), small_params(i)
    table_at, table_n = column_layout(tables)
    small_at, small_n = column_layout(small)
    up = i["w_up_2"][0].reshape(EXPERTS, KT, P, 2, 2, STEP)
    up = up.transpose(0, 4, 3, 2, 1, 5).reshape(EXPERTS, 4, P, UNIT)
    down = i["w_down_2"][0].reshape(EXPERTS, 2, 4, P, 2, STEP)
    down = down.transpose(0, 1, 3, 4, 2, 5).reshape(EXPERTS, 2, P, UNIT)
    p_all = np.concatenate([i["p"][:, 0], i["p_2"][:, 0]], 0)
    arrays = {
        "tokens": i["x"][0].reshape(TILES, P, D).transpose(1, 0, 2),
        "weights": np.stack(list(units.values()), 0),
        "experts": np.concatenate([up, down], 1),
        "rows": np.stack(list(rows.values()), 0),
        "expert_b": i["b_up_2"][0],
        "b_down": i["b_down_2"][0],
        "ple_in": p_all.transpose(0, 2, 1).reshape(3, 2, P, SEQ).transpose(2, 0, 1, 3),
        "small": np.concatenate(list(small.values()), 1),
        "tables": np.concatenate(list(tables.values()), 1),
        "bands": band_tables(),
    }
    places = {"unit": {n: k for k, n in enumerate(units)}, "row": {n: k for k, n in enumerate(rows)},
              "table": table_at, "small": small_at}
    return {k: np.ascontiguousarray(v) for k, v in arrays.items()}, places


def build(nc, places, tokens, weights, experts, rows, expert_b, b_down, ple_in, small, tables, bands, out):
    with ExitStack() as ctx:
        def sb(name, shape, dt=F32):
            return ctx.enter_context(nc.sbuf_tensor(name, shape, dt))

        sems = {}

        def sem(name):
            if name not in sems:
                sems[name] = ctx.enter_context(nc.semaphore(name))
            return sems[name]

        def shared(name, shape):
            with nc.sbuf_tensor(name, shape, F32) as plain:
                pass
            return plain, sb(name + "_split", shape, F32R)

        ring, ring_split = shared("ring", [P, SLOTS, UNIT])
        x = sb("x", [P, TILES, D])
        xT = sb("xT", [P, KT, SEQ])
        pre = sb("pre", [P, TILES, D])
        side, side_split = shared("side", [P, TILES, D])
        row_buf, row_split = shared("row_buf", [P, 3, D])
        tab = sb("tab", [P, tables.shape[1]])
        par = sb("par", [P, small.shape[1]])
        pleT = sb("pleT", [P, 3, 2, SEQ])
        stats = sb("stats", [P, TILES, 2, 6])
        mv = sb("mv", [P, TILES, 2])
        std = sb("std", [P, TILES])
        rstd = sb("rstd", [P, TILES])
        arena, arena_split = shared("arena", [P, 9728])
        ps = ctx.enter_context(nc.psum_tensor("ps", [P, 4, 1024], F32))

        def table(name):
            at, n = places["table"][name]
            return tab[:, at:at + n]

        def param(name):
            at, n = places["small"][name]
            return par[:, at:at + n]

        ident, ones, upto = table("ident"), table("ones"), table("upto")

        def eps(k):
            return table("eps")[:, k:k + 1]

        EPS5, EPS6, EPS6_128, ONE = 0, 1, 2, 3

        def scratch(at, *shape):
            n = int(np.prod(shape))
            return view(arena[:, at:at + n], shape)

        def split_scratch(at, *shape):
            n = int(np.prod(shape))
            return view(arena_split[:, at:at + n], shape)

        def view(flat, shape):
            if len(shape) == 1:
                return flat
            names = "abcd"[:len(shape)]
            return flat.rearrange(f"p ({' '.join(names)}) -> p {' '.join(names)}", **{n: s for n, s in zip(names, shape)})

        def spread(ap, n):
            return ap[:, :, None].to_broadcast((*ap.shape, n))

        def repeat(ap, n):
            return ap[:, None, :].to_broadcast((ap.shape[0], n, ap.shape[1]))

        unit_full = [sem(f"unit_full{s}") for s in range(SLOTS)]
        taken = [0] * SLOTS

        def fill(sp, name, slot, after=None, count=0, width=UNIT):
            if after is not None:
                sp.wait_ge(sem(after), count)
            sp.dma_start(ring[:, slot, 0:width], weights[places["unit"][name], :, 0:width]).then_inc(unit_full[slot], 16)

        def take(pe, slot):
            taken[slot] += 1
            pe.wait_ge(unit_full[slot], 16 * taken[slot])
            return ring[:, slot, :]

        row_full = [sem(f"row_full{s}") for s in range(3)]
        rows_taken = [0]

        def row(dve, name):
            n = places["row"][name]
            assert n == rows_taken[0], name
            rows_taken[0] += 1
            dve.wait_ge(row_full[n % 3], 16 * (n // 3 + 1))
            return row_buf[:, n % 3, :]

        def row_done(dve, ins):
            ins.then_inc(sem("row_used"), 1)
            dve.wait_ge(sem("row_used"), rows_taken[0])

        NORMS = ("ln00", "ln01", "ln10", "ln11", "rn1", "rn2", "rnp", "rnf")
        LAYER_NORMS = NORMS[:4]
        TURNS = ("ln00", "ln01", "gdny", "ln10", "rn1", "att", "rn2", "rnp")

        def before(stages_, tag):
            return TILES * stages_.index(tag)

        flags_up = {e: 0 for e in FLAGS}

        def flag_up(name):
            e = next(e for e in FLAGS if name in FLAGS[e])
            assert FLAGS[e][flags_up[e]] == name, (name, FLAGS[e][flags_up[e]])
            flags_up[e] += 1
            return sem(f"{e}_flags")

        def flag(name):
            e = next(e for e in FLAGS if name in FLAGS[e])
            return sem(f"{e}_flags"), FLAGS[e].index(name) + 1

        chained = {"v": 0, "a": 0}

        def link(eng, ins, which="v"):
            chained[which] += 1
            ins.then_inc(sem("chain_" + which), 1)
            eng.wait_ge(sem("chain_" + which), chained[which])

        V, A, G, T = nc.vector, nc.scalar, nc.gpsimd, nc.tensor

        def sp_constants(sp):
            sp.dma_start(x[:], tokens).then_inc(sem("x_loaded"), 16)
            sp.dma_start(arena[:, 0:1536], bands).then_inc(sem("bands_loaded"), 16)
            fill(sp, "pool_proj0", 4)
            sp.dma_start(tab[:], tables).then_inc(sem("tables_loaded"), 16)
            sp.dma_start(par[:], small).then_inc(sem("small_loaded"), 16)
            sp.dma_start(pleT[:], ple_in).then_inc(sem("ple_loaded"), 16)
            fill(sp, "gate00", 5)
            fill(sp, "gate01", 3)

        def pool_rows(pool, first, last):
            for n in range(first, last):
                if n >= 3:
                    pool.wait_ge(sem("row_used"), n - 2)
                pool.dma_start(row_buf[:, n % 3, :], rows[n:n + 1, :].to_broadcast((P, D))).then_inc(row_full[n % 3], 16)

        def v_layer_norm(v, tag, src, gain, bias):
            for t in range(TILES):
                V.bn_stats(stats[:, t, 0, :], src[:, t, 0:512])
                link(v, V.bn_stats(stats[:, t, 1, :], src[:, t, 512:1024]))
                V.bn_aggr(mv[:, t, :], stats[:, t].rearrange("p a b -> p (a b)")).then_inc(sem("norm_var"), 1)
            g = row(v, gain)
            for t in range(TILES):
                v.wait_ge(sem("norm_std"), before(NORMS, tag) + t + 1)
                link(v, V.reciprocal(rstd[:, t:t + 1], std[:, t:t + 1]))
                link(v, V.tensor_scalar(src[:, t, :], src[:, t, :], mv[:, t, 0:1], rstd[:, t:t + 1], ALU.subtract, ALU.mult))
                last = V.tensor_tensor(src[:, t, :], src[:, t, :], g, ALU.mult)
                if t < TILES - 1:
                    link(v, last)
            row_done(v, last)
            b = row(v, bias)
            for t in range(TILES):
                V.tensor_tensor(x[:, t, :], src[:, t, :], b, ALU.add).then_inc(sem("norm_x"), 1)
            v.wait_ge(sem("norm_x"), before(NORMS, tag) + TILES)
            v.sem_inc(sem("row_used"), 1)

        def a_layer_norm(a, tag):
            for t in range(TILES):
                a.wait_ge(sem("norm_var"), before(LAYER_NORMS, tag) + t + 1)
                A.activation(std[:, t:t + 1], mv[:, t, 1:2], ACT.Sqrt, bias=eps(EPS5)).then_inc(sem("norm_std"), 1)

        def v_rms_norm(v, tag, gain, halves=1):
            g = row(v, gain)
            for t in range(TILES):
                v.wait_ge(sem("norm_std"), before(NORMS, tag) + t + 1)
                link(v, V.reciprocal(rstd[:, t:t + 1], std[:, t:t + 1]))
                last = V.scalar_tensor_tensor(out=pre[:, t, :], in0=x[:, t, :], scalar=rstd[:, t:t + 1], in1=g,
                                              op0=ALU.mult, op1=ALU.mult)
                last.then_inc(sem("norm_x"), 1)
            v.wait_ge(sem("norm_x"), before(NORMS, tag) + TILES)
            v.sem_inc(sem("row_used"), 1)

        def a_rms_norm(a, tag, ready, count):
            for t in range(TILES):
                if ready is not None:
                    a.wait_ge(sem(ready), count + t + 1)
                link(a, A.activation(pre[:, t, :], x[:, t, :], ACT.Square, accum_out=mv[:, t, 1:2]), "a")
                A.activation(std[:, t:t + 1], mv[:, t, 1:2], ACT.Sqrt, bias=eps(EPS6), scale=1.0 / D).then_inc(sem("norm_std"), 1)

        def pe_transpose(pe, tag, src, ready, count=0):
            for t in range(TILES):
                pe.wait_ge(sem(ready), count + t + 1)
                for c in range(KT):
                    at = (c % 4) * SEQ + t * P
                    m = T.transpose(ps[:, c // 4, at:at + P], src[:, t, c * P:(c + 1) * P], ident)
                    if t == TILES - 1 and c % 4 == 3:
                        m.then_inc(sem("T_psum"), 1)

        def v_transpose(v, tag):
            v.wait_ge(sem("T_psum"), before(TURNS, tag) + 1)
            V.tensor_copy(xT[:, 0:4, :], view(ps[:, 0, :], (4, SEQ))).then_inc(sem("T"), 1)

        def a_transpose(a, tag):
            a.wait_ge(sem("T_psum"), before(TURNS, tag) + 2)
            A.copy(xT[:, 4:8, :], view(ps[:, 1, :], (4, SEQ))).then_inc(sem("T"), 1)

        def pe_dense(pe, done, pair_of, slots):
            for t in range(TILES):
                for half in range(2):
                    for k in range(KT):
                        slot = slots[k // 4]
                        if t == 0 and half == 0 and k % 4 == 0:
                            take(pe, slot)
                        at = (k % 4) * D + half * 512
                        m = T.matmul(ps[:, pair_of[t], half * 512:half * 512 + 512], xT[:, k, t * P:(t + 1) * P],
                                     ring[:, slot, at:at + 512], start=(k == 0), stop=(k == KT - 1))
                m.then_inc(sem(done), 1)

        def pe_pool(pe):
            pe.wait_ge(sem("x_loaded"), 16)
            pe.wait_ge(sem("bands_loaded"), 16)
            for c in range(KT):
                g, at = c // 2, (c % 4) * SEQ
                band0, band1 = arena[:, g * SEQ:(g + 1) * SEQ], arena[:, 1024 + g * P:1024 + (g + 1) * P]
                T.matmul(ps[:, c // 4, at:at + SEQ], x[:, 0, c * P:(c + 1) * P], band0, start=True, stop=False)
                m = T.matmul(ps[:, c // 4, at + P:at + SEQ], x[:, 1, c * P:(c + 1) * P], band1, start=False, stop=True)
                if c % 4 == 3:
                    m.then_inc(sem("pool_T_psum"), 1)
            w = take(pe, 4)
            pe.wait_ge(sem("pool_T"), 2)
            for t in range(TILES):
                for g in range(4):
                    for k in range(2):
                        m = T.matmul(ps[:, 2 + t, g * 256:(g + 1) * 256], xT[:, 2 * g + k, t * P:(t + 1) * P],
                                     w[:, (2 * g + k) * 256:(2 * g + k + 1) * 256], start=(k == 0), stop=(k == 1))
                m.then_inc(sem("pool_psum"), 1)

        def v_pool(v):
            b = row(v, "pool_b")
            for t in range(TILES):
                v.wait_ge(sem("pool_psum"), t + 1)
                last = V.tensor_tensor(pre[:, t, :], ps[:, 2 + t, :], b, ALU.add)
            row_done(v, last)
            s = row(v, "pool_scale")
            for t in range(TILES):
                last = V.tensor_tensor(pre[:, t, :], pre[:, t, :], s, ALU.mult)
            row_done(v, last)
            for t in range(TILES):
                last = V.scalar_tensor_tensor(out=pre[:, t, :], in0=x[:, t, :], scalar=ALPHA, in1=pre[:, t, :],
                                              op0=ALU.mult, op1=ALU.add)
            link(v, last)

        def pe_ple(pe, tag, layer, gate_slots, proj_slot, proj_at, proj_taken=False):
            pe.wait_ge(sem("T"), before(TURNS, tag) + 2)
            pe_dense(pe, "ple_gate_psum", (0, 1), gate_slots)
            if not proj_taken:
                take(pe, proj_slot)
            for t in range(TILES):
                for half in range(2):
                    for k in range(2):
                        at = proj_at + k * D + half * 512
                        m = T.matmul(ps[:, 2 + t, half * 512:half * 512 + 512], pleT[:, layer, k, t * P:(t + 1) * P],
                                     ring[:, proj_slot, at:at + 512], start=(k == 0), stop=(k == 1))
                m.then_inc(sem("ple_proj_psum"), 1)

        def v_ple(v, layer):
            b = row(v, f"gate_b{layer}")
            for t in range(TILES):
                v.wait_ge(sem("ple_gate_psum"), TILES * layer + t + 1)
                last = V.tensor_tensor(side[:, t, :], ps[:, t, :], b, ALU.add).then_inc(sem("ple_logit"), 1)
            v.wait_ge(sem("ple_logit"), TILES * layer + 2)
            v.sem_inc(sem("row_used"), 1)
            for t in range(TILES):
                v.wait_ge(sem("ple_proj_psum"), TILES * layer + t + 1)
                v.wait_ge(sem("ple_gate"), TILES * layer + t + 1)
                V.tensor_tensor(side[:, t, :], side[:, t, :], ps[:, 2 + t, :], ALU.mult).then_inc(sem("ple_side"), 1)

        def a_ple(a, layer):
            for t in range(TILES):
                a.wait_ge(sem("ple_logit"), TILES * layer + t + 1)
                A.activation(side[:, t, :], side[:, t, :], ACT.Sigmoid).then_inc(sem("ple_gate"), 1)

        relu = scratch(0, 2, TILES, STEP)
        hidT = scratch(2048, 2, 4, SEQ)
        mlp_base = {}

        def sp_mlp(sp, layer):
            ups = weights[places["unit"][f"mlp{layer}_up0"]:places["unit"][f"mlp{layer}_up0"] + 2 * MLP_STEPS]
            ups = ups.rearrange("(i j m) p n -> i j m p n", j=2, m=2)
            with sp.Fori(0, MLP_STEPS // 2 - 1) as i:
                for j in range(2):
                    sp.wait_ge(sem("mlp_h_psum"), 16 * layer + 4 * i + 2 * j + 2)
                    sp.dma_start(ring[:, 2 * j, :], ups[i + 1, j, 0]).then_inc(unit_full[2 * j], 16)
                    sp.wait_ge(sem("mlp_down"), 8 * layer + 2 * i + j + 1)
                    sp.dma_start(ring[:, 2 * j + 1, :], ups[i + 1, j, 1]).then_inc(unit_full[2 * j + 1], 16)

        def pe_mlp(pe, layer):
            base = taken[:4]
            h_psum, relu_done = sem("mlp_h_psum"), sem("mlp_relu")
            hT_psum, hT, down = sem("mlp_hT_psum"), sem("mlp_hT"), sem("mlp_down")

            def up(s, par, round_, t, first=False):
                slot = 2 * par
                if t == 0:
                    pe.wait_ge(unit_full[slot], round_ * 16 + 16 * (base[slot] + 1))
                if not first:
                    pe.wait_ge(relu_done, 16 * layer + 2 * s + (t - 1))
                for k in range(KT):
                    m = T.matmul(ps[:, 0, t * 512:t * 512 + 512], xT[:, k, t * P:(t + 1) * P],
                                 ring[:, slot, k * STEP:(k + 1) * STEP], start=(k == 0), stop=(k == KT - 1))
                m.then_inc(h_psum, 1)

            def turn(s, par, first=False):
                pe.wait_ge(relu_done, 16 * layer + 2 * s + 2)
                if not first:
                    pe.wait_ge(hT, 8 * layer + s)
                for t in range(TILES):
                    for k in range(4):
                        m = T.transpose(ps[:, 1, k * SEQ + t * P:k * SEQ + (t + 1) * P],
                                        relu[:, par, t, k * P:(k + 1) * P], ident)
                m.then_inc(hT_psum, 1)

            def out_of(s, par, round_, first=False, last=False):
                slot = 2 * par + 1
                pe.wait_ge(unit_full[slot], round_ * 16 + 16 * (base[slot] + 1))
                pe.wait_ge(hT, 8 * layer + s + 1)
                for t in range(TILES):
                    for half in range(2):
                        for k in range(4):
                            m = T.matmul(ps[:, 2 + t, half * 512:half * 512 + 512], hidT[:, par, k, t * P:(t + 1) * P],
                                         ring[:, slot, k * D + half * 512:k * D + half * 512 + 512],
                                         start=(first and k == 0), stop=(last and k == 3), skip_group_check=True)
                m.then_inc(down, 1)

            def step(s, par, round_, next_round, first=False):
                up(s + 1, 1 - par, next_round, 0)
                turn(s, par, first)
                up(s + 1, 1 - par, next_round, 1)
                out_of(s, par, round_, first)

            pe.wait_ge(sem("ple_side"), TILES * layer + 2)
            up(0, 0, 0, 0, first=True)
            up(0, 0, 0, 1, first=True)
            step(0, 0, 0, 0, first=True)
            with pe.Fori(0, 3) as i:
                step(2 * i + 1, 1, i, i + 1)
                step(2 * i + 2, 0, i + 1, i + 1)
            turn(7, 1)
            out_of(7, 1, 3, last=True)
            for slot in range(4):
                taken[slot] += 4

        def v_mlp(v, layer):
            h_psum, relu_done, hT_psum = (sem(f"mlp_{n}") for n in ("h_psum", "relu", "hT_psum"))

            def step(s, par, early=False):
                for t in range(TILES):
                    v.wait_ge(h_psum, 16 * layer + 2 * s + t + 1)
                    if t == 0 and not early:
                        v.wait_ge(hT_psum, 8 * layer + s - 1)
                    V.tensor_scalar(relu[:, par, t, :], ps[:, 0, t * 512:t * 512 + 512], 0.0, None, ALU.max)\
                     .then_inc(relu_done, 1)

            step(0, 0, early=True)
            step(1, 1, early=True)
            with v.Fori(1, 4) as i:
                step(2 * i, 0)
                step(2 * i + 1, 1)
            v.wait_ge(sem("mlp_down"), MLP_STEPS * (layer + 1))
            for t in range(TILES):
                link(v, V.scalar_tensor_tensor(out=pre[:, t, :], in0=x[:, t, :], scalar=ALPHA, in1=ps[:, 2 + t, :],
                                               op0=ALU.mult, op1=ALU.add))
                link(v, V.tensor_tensor(pre[:, t, :], pre[:, t, :], side[:, t, :], ALU.add))

        def a_mlp(a, layer):
            hT_psum, hT, down = (sem(f"mlp_{n}") for n in ("hT_psum", "hT", "down"))

            def step(s, par, early=False):
                a.wait_ge(hT_psum, 8 * layer + s + 1)
                if not early:
                    a.wait_ge(down, 8 * layer + s - 1)
                A.activation(hidT[:, par], view(ps[:, 1, :], (4, SEQ)), ACT.Square).then_inc(hT, 1)

            step(0, 0, early=True)
            step(1, 1, early=True)
            with a.Fori(1, 4) as i:
                step(2 * i, 0)
                step(2 * i + 1, 1)

        qkvT = scratch(0, 24, SEQ)
        z_silu = scratch(6144, TILES, D)
        g_small = arena[:, 8192:9728]
        logits2 = view(g_small[:, 0:32], (16, TILES))
        beta, g_in, g_log, g_abs, g_dec, gc, exp_gc, bg, g_ea = (
            view(g_small[:, 32 + 16 * n:48 + 16 * n], (HEADS, TILES)) for n in range(9))
        rms16 = g_small[:, 192:208]
        rowsT = view(g_small[0:8, 256:768], (2, TILES, P))
        slot01 = ring[:, 0:2, :].rearrange("p a b -> p (a b)")
        slot23 = ring[:, 2:4, :].rearrange("p a b -> p (a b)")

        def heads16(flat):
            return flat.rearrange("p (h t c) -> p h t c", h=HEADS, t=TILES)

        LT, TI, TT, PR = (slot01[:, 2048 * n:2048 * (n + 1)] for n in range(4))
        DEC, QKT, VB = (slot23[:, 2048 * n:2048 * (n + 1)] for n in range(3))
        KBG, KD = slot23[:, 6144:7168], slot23[:, 7168:8192]
        MT = pre[:].rearrange("p a b -> p (a b)")
        U0, VNEW = side[:, 0, :], side[:, 1, :]
        WTN, STATE = TI[:, 0:1024], TI[:, 1024:2048]
        O = view(PR, (TILES, D))
        pair01 = ps[:, 0:2, :].rearrange("p a b -> p (a b)")
        pair23 = ps[:, 2:4, :].rearrange("p a b -> p (a b)")
        LEVELS = 7

        def half(flat, g):
            return flat[:, 1024 * g:1024 * (g + 1)]

        def system(flat, h, t):
            return flat[:, (2 * h + t) * P:(2 * h + t + 1) * P]

        def pe_gdn_in(pe):
            pe.wait_ge(sem("T"), before(TURNS, "ln01") + 2)
            pe.wait_ge(sem("small_loaded"), 16)
            w_ba = view(param("w_ba"), (KT, 16))
            for t in range(TILES):
                for k in range(KT):
                    m = T.matmul(ps[:, 3, 512 + 16 * t:528 + 16 * t], xT[:, k, t * P:(t + 1) * P], w_ba[:, k, :],
                                 start=(k == 0), stop=(k == KT - 1))
            m.then_inc(flag_up("gdn_ba_psum"), 1)
            for n in range(6):
                w = take(pe, GDN_IN_SLOTS[n])
                if n == 3:
                    pe.wait_ge(*flag("gdn_g"))
                    pe.wait_ge(*flag("gdn_beta"))
                    for t in range(TILES):
                        T.matmul(ps[:, 3, 8 * t:8 * t + 8], upto, g_dec[:, :, t], start=True, stop=True)
                        T.matmul(ps[0:8, 3, 512 + P * t:512 + P * (t + 1)], g_dec[:, :, t], upto, start=True, stop=True)
                        m = T.transpose(ps[0:8, 3, 768 + P * t:768 + P * (t + 1)], beta[:, :, t], ident)
                    m.then_inc(flag_up("gdn_rows_psum"), 1)
                    pe.wait_ge(sem("gdn_rows"), 2)
                if n >= 4:
                    pe.wait_ge(sem("gdn_conv"), n - 3)
                for b in range(4):
                    for k in range(KT):
                        m = T.matmul(ps[:, n % 4, b * SEQ:(b + 1) * SEQ], w[:, k * STEP + b * P:k * STEP + (b + 1) * P],
                                     xT[:, k, :], start=(k == 0), stop=(k == KT - 1))
                m.then_inc(sem("gdn_in_psum"), 1)
            pe.wait_ge(sem("gdn_conv"), 4)
            for half_ in range(2):
                w = take(pe, GDN_IN_SLOTS[6 + half_])
                for t in range(TILES):
                    for k in range(KT):
                        m = T.matmul(ps[:, 2 + t, half_ * 512:half_ * 512 + 512], xT[:, k, t * P:(t + 1) * P],
                                     w[:, k * STEP:(k + 1) * STEP], start=(k == 0), stop=(k == KT - 1))
                m.then_inc(sem("gdn_z_psum"), 1)

        GDN_IN_SLOTS = (4, 5, 0, 1, 2, 3, 4, 5)
        conv_w = view(param("conv"), (24, 4))

        def a_gdn_in(a):
            a.wait_ge(sem("small_loaded"), 16)
            a.wait_ge(*flag("gdn_ba"))
            A.activation(beta, logits2[:, 0:8, :], ACT.Sigmoid).then_inc(flag_up("gdn_beta"), 1)
            a.wait_ge(*flag("gdn_g_in"))
            link(a, A.activation(g_abs, g_in, ACT.Abs), "a")
            link(a, A.activation(g_abs, g_abs, ACT.Exp, scale=-1.0), "a")
            A.activation(g_ea, spread(param("a_log"), TILES), ACT.Exp)
            A.activation(g_log, g_abs, ACT.Ln, bias=eps(ONE)).then_inc(flag_up("gdn_log"), 1)

            def taps(n):
                a.wait_ge(sem("gdn_in_psum"), n + 1)
                for b in range(4):
                    m = A.activation(qkvT[:, 4 * n + b, :], ps[:, n % 4, b * SEQ:(b + 1) * SEQ], ACT.Copy,
                                     scale=conv_w[:, 4 * n + b, 3:4])
                m.then_inc(sem("gdn_tap"), 1)

            def silu(n):
                a.wait_ge(sem("gdn_conv"), n + 1)
                A.activation(qkvT[:, 4 * n:4 * n + 4, :], qkvT[:, 4 * n:4 * n + 4, :], ACT.Silu).then_inc(sem("gdn_qkv"), 1)

            for n in range(6):
                taps(n)
                if n == 2:
                    a.wait_ge(sem("gdn_rows"), 1)
                    A.activation(exp_gc, gc, ACT.Exp).then_inc(flag_up("gdn_exp_gc"), 1)
                silu(n)
            a.wait_ge(sem("gdn_z_psum"), 2)
            A.activation(z_silu, ps[:, 2:4, :], ACT.Silu).then_inc(flag_up("gdn_z"), 1)
            a.wait_ge(sem("gdn_qkv"), 4)
            A.activation(pre[:], view(qkvT[:, 0:8, :].rearrange("p a b -> p (a b)"), (TILES, D)), ACT.Square).then_inc(sem("gdn_sq"), 1)
            A.activation(side[:], view(qkvT[:, 8:16, :].rearrange("p a b -> p (a b)"), (TILES, D)), ACT.Square).then_inc(sem("gdn_sq"), 1)
            a.wait_ge(sem("gdn_sum_psum"), 1)
            A.activation(pre[:], ps[:, 0:2, :], ACT.Sqrt, bias=eps(EPS6_128), scale=float(P)).then_inc(sem("gdn_root"), 1)
            a.wait_ge(sem("gdn_sum_psum"), 2)
            A.activation(side[:], ps[:, 2:4, :], ACT.Sqrt, bias=eps(EPS6)).then_inc(sem("gdn_root"), 1)

        def v_gdn_in(v):
            v.wait_ge(sem("small_loaded"), 16)
            v.wait_ge(*flag("gdn_ba_psum"))
            for t in range(TILES):
                m = V.tensor_copy(logits2[:, :, t], ps[:, 3, 512 + 16 * t:528 + 16 * t])
            m.then_inc(flag_up("gdn_ba"), 1)
            v.wait_ge(*flag("gdn_ba"))
            V.tensor_tensor(g_in, logits2[:, 8:16, :], spread(param("dt_bias"), TILES), ALU.add).then_inc(flag_up("gdn_g_in"), 1)
            v.wait_ge(*flag("gdn_log"))
            v.wait_ge(*flag("gdn_g_in"))
            link(v, V.scalar_tensor_tensor(out=g_log, in0=g_in, scalar=0.0, in1=g_log, op0=ALU.max, op1=ALU.add))
            V.scalar_tensor_tensor(out=g_dec, in0=g_log, scalar=-1.0, in1=g_ea, op0=ALU.mult, op1=ALU.mult)\
             .then_inc(flag_up("gdn_g"), 1)
            for n in range(6):
                v.wait_ge(sem("gdn_tap"), n + 1)
                for tap in (2, 1, 0):
                    s = 3 - tap
                    for b in range(4):
                        m = V.scalar_tensor_tensor(out=qkvT[:, 4 * n + b, s:SEQ], in0=ps[:, n % 4, b * SEQ:(b + 1) * SEQ - s],
                                                   scalar=conv_w[:, 4 * n + b, tap:tap + 1], in1=qkvT[:, 4 * n + b, s:SEQ],
                                                   op0=ALU.mult, op1=ALU.add)
                    if tap:
                        link(v, m)
                m.then_inc(sem("gdn_conv"), 1)
                if n == 1:
                    v.wait_ge(*flag("gdn_rows_psum"))
                    V.tensor_copy(gc, ps[:, 3, 0:16].rearrange("p (t h) -> p h t", t=TILES)).then_inc(sem("gdn_rows"), 1)
                    V.tensor_copy(rowsT.rearrange("p a t c -> p (a t c)"), ps[0:8, 3, 512:1024]).then_inc(sem("gdn_rows"), 1)
            v.wait_ge(*flag("gdn_exp_gc"))
            link(v, V.tensor_tensor(bg, beta, exp_gc, ALU.mult))
            for n, root in enumerate((pre, side)):
                v.wait_ge(sem("gdn_root"), n + 1)
                flat = root[:].rearrange("p a b -> p (a b)")
                link(v, V.reciprocal(flat, flat))
                blocks = qkvT[:, 8 * n:8 * n + 8, :].rearrange("p a b -> p (a b)")
                V.tensor_tensor(blocks, blocks, flat, ALU.mult).then_inc(sem("gdn_unit"), 1)

        def pe_gdn_sums(pe):
            for n, src in enumerate((pre, side)):
                pe.wait_ge(sem("gdn_sq"), n + 1)
                if n == 0:
                    pe.wait_ge(sem("gdn_conv"), 6)
                else:
                    pe.wait_ge(*flag("gdn_z"))
                for q in range(4):
                    m = T.matmul(ps[:, 2 * n + q // 2, (q % 2) * 512:(q % 2) * 512 + 512], ones,
                                 src[:, q // 2, (q % 2) * 512:(q % 2) * 512 + 512], start=True, stop=True)
                m.then_inc(sem("gdn_sum_psum"), 1)

        def pe_gdn_scores(pe):
            pick = table("pick_head")

            def rows_out(which, out_, done):
                for h in range(HEADS):
                    m = T.matmul(out_[:, h * SEQ:(h + 1) * SEQ], pick[0:8, h * P:(h + 1) * P],
                                 rowsT[:, which].rearrange("p t c -> p (t c)"), start=True, stop=True)
                m.then_inc(sem(done), 1)

            pe.wait_ge(sem("gdn_root"), 2)
            rows_out(0, pair01, "gdn_G_psum")
            rows_out(1, pair23, "gdn_B_psum")
            pe.wait_ge(sem("gdn_unit"), 2)
            pe.wait_ge(*flag("gdn_diff"))
            for h in range(HEADS):
                for t in range(TILES):
                    k = qkvT[:, 8 + h, t * P:(t + 1) * P]
                    m = T.matmul(system(pair01, h, t), k, k, start=True, stop=True)
            m.then_inc(flag_up("gdn_KK_psum"), 1)
            pe.wait_ge(*flag("gdn_DB"))
            for h in range(HEADS):
                for t in range(TILES):
                    m = T.matmul(system(pair23, h, t), qkvT[:, 8 + h, t * P:(t + 1) * P], qkvT[:, h, t * P:(t + 1) * P],
                                 start=True, stop=True)
            m.then_inc(flag_up("gdn_QK_psum"), 1)
            pe.wait_ge(*flag("gdn_LT"))
            for h in range(HEADS):
                for t in range(TILES):
                    m = T.transpose(system(pair01, h, t), qkvT[:, 8 + h, t * P:(t + 1) * P], ident)
            m.then_inc(flag_up("gdn_k_psum"), 1)
            pe.wait_ge(*flag("gdn_QKT"))
            for h in range(HEADS):
                for t in range(TILES):
                    m = T.transpose(system(pair23, h, t), qkvT[:, 16 + h, t * P:(t + 1) * P], ident)
            m.then_inc(flag_up("gdn_v_psum"), 1)

        def a_gdn_scores(a):
            a.wait_ge(*flag("gdn_diff"))
            A.activation(DEC, DEC, ACT.Exp).then_inc(flag_up("gdn_exp"), 1)

        def v_gdn_scores(v):
            g3 = lambda flat: flat.rearrange("p (s c) -> p s c", c=P)
            v.wait_ge(sem("gdn_G_psum"), 1)
            for h in range(HEADS):
                for t in range(TILES):
                    m = V.tensor_scalar(system(DEC, h, t), system(pair01, h, t), gc[:, h, t:t + 1], 0.0,
                                        ALU.subtract, ALU.min)
            m.then_inc(flag_up("gdn_diff"), 1)
            v.wait_ge(*flag("gdn_exp"))
            link(v, V.tensor_tensor(g3(DEC), g3(DEC), repeat(upto, 16), ALU.mult))
            v.wait_ge(sem("gdn_B_psum"), 1)
            V.tensor_tensor(LT, DEC, pair23, ALU.mult).then_inc(flag_up("gdn_DB"), 1)
            v.wait_ge(*flag("gdn_DB"))
            link(v, V.tensor_tensor(g3(LT), g3(LT), repeat(table("strict"), 16), ALU.mult))
            v.wait_ge(*flag("gdn_KK_psum"))
            V.tensor_tensor(LT, LT, pair01, ALU.mult).then_inc(flag_up("gdn_LT"), 1)
            v.wait_ge(*flag("gdn_QK_psum"))
            V.tensor_tensor(QKT, DEC, pair23, ALU.mult).then_inc(flag_up("gdn_QKT"), 1)
            v.wait_ge(*flag("gdn_LT"))
            for g in range(2):
                V.tensor_tensor(g3(half(MT, g)), g3(half(LT, g)), repeat(table("level0"), 8), ALU.mult)\
                 .then_inc(sem("gdn_MT"), 1)
            v.wait_ge(sem("gdn_MT"), 2)
            for g in range(2):
                V.tensor_tensor(g3(half(TT, g)), repeat(ident, 8), g3(half(MT, g)), ALU.subtract).then_inc(sem("gdn_TT"), 1)
            v.wait_ge(*flag("gdn_k_psum"))
            last_col = heads16(DEC)[:, :, 0, P - 1:P].to_broadcast((P, HEADS, P))
            V.tensor_tensor(g3(KD), heads16(pair01)[:, :, 0, :], last_col, ALU.mult)
            V.tensor_tensor(g3(KBG), heads16(pair01)[:, :, 1, :], bg[:, :, 1:2].to_broadcast((P, HEADS, P)), ALU.mult)\
             .then_inc(flag_up("gdn_k_ready"), 1)
            v.wait_ge(*flag("gdn_v_psum"))
            V.tensor_tensor(g3(VB), g3(pair23), spread(beta.rearrange("p h t -> p (h t)"), P), ALU.mult)\
             .then_inc(flag_up("gdn_v_ready"), 1)

        def pe_gdn_inverse(pe):
            s_MT, s_T, s_TT, s_P = sem("gdn_MT"), sem("gdn_T"), sem("gdn_TT"), sem("gdn_P")
            P_psum, T_psum, TT_psum = sem("gdn_P_psum"), sem("gdn_T_psum"), sem("gdn_TT_psum")

            def systems(out_, lhsT, rhs, g, done):
                for q in range(8):
                    a_, b_ = 1024 * g + P * q, 1024 * g + P * (q + 1)
                    m = T.matmul(out_[:, P * q:P * (q + 1)], lhsT[:, a_:b_], rhs[:, a_:b_] if rhs is not None else ident,
                                 start=True, stop=True)
                m.then_inc(done, 1)

            def level(l, update_T=True):
                for g in range(2):
                    pe.wait_ge(s_MT, 2 * l + g + 1)
                    pe.wait_ge(s_T, 2 * l + g - 1)
                    pe.wait_ge(s_TT, 2 * l + g - 1)
                    systems(ps[:, g, :], MT, TI, g, P_psum)
                for g in range(2):
                    pe.wait_ge(s_P, 2 * l + g - 1)
                    if update_T:
                        systems(ps[:, 2 + g, :], TT, PR, g, T_psum)
                    systems(ps[:, g, :], PR, TT, g, TT_psum)

            pe.wait_ge(*flag("gdn_k_ready"))
            for g in range(2):
                pe.wait_ge(s_MT, g + 1)
                systems(ps[:, g, :], MT, None, g, P_psum)
            pe.wait_ge(*flag("gdn_v_ready"))
            with pe.Fori(1, LEVELS - 1) as l:
                level(l)
            level(LEVELS - 1, update_T=False)

        def a_gdn_inverse(a):
            def level(l):
                for g in range(2):
                    a.wait_ge(sem("gdn_P_psum"), 2 * l + g + 1)
                    A.copy(half(PR, g), ps[:, g, :]).then_inc(sem("gdn_P"), 1)

            with a.Fori(1, LEVELS) as l:
                level(l)

        def v_gdn_inverse(v):
            g3 = lambda flat: flat.rearrange("p (s c) -> p s c", c=P)
            masks_at, _ = places["table"]["level0"]

            def mask(l):
                return tab[:, masks_at:masks_at + LEVELS * P].rearrange("p (l c) -> p l c", c=P)[:, l, :]

            def next_M(l):
                for g in range(2):
                    v.wait_ge(sem("gdn_P_psum"), 2 * l + g - 1)
                    V.tensor_tensor(g3(half(MT, g)), g3(half(LT, g)), repeat(mask(l), 8), ALU.mult)\
                     .then_inc(sem("gdn_MT"), 1)

            def update_TT(l, g):
                v.wait_ge(sem("gdn_TT_psum"), 2 * l + g - 1)
                V.tensor_tensor(half(TT, g), half(TT, g), ps[:, g, :], ALU.subtract).then_inc(sem("gdn_TT"), 1)

            for g in range(2):
                v.wait_ge(sem("gdn_P_psum"), g + 1)
                V.tensor_tensor(g3(half(TI, g)), repeat(ident, 8), g3(ps[:, g, :]), ALU.subtract).then_inc(sem("gdn_T"), 1)
            next_M(1)
            with v.Fori(1, LEVELS - 1) as l:
                next_M(l + 1)
                for g in range(2):
                    v.wait_ge(sem("gdn_T_psum"), 2 * l + g - 1)
                    V.tensor_tensor(half(TI, g), half(TI, g), ps[:, 2 + g, :], ALU.subtract).then_inc(sem("gdn_T"), 1)
                    update_TT(l, g)
            for g in range(2):
                update_TT(LEVELS - 1, g)

        def pe_gdn_out(pe):
            head = lambda flat, h: flat[:, h * P:(h + 1) * P]
            pe.wait_ge(sem("gdn_TT"), 2 * LEVELS)
            for h in range(HEADS):
                m = T.matmul(head(ps[:, 0, :], h), system(TT, h, 0), system(VB, h, 0), start=True, stop=True)
            m.then_inc(flag_up("gdn_u0_psum"), 1)
            for h in range(HEADS):
                m = T.matmul(head(ps[:, 1, :], h), head(KBG, h), system(TT, h, 1), start=True, stop=True)
            m.then_inc(flag_up("gdn_wT_psum"), 1)
            pe.wait_ge(*flag("gdn_u0"))
            for h in range(HEADS):
                m = T.matmul(head(ps[:, 2, :], h), head(KD, h), head(U0, h), start=True, stop=True)
            m.then_inc(flag_up("gdn_state_psum"), 1)
            for h in range(HEADS):
                m = T.matmul(head(ps[:, 0, :], h), system(QKT, h, 0), head(U0, h), start=True, stop=True)
            m.then_inc(flag_up("gdn_o0_psum"), 1)
            pe.wait_ge(*flag("gdn_wT"))
            pe.wait_ge(*flag("gdn_state"))
            for h in range(HEADS):
                T.matmul(head(ps[:, 3, :], h), system(TT, h, 1), system(VB, h, 1), start=True, stop=False)
                m = T.matmul(head(ps[:, 3, :], h), head(WTN, h), head(STATE, h), start=False, stop=True)
            m.then_inc(flag_up("gdn_vnew_psum"), 1)
            for h in range(HEADS):
                m = T.matmul(head(ps[:, 1, :], h), qkvT[:, h, P:SEQ], head(STATE, h), start=True, stop=True)
            m.then_inc(flag_up("gdn_os_psum"), 1)
            pe.wait_ge(*flag("gdn_vnew"))
            for h in range(HEADS):
                m = T.matmul(head(ps[:, 2, :], h), system(QKT, h, 1), head(VNEW, h), start=True, stop=True)
            m.then_inc(flag_up("gdn_o1_psum"), 1)

        def a_gdn_out(a):
            a.wait_ge(*flag("gdn_u0_psum"))
            A.copy(U0, ps[:, 0, :]).then_inc(flag_up("gdn_u0"), 1)
            a.wait_ge(*flag("gdn_state_psum"))
            A.copy(STATE, ps[:, 2, :]).then_inc(flag_up("gdn_state"), 1)
            a.wait_ge(*flag("gdn_vnew_psum"))
            A.copy(VNEW, ps[:, 3, :]).then_inc(flag_up("gdn_vnew"), 1)
            a.wait_ge(sem("gdn_o"), 2)
            A.activation(pre[:], O, ACT.Square).then_inc(flag_up("gdn_o_sq"), 1)
            a.wait_ge(*flag("gdn_o_ss"))
            A.activation(rms16, rms16, ACT.Sqrt, bias=eps(EPS6), scale=1.0 / P).then_inc(flag_up("gdn_o_rms"), 1)

        def v_gdn_out(v):
            g3 = lambda flat: flat.rearrange("p (s c) -> p s c", c=P)
            v.wait_ge(*flag("gdn_wT_psum"))
            V.tensor_scalar(WTN, ps[:, 1, :], -1.0, None, ALU.mult).then_inc(flag_up("gdn_wT"), 1)
            v.wait_ge(*flag("gdn_o0_psum"))
            V.tensor_copy(O[:, 0, :], ps[:, 0, :]).then_inc(sem("gdn_o"), 1)
            v.wait_ge(*flag("gdn_os_psum"))
            link(v, V.tensor_tensor(g3(O[:, 1, :]), g3(ps[:, 1, :]), exp_gc[:, :, 1:2].to_broadcast((P, HEADS, P)), ALU.mult))
            v.wait_ge(*flag("gdn_o1_psum"))
            V.tensor_tensor(O[:, 1, :], O[:, 1, :], ps[:, 2, :], ALU.add).then_inc(sem("gdn_o"), 1)
            v.wait_ge(*flag("gdn_o_sq"))
            V.tensor_reduce(rms16, pre[:].rearrange("p t (h c) -> p (t h) c", c=P), AX.X, ALU.add).then_inc(flag_up("gdn_o_ss"), 1)
            v.wait_ge(*flag("gdn_o_rms"))
            link(v, V.reciprocal(rms16, rms16))
            o3 = PR.rearrange("p (s c) -> p s c", c=P)
            link(v, V.tensor_tensor(o3, o3, spread(rms16, P), ALU.mult))
            link(v, V.tensor_tensor(o3, o3, repeat(param("norm_w"), 16), ALU.mult))
            for t in range(TILES):
                V.tensor_tensor(pre[:, t, :], O[:, t, :], z_silu[:, t, :], ALU.mult).then_inc(sem("gdn_y"), 1)

        def v_residual(v, done, pairs, scale):
            for t in range(TILES):
                v.wait_ge(sem(done), t + 1)
                m = V.scalar_tensor_tensor(out=pre[:, t, :], in0=x[:, t, :], scalar=scale, in1=ps[:, pairs[t], :],
                                           op0=ALU.mult, op1=ALU.add)
            link(v, m)

        SEL, WIN, FOX = range(3)
        HD = 64
        COLS = P + SEQ
        projT = scratch(0, 16, SEQ)
        qnT, kvcT, ksT, kwT, qfT, kfT = projT[:, 0:4], projT[:, 4:6], projT[:, 6], projT[:, 7], projT[:, 8:12], projT[:, 12:16]
        nat = scratch(4096, TILES, 288)
        vf = scratch(4672, TILES, 512)
        cmp_in = scratch(5696, 32, 30)
        fox_bias = scratch(6656, HEADS, COLS)
        prob = view(slot01[:, 0:1536], (2, 2, COLS))
        probT = view(slot01[:, 1536:3072], (2, 6, P))
        o_att = view(slot01[:, 3072:6144], (3, TILES, 512))
        v_blk = view(slot01[:, 6144:6656], (2, 4, HD))
        pc32 = view(slot01[:, 6656:7168], (16, 32))
        pcT = view(slot01[:, 7168:7680], (4, P))
        m_small = side[:, 1, 0:512]
        raw_c = view(m_small[:, 0:256], (16, 16))
        c16 = m_small[:, 256:272]
        hid = view(m_small[:, 272:336], (2, 2, 16))
        kcc = m_small[:, 336:352]
        mx = view(m_small[:, 352:368], (2, 8))
        f_c, f_abs, f_log = (view(m_small[:, 368 + 16 * n:384 + 16 * n], (HEADS, TILES)) for n in range(3))
        sums = view(m_small[:, 416:464], (3, TILES, HEADS))
        att4, att4b = m_small[:, 464:468], m_small[:, 468:472]
        f_cum = view(m_small[:, 472:488], (HEADS, TILES))
        gate48 = side[:, 0, 0:48]
        hv4 = view(side[:, 0, 64:320], (2, 4, 32))
        cumT = side[0:8, 0, 512:768]
        mix = pre
        ATT_SLOTS = (4, 5, 0, 1, 2, 3)
        STEPS = [(b, r) for b in (SEL, WIN, FOX) for r in range(4)]

        def pe_att_in(pe):
            pe.wait_ge(sem("T"), before(TURNS, "rn1") + 2)

            def turned(out_, w, width, cols):
                for k in range(KT):
                    m = T.matmul(out_, cols(w[:, k * width:(k + 1) * width]), xT[:, k, :], start=(k == 0), stop=(k == KT - 1))
                return m

            def plain(out_, t, w, width, c0, cn):
                for k in range(KT):
                    m = T.matmul(out_, xT[:, k, t * P:(t + 1) * P], w[:, k * width + c0:k * width + c0 + cn],
                                 start=(k == 0), stop=(k == KT - 1))
                return m

            w = take(pe, 4)
            for r in range(4):
                m = turned(ps[:, 0, r * SEQ:(r + 1) * SEQ], w, 512,
                           lambda a: a[:, r * P:(r + 1) * P])
            m.then_inc(sem("att_qn_psum"), 1)
            w = take(pe, 5)
            for g in range(2):
                turned(ps[:, 1, g * SEQ:(g + 1) * SEQ], w, 512,
                       lambda a: a[:, g * P:(g + 1) * P])
            turned(ps[:, 1, 512:768], w, 512, lambda a: a[:, 256:384])
            for t in range(TILES):
                m = plain(ps[:, 3, 512 * t:512 * t + 128], t, w, 512, 384, 128)
            m.then_inc(sem("att_in1_read"), 1)
            w = take(pe, 0)
            turned(ps[:, 1, 768:1024], w, 280, lambda a: a[:, 0:128]).then_inc(flag_up("att_kv_psum"), 1)
            w_fg = param("w_fg")
            for t in range(TILES):
                plain(ps[:, 3, 512 * t + 128:512 * t + 280], t, w, 280, 128, 152)
                m = plain(ps[:, 3, 512 * t + 280:512 * t + 288], t, w_fg, 8, 0, 8)
            m.then_inc(flag_up("att_nat_psum"), 1)
            w = take(pe, 1)
            for r in range(4):
                m = turned(ps[:, 2, r * SEQ:(r + 1) * SEQ], w, 512, lambda a: a[:, r * P:(r + 1) * P])
            m.then_inc(flag_up("att_qf_psum"), 1)
            w = take(pe, 2)
            pe.wait_ge(*flag("att_qn"))
            for r in range(4):
                m = turned(ps[:, 0, r * SEQ:(r + 1) * SEQ], w, 512, lambda a: a[:, r * P:(r + 1) * P])
            m.then_inc(sem("att_kf_psum"), 1)
            w = take(pe, 3)
            pe.wait_ge(*flag("att_kv"))
            for t in range(TILES):
                m = plain(ps[:, 1, 512 * t:512 * t + 512], t, w, 512, 0, 512)
            m.then_inc(sem("att_vf_psum"), 1)

        def v_att_in(v):
            v.wait_ge(*flag("att_kv_psum"))
            V.tensor_copy(projT[:, 4:8, :], view(ps[:, 1, :], (4, SEQ))).then_inc(flag_up("att_kv"), 1)
            v.wait_ge(*flag("att_nat_psum"))
            V.tensor_copy(nat, view(ps[:, 3, :], (TILES, 512))[:, :, 0:288]).then_inc(flag_up("att_nat"), 1)
            v.wait_ge(*flag("att_kv"))
            pe_cols = param("pe")
            for g in range(2):
                for q in range(2):
                    tokens_ = kvcT[:, g, 16 * q:16 * q + 240].rearrange("p (j i) -> p i j", i=16)
                    m = V.tensor_tensor(cmp_in[:, 16 * q:16 * q + 16, 15 * g:15 * g + 15], tokens_,
                                        spread(pe_cols[:, 16 * q:16 * q + 16], 15), ALU.add)
            m.then_inc(flag_up("cmp_in"), 1)
            v.wait_ge(*flag("att_nat"))
            b_fg = param("b_fg")[:, None, :].to_broadcast((P, TILES, HEADS))
            V.tensor_tensor(f_c.rearrange("p h t -> p t h"), nat[:, :, 280:288], b_fg, ALU.add).then_inc(flag_up("fox_f"), 1)
            v.wait_ge(sem("att_kf_psum"), 1)
            V.tensor_copy(projT[:, 12:16, :], view(ps[:, 0, :], (4, SEQ))).then_inc(flag_up("att_kf"), 1)
            v.wait_ge(*flag("fox_log"))
            V.scalar_tensor_tensor(out=f_log, in0=f_c, scalar=0.0, in1=f_log, op0=ALU.min, op1=ALU.subtract)\
             .then_inc(flag_up("fox_lf"), 1)

        def a_att_in(a):
            a.wait_ge(sem("att_qn_psum"), 1)
            A.copy(projT[:, 0:4, :], view(ps[:, 0, :], (4, SEQ))).then_inc(flag_up("att_qn"), 1)
            a.wait_ge(*flag("att_nat"))
            A.activation(view(gate48, (TILES, 24)), nat[:, :, 256:280], ACT.Sigmoid).then_inc(flag_up("att_gates"), 1)
            a.wait_ge(*flag("fox_f"))
            link(a, A.activation(f_abs, f_c, ACT.Abs), "a")
            link(a, A.activation(f_abs, f_abs, ACT.Exp, scale=-1.0), "a")
            A.activation(f_log, f_abs, ACT.Ln, bias=eps(ONE)).then_inc(flag_up("fox_log"), 1)
            a.wait_ge(*flag("att_qf_psum"))
            A.copy(projT[:, 8:12, :], view(ps[:, 2, :], (4, SEQ))).then_inc(flag_up("att_qf"), 1)
            a.wait_ge(sem("att_vf_psum"), 1)
            A.copy(vf, view(ps[:, 1, :], (TILES, 512))).then_inc(flag_up("att_vf"), 1)

        def pe_fox_bias(pe):
            lf = f_log
            pe.wait_ge(*flag("fox_lf"))
            pe.wait_ge(*flag("att_qf"))
            both = tab[:, places["table"]["upto"][0]:places["table"]["upto"][0] + 2 * P]
            T.matmul(ps[:, 2, 0:8], upto, lf[:, :, 0], start=True, stop=True)
            T.matmul(ps[:, 2, 8:16], ones, lf[:, :, 0], start=True, stop=False)
            T.matmul(ps[:, 2, 8:16], upto, lf[:, :, 1], start=False, stop=True)
            T.matmul(ps[0:8, 2, 512:768], lf[:, :, 0], both, start=True, stop=False)
            T.matmul(ps[0:8, 2, 640:768], lf[:, :, 1], upto, start=False, stop=True).then_inc(flag_up("fox_cum_psum"), 1)
            pe.wait_ge(sem("fox_cum"), 2)
            pe.wait_ge(*flag("att_kf"))
            pe.wait_ge(*flag("att_vf"))
            pick = table("pick_head")
            for h in range(HEADS):
                m = T.matmul(pair01[:, h * SEQ:(h + 1) * SEQ], pick[0:8, h * P:(h + 1) * P], cumT, start=True, stop=True)
            m.then_inc(flag_up("fox_rows_psum"), 1)

        def v_fox_bias(v):
            v.wait_ge(*flag("fox_cum_psum"))
            V.tensor_copy(f_cum.rearrange("p h t -> p t h"), view(ps[:, 2, 0:16], (TILES, HEADS))).then_inc(sem("fox_cum"), 1)
            V.tensor_copy(cumT, ps[0:8, 2, 512:768]).then_inc(sem("fox_cum"), 1)
            v.wait_ge(sem("fox_cum"), 2)
            v.wait_ge(*flag("fox_rows_psum"))
            masks = table("mask_neg")
            for h in range(HEADS):
                for t, (c0, c1) in enumerate(((0, P), (P, COLS))):
                    m = V.scalar_tensor_tensor(out=fox_bias[:, h, c0:c1], in0=pair01[:, h * SEQ:h * SEQ + c1 - c0],
                                               scalar=f_cum[:, h, t:t + 1], in1=masks[:, c0:c1],
                                               op0=ALU.subtract, op1=ALU.subtract)
            m.then_inc(flag_up("fox_bias"), 1)

        def pe_compress(pe):
            w = take(pe, 4)
            pe.wait_ge(*flag("cmp_in"))
            pe.wait_ge(sem("fox_cum"), 2)
            for i in range(32):
                for kv in range(2):
                    rows_ = slice(64 * kv, 64 * kv + 64)
                    m = T.matmul(ps[:, 2, 512 * kv:512 * kv + 30], w[rows_, i * P:(i + 1) * P], cmp_in[rows_, i, :],
                                 start=(i == 0), stop=(i == 31))
            m.then_inc(flag_up("cmp_hid_psum"), 1)
            pe.wait_ge(sem("cmp_hid"), 2)
            pe.wait_ge(*flag("cmp_hv4"))
            pe.wait_ge(*flag("att_nat"))
            for g in range(2):
                T.matmul(ps[HD * g:HD * g + HD, 3, 0:15], param("cmp2_k"), hid[:, 0, g, 0:15], start=True, stop=True)
            for g in range(2):
                m = T.matmul(ps[:, 3, 512 + HD * g:512 + HD * g + HD], hv4[:, g].rearrange("p r j -> p (r j)"), param("cmp2_v"),
                             start=True, stop=True)
            m.then_inc(flag_up("cmp_kv_psum"), 1)
            pe.wait_ge(*flag("cmp_kcc"))
            for g in range(2):
                rows_ = slice(HD * g, HD * g + HD)
                for t in range(TILES):
                    for r in range(4):
                        at = 512 * g + (4 * t + r) * 16
                        m = T.matmul(ps[:, 2, at:at + 16], qnT[rows_, r, t * P:(t + 1) * P], kcc[rows_, :], start=True, stop=True)
            m.then_inc(flag_up("cmp_score_psum"), 1)
            pe.wait_ge(*flag("cmp_prob"))
            pe.wait_ge(*flag("cmp_vblk"))
            for q in range(4):
                m = T.transpose(ps[:, 2, q * P:(q + 1) * P], pc32[:, 4 * q:4 * q + 4, :].rearrange("p r j -> p (r j)"), ident)
            m.then_inc(flag_up("cmp_pT_psum"), 1)
            pe.wait_ge(*flag("cmp_pT"))
            for t in range(TILES):
                for g in range(2):
                    m = T.matmul(ps[:, 3, 512 * t + 256 * g:512 * t + 256 * g + 256], pcT[:, 2 * g + t, :],
                                 v_blk[:, g].rearrange("p r d -> p (r d)"), start=True, stop=True)
            m.then_inc(flag_up("cmp_o_psum"), 1)

        def a_compress(a):
            a.wait_ge(*flag("cmp_clear"))
            a.wait_ge(*flag("cmp_hid_psum"))
            for kv in range(2):
                A.activation(hid[:, kv, :, 0:15], view(ps[:, 2, 512 * kv:512 * kv + 30], (2, 15)), ACT.Gelu_apprx_tanh)\
                 .then_inc(sem("cmp_hid"), 1)
            a.wait_ge(*flag("cmp_diff"))
            A.activation(raw_c, raw_c, ACT.Exp).then_inc(flag_up("cmp_exp"), 1)

        def v_compress(v):
            V.memset(m_small[:, 272:352], 0.0).then_inc(flag_up("cmp_clear"), 1)
            V.memset(pc32, 0.0).then_inc(sem("cmp_clear2"), 1)
            V.memset(hv4, 0.0).then_inc(sem("cmp_clear2"), 1)
            v.wait_ge(sem("cmp_clear2"), 2)
            v.wait_ge(*flag("cmp_clear"))
            v.wait_ge(sem("cmp_hid"), 2)
            for g in range(2):
                m = V.tensor_copy(hv4[:, g, :, 0:16], hid[:, 1, g, None, :].to_broadcast((P, 4, 16)))
            m.then_inc(flag_up("cmp_hv4"), 1)
            v.wait_ge(*flag("cmp_kv_psum"))
            V.tensor_copy(kcc[:, 0:15], ps[:, 3, 0:15]).then_inc(flag_up("cmp_kcc"), 1)
            for g in range(2):
                m = V.tensor_tensor(v_blk[:, g], ps[:, 3, None, 512 + HD * g:512 + HD * g + HD].to_broadcast((P, 4, HD)),
                                    spread(table("own_row"), HD), ALU.mult)
            m.then_inc(flag_up("cmp_vblk"), 1)
            v.wait_ge(*flag("cmp_score_psum"))
            bias, mask = view(table("cmp_bias"), (16, 16)), view(table("cmp_mask"), (16, 16))
            for g in range(2):
                m = V.scalar_tensor_tensor(out=raw_c[:, 8 * g:8 * g + 8, :], in0=view(ps[:, 2, 512 * g:512 * g + 128], (8, 16)),
                                           scalar=HD ** -0.5, in1=bias[:, 8 * g:8 * g + 8, :], op0=ALU.mult, op1=ALU.add)
            link(v, m)
            link(v, V.tensor_reduce(c16, raw_c, AX.X, ALU.max))
            V.tensor_tensor(raw_c, raw_c, spread(c16, 16), ALU.subtract).then_inc(flag_up("cmp_diff"), 1)
            v.wait_ge(*flag("cmp_exp"))
            link(v, V.tensor_tensor(raw_c, raw_c, mask, ALU.mult))
            link(v, V.tensor_reduce(c16, raw_c, AX.X, ALU.add))
            link(v, V.tensor_scalar(c16, c16, 1e-30, None, ALU.max))
            link(v, V.reciprocal(c16, c16))
            V.tensor_tensor(pc32[:, :, 0:16], raw_c, spread(c16, 16), ALU.mult).then_inc(flag_up("cmp_prob"), 1)
            v.wait_ge(*flag("cmp_pT_psum"))
            V.tensor_copy(pcT, view(ps[:, 2, 0:512], (4, P))).then_inc(flag_up("cmp_pT"), 1)
            v.wait_ge(*flag("cmp_o_psum"))
            v.wait_ge(*flag("att_gates"))
            V.tensor_tensor(mix[:, :, 0:512].rearrange("p t (h d) -> p t h d", d=HD),
                            ps[:, 3, :].rearrange("p (t h d) -> p t h d", t=TILES, d=HD),
                            gate48.rearrange("p (t h b) -> p t h b", t=TILES, b=3)[:, :, :, 0:1].to_broadcast((P, TILES, HEADS, HD)),
                            ALU.mult).then_inc(flag_up("cmp_o"), 1)

        def head_of(branch, r, half_):
            return 2 * r + half_ if branch == FOX else 4 * half_ + r

        def pe_attention(pe):
            def scores(n):
                branch, r = STEPS[n]
                if n == 0:
                    pe.wait_ge(*flag("fox_bias"))
                if n >= 2:
                    pe.wait_ge(sem("att_raw"), n - 1)
                for half_ in range(2):
                    rows_ = slice(HD * half_, HD * half_ + HD)
                    q = (qfT if branch == FOX else qnT)[rows_, r, :]
                    k = {SEL: ksT, WIN: kwT, FOX: kfT[:, r, :]}[branch][rows_, :]
                    out_ = ps[:, n % 2, 512 * half_:512 * half_ + COLS]
                    T.matmul(out_[:, 0:P], q[:, 0:P], k[:, 0:P], start=True, stop=True)
                    m = T.matmul(out_[:, P:COLS], q[:, P:SEQ], k, start=True, stop=True)
                m.then_inc(sem("att_score_psum"), 1)

            def turn(n):
                pe.wait_ge(sem("att_prob"), n + 1)
                if n >= 1:
                    pe.wait_ge(sem("att_probT"), n)
                else:
                    pe.wait_ge(*flag("cmp_pT"))
                for half_ in range(2):
                    for b in range(3):
                        at = (3 * half_ + b) * P
                        m = T.transpose(ps[:, 2, at:at + P], prob[:, n % 2, half_, b * P:(b + 1) * P], ident)
                m.then_inc(sem("att_probT_psum"), 1)

            def values(n):
                branch, r = STEPS[n]
                pe.wait_ge(sem("att_probT"), n + 1)
                if r == 0:
                    if branch == SEL:
                        pe.wait_ge(*flag("cmp_o"))
                    else:
                        pe.wait_ge(sem("att_o"), branch)
                for half_ in range(2):
                    h = head_of(branch, r, half_)

                    def val(t):
                        return vf[:, t, HD * h:HD * h + HD] if branch == FOX else \
                            nat[:, t, 128 * branch + HD * half_:128 * branch + HD * half_ + HD]

                    o0, o1 = ps[:, 3, HD * h:HD * h + HD], ps[:, 3, 512 + HD * h:512 + HD * h + HD]
                    T.matmul(o0, probT[:, n % 2, 3 * half_, :], val(0), start=True, stop=True)
                    T.matmul(o1, probT[:, n % 2, 3 * half_ + 1, :], val(0), start=True, stop=False)
                    m = T.matmul(o1, probT[:, n % 2, 3 * half_ + 2, :], val(1), start=False, stop=True)
                m.then_inc(sem("att_value_psum"), 1)

            scores(0)
            for n in range(len(STEPS)):
                if n + 1 < len(STEPS):
                    scores(n + 1)
                turn(n)
                values(n)

        def v_attention(v):
            for n, (branch, r) in enumerate(STEPS):
                v.wait_ge(sem("att_score_psum"), n + 1)
                if n >= 2:
                    v.wait_ge(sem("att_probT_psum"), n - 1)
                for half_ in range(2):
                    h = head_of(branch, r, half_)
                    raw, src = prob[:, n % 2, half_, :], ps[:, n % 2, 512 * half_:512 * half_ + COLS]
                    if branch == FOX:
                        m = V.scalar_tensor_tensor(out=raw, in0=src, scalar=HD ** -0.5, in1=fox_bias[:, h, :],
                                                   op0=ALU.mult, op1=ALU.subtract)
                    else:
                        m = V.scalar_tensor_tensor(out=raw, in0=src, scalar=HD ** -0.5 * 2.0 ** (h + 1),
                                                   in1=table("neg_dist"), op0=ALU.mult, op1=ALU.add)
                m.then_inc(sem("att_raw"), 1)
                v.wait_ge(sem("att_raw"), n + 1)
                top = view(mx[:, n % 2, 0:4], (2, TILES))
                V.tensor_reduce(top[:, :, 0:1], prob[:, n % 2, :, 0:P], AX.X, ALU.max, negate=True)
                link(v, V.tensor_reduce(top[:, :, 1:2], prob[:, n % 2, :, P:COLS], AX.X, ALU.max, negate=True))
                scale = ones[:, 0:4] if branch == FOX else table("slopes")[:, 4 * r:4 * r + 4]
                V.tensor_tensor(mx[:, n % 2, 4:8], mx[:, n % 2, 0:4], scale, ALU.mult).then_inc(sem("att_top"), 1)
                if r == 0 and branch > SEL:
                    v_att_out(v, branch - 1)
            v_att_out(v, FOX)

        def v_att_out(v, branch):
            v.wait_ge(sem("att_value_psum"), 4 * branch + 4)
            V.tensor_copy(o_att[:, branch], view(ps[:, 3, :], (TILES, 512))).then_inc(sem("att_o"), 1)

        def a_attention(a):
            def turn(n):
                a.wait_ge(sem("att_probT_psum"), n + 1)
                if n >= 2:
                    a.wait_ge(sem("att_value_psum"), n - 1)
                A.copy(probT[:, n % 2], view(ps[:, 2, 0:768], (6, P))).then_inc(sem("att_probT"), 1)

            for n, (branch, r) in enumerate(STEPS):
                a.wait_ge(sem("att_top"), n + 1)
                for half_ in range(2):
                    h = head_of(branch, r, half_)
                    for t, (c0, c1) in enumerate(((0, P), (P, COLS))):
                        m = A.activation(prob[:, n % 2, half_, c0:c1], prob[:, n % 2, half_, c0:c1], ACT.Exp,
                                         bias=mx[:, n % 2, 4 + 2 * half_ + t:5 + 2 * half_ + t],
                                         scale=1.0 if branch == FOX else 2.0 ** -(h + 1),
                                         accum_out=sums[:, branch, t, h:h + 1])
                m.then_inc(sem("att_prob"), 1)
                if n >= 1:
                    turn(n - 1)
            turn(len(STEPS) - 1)

        def v_att_mix(v):
            v.wait_ge(sem("att_prob"), len(STEPS))
            v.wait_ge(sem("att_o"), 3)
            flat = sums.rearrange("p b t h -> p (b t h)")
            link(v, V.reciprocal(flat, flat))
            gates = gate48.rearrange("p (t h b) -> p t h b", t=TILES, b=3)
            for b in (SEL, WIN):
                m = V.tensor_tensor(sums[:, b], sums[:, b], gates[:, :, :, 1 + b], ALU.mult)
            link(v, m)
            for b in range(3):
                o = o_att[:, b].rearrange("p t (h d) -> p t h d", d=HD)
                dst = mix[:, :, 512:1024].rearrange("p t (h d) -> p t h d", d=HD) if b == FOX else o
                m = V.tensor_tensor(dst, o, sums[:, b, :, :, None].to_broadcast((P, TILES, HEADS, HD)), ALU.mult)
            link(v, m)
            for b in (SEL, WIN):
                link(v, V.tensor_tensor(mix[:, :, 0:512], mix[:, :, 0:512], o_att[:, b], ALU.add))
            v.sem_inc(sem("att_mix"), 1)
            v.wait_ge(*flag("att_rms"))
            link(v, V.reciprocal(att4b, att4))
            g = row(v, "gn")
            for t in range(TILES):
                for q in range(2):
                    part = mix[:, t, 512 * q:512 * q + 512]
                    m = V.scalar_tensor_tensor(out=part, in0=part, scalar=att4b[:, 2 * t + q:2 * t + q + 1],
                                               in1=g[:, 512 * q:512 * q + 512], op0=ALU.mult, op1=ALU.mult)
                m.then_inc(sem("att_y"), 1)
            v.wait_ge(sem("att_y"), TILES)
            v.sem_inc(sem("row_used"), 1)

        def a_att_mix(a):
            a.wait_ge(sem("att_mix"), 1)
            for t in range(TILES):
                for q in range(2):
                    m = A.activation(o_att[:, q, t, :], mix[:, t, 512 * q:512 * q + 512], ACT.Square,
                                     accum_out=att4[:, 2 * t + q:2 * t + q + 1])
            link(a, m, "a")
            A.activation(att4, att4, ACT.Sqrt, bias=eps(EPS6), scale=1.0 / 512).then_inc(flag_up("att_rms"), 1)

        def v_add_product(v, tag, done, pairs):
            for t in range(TILES):
                v.wait_ge(sem(done), t + 1)
                V.tensor_tensor(x[:, t, :], x[:, t, :], ps[:, pairs[t], :], ALU.add).then_inc(sem(f"{tag}_x"), 1)
            v.wait_ge(sem(f"{tag}_x"), TILES)

        R = side[:, 1, :]
        logit = view(R[:, 0:64], (TILES, EXPERTS))
        chosen = view(R[:, 64:128], (TILES, EXPERTS))
        weight = view(R[:, 128:192], (TILES, EXPERTS))
        rank = view(R[:, 192:256], (TILES, EXPERTS))
        top8 = view(R[:, 256:272], (TILES, 8))
        neg_top = R[:, 272:274]
        wsum = R[:, 274:276]
        count_f = R[:, 276:277]
        b_down_sb = arena[0:EXPERTS, 7168:8192]
        ple2 = xT[:].rearrange("p k t -> p (k t)")
        weightT = side[0:EXPERTS, 0, 0:SEQ]
        count_i = sb("count_i", [P, 2], I32)

        def pe_router(pe):
            w = view(param("w_router"), (KT, EXPERTS))
            pe.wait_ge(sem("T"), before(TURNS, "rn2") + 2)
            for t in range(TILES):
                for k in range(KT):
                    m = T.matmul(ps[:, 2, EXPERTS * t:EXPERTS * (t + 1)], xT[:, k, t * P:(t + 1) * P], w[:, k, :],
                                 start=(k == 0), stop=(k == KT - 1))
            m.then_inc(flag_up("router_psum"), 1)
            pe.wait_ge(*flag("router_chosen"))
            strict = table("strict")
            T.matmul(ps[:, 2, 512:544], strict, chosen[:, 0, :], start=True, stop=True)
            T.matmul(ps[:, 2, 544:576], ones, chosen[:, 0, :], start=True, stop=False)
            T.matmul(ps[:, 2, 544:576], strict, chosen[:, 1, :], start=False, stop=True)
            T.matmul(ps[:, 2, 576:608], ones, chosen[:, 0, :], start=True, stop=False)
            T.matmul(ps[:, 2, 576:608], ones, chosen[:, 1, :], start=False, stop=True).then_inc(flag_up("router_rank_psum"), 1)
            pe.wait_ge(*flag("router_weight"))
            for t in range(TILES):
                m = T.transpose(ps[0:EXPERTS, 3, t * P:(t + 1) * P], weight[:, t, :], ident)
            m.then_inc(flag_up("router_wT_psum"), 1)
            pe.wait_ge(*flag("router_wT"))
            pe.wait_ge(sem("b_down_loaded"), 16)
            for t in range(TILES):
                for half_ in range(2):
                    m = T.matmul(pair01[:, t * D + half_ * 512:t * D + half_ * 512 + 512], weightT[:, t * P:(t + 1) * P],
                                 b_down_sb[:, half_ * 512:half_ * 512 + 512], start=True, stop=True)
            m.then_inc(flag_up("router_bias_psum"), 1)

        def v_router(v):
            v.wait_ge(*flag("router_psum"))
            for t in range(TILES):
                m = V.tensor_tensor(logit[:, t, :], ps[:, 2, EXPERTS * t:EXPERTS * (t + 1)], param("b_router"), ALU.add)
            link(v, m)
            for t in range(TILES):
                m = V.max(top8[:, t, :], logit[:, t, :])
            link(v, m)
            V.tensor_scalar(neg_top, top8[:, :, 0], -1.0, None, ALU.mult).then_inc(flag_up("router_top"), 1)
            v.wait_ge(*flag("router_top"))
            link(v, V.memset(top8[:, :, TOP_K:8], 3e38))
            for t in range(TILES):
                m = V.match_replace(chosen[:, t, :], top8[:, t, :], logit[:, t, :], -3e38)
            link(v, m)
            V.tensor_tensor(chosen, chosen, logit, ALU.not_equal).then_inc(flag_up("router_chosen"), 1)
            v.wait_ge(*flag("router_chosen"))
            v.wait_ge(sem("router_exp"), TILES)
            link(v, V.tensor_tensor(weight, weight, chosen, ALU.mult))
            link(v, V.tensor_reduce(wsum, weight, AX.X, ALU.add))
            link(v, V.reciprocal(wsum, wsum))
            V.tensor_tensor(weight, weight, spread(wsum, EXPERTS), ALU.mult).then_inc(flag_up("router_weight"), 1)
            v.wait_ge(*flag("router_rank_psum"))
            link(v, V.scalar_tensor_tensor(out=rank, in0=view(ps[:, 2, 512:576], (TILES, EXPERTS)), scalar=1.0, in1=chosen,
                                           op0=ALU.add, op1=ALU.mult))
            V.tensor_scalar(rank, rank, -1.0, None, ALU.add).then_inc(flag_up("router_rank"), 1)
            link(v, V.tensor_reduce(count_f, ps[:, 2, 576:608], AX.X, ALU.max))
            V.tensor_copy(count_i[:, 0:1], count_f).then_inc(flag_up("router_count"), 1)
            v.wait_ge(*flag("router_wT_psum"))
            V.tensor_copy(weightT, ps[0:EXPERTS, 3, 0:SEQ]).then_inc(flag_up("router_wT"), 1)
            v.wait_ge(*flag("router_rank"))
            v.wait_ge(*flag("router_bias_psum"))
            V.tensor_tensor(x[:], x[:], ps[:, 0:2, :], ALU.add).then_inc(flag_up("router_x"), 1)
            v.wait_ge(*flag("router_x"))

        def a_router(a):
            a.wait_ge(*flag("router_top"))
            for t in range(TILES):
                A.activation(weight[:, t, :], logit[:, t, :], ACT.Exp, bias=neg_top[:, t:t + 1]).then_inc(sem("router_exp"), 1)

        def pe_ple2(pe):
            pe.wait_ge(*flag("router_rank"))
            pe.wait_ge(*flag("router_count"))
            pe.wait_ge(*flag("router_wT"))
            take(pe, 5)
            for t in range(TILES):
                for half_ in range(2):
                    for k in range(2):
                        at = k * D + half_ * 512
                        m = T.matmul(ps[:, 2 + t, half_ * 512:half_ * 512 + 512], pleT[:, 2, k, t * P:(t + 1) * P],
                                     ring[:, 5, at:at + 512], start=(k == 0), stop=(k == 1))
            m.then_inc(flag_up("ple2_psum"), 1)

        def v_ple2(v):
            v.wait_ge(*flag("ple2_psum"))
            V.tensor_copy(ple2, pair23).then_inc(flag_up("ple2_copied"), 1)

        up_bias = scratch(0, 2, 2, STEP)
        xs_high, xs_low = split_scratch(2048, KT, P), split_scratch(3072, KT, P)
        e_up, e_act = scratch(4096, 2, 2, STEP), scratch(6144, 2, STEP)
        actT_high, actT_low = split_scratch(7168, 2, 4, P), split_scratch(8192, 2, 4, P)
        onehotT = split_scratch(9472, TILES, P)
        y_high, y_low = row_split[:, 2, :], side_split[:, 0, :]
        onehot = view(R[:, 512:768], (TILES, P))
        onehot_add = view(R[:, 768:1024], (TILES, P))
        bias_rows = expert_b.rearrange("e (m j f) -> e j m f", m=2, j=2)

        CHUNKS, BUFFERS = 24, 6
        HALVES, HALF_SLOTS = 12, 6
        CHUNK, HALF = UNIT // 4, UNIT // 2
        USES = 8 * (EXPERTS - 1) - 2 + 6 + 4
        ring_flat = ring[:].rearrange("p s n -> p (s n)")

        def split_buffer(c):
            at = HALF_SLOTS * HALF + (c % BUFFERS) * 2 * CHUNK
            flat = ring_split[:].rearrange("p s n -> p (s n)")
            return flat[:, at:at + CHUNK], flat[:, at + CHUNK:at + 2 * CHUNK]

        def raw_chunk(c):
            at = (c // 2) % HALF_SLOTS * HALF + (c % 2) * CHUNK
            return ring_flat[:, at:at + CHUNK]

        def uses_before(e):
            return 8 * e - 2

        def sp_expert(sp, n, e, first=False):
            for h in range(HALVES):
                slot = h % HALF_SLOTS
                if not first or h >= HALF_SLOTS:
                    sp.wait_ge(sem(f"moe{n}_low"), CHUNKS * e + 2 * (h + 1 - HALF_SLOTS))
                elif n == 1:
                    sp.wait_ge(sem("moe0_low"), CHUNKS * EXPERTS)
                elif h < 4:
                    sp.wait_ge(sem("att_y"), TILES)
                else:
                    sp.wait_ge(sem("att_out_psum"), TILES)
                sp.dma_start(ring_flat[:, slot * HALF:(slot + 1) * HALF], experts[e, h // 2, :, (h % 2) * HALF:(h % 2 + 1) * HALF])\
                  .then_inc(sem(f"moe{n}_full{slot}"), 16)
                if h in (3, 7):
                    j = h // 4
                    if not first:
                        sp.wait_ge(sem(f"moe{n}_biased"), 2 * e + j - 1)
                    elif n == 1:
                        sp.wait_ge(sem("moe0_biased"), 2 * EXPERTS)
                    sp.dma_start(up_bias[:, j], bias_rows[e, j].partition_broadcast(P))\
                      .then_inc(sem(f"moe{n}_bias{j}"), 16)

        def sp_experts(sp, n):
            sp_expert(sp, n, 0, first=True)
            with sp.Fori(1, EXPERTS) as e:
                sp_expert(sp, n, e)

        def pe_experts(pe, n):
            s = lambda k: sem(f"moe{n}_{k}")

            def bank(u, base=0):
                pe.wait_ge(s("emptied"), base + u - 1)
                return ps[:, 3, 512 * (u % 2):512 * (u % 2) + 512]

            def chunk(e, c, out_, high, low, k0, start, stop):
                pe.wait_ge(s("low"), CHUNKS * e + c + 1)
                w_high, w_low = split_buffer(c)
                for k in range(2):
                    wh, wl = w_high[:, k * STEP:(k + 1) * STEP], w_low[:, k * STEP:(k + 1) * STEP]
                    T.matmul(out_, high[:, k0 + k, :], wh, start=(start and k == 0), stop=False, skip_group_check=True)
                    T.matmul(out_, high[:, k0 + k, :], wl, start=False, stop=False, skip_group_check=True)
                    ins = T.matmul(out_, low[:, k0 + k, :], wh, start=False, stop=(stop and k == 1), skip_group_check=True)
                ins.then_inc(s("product"), 1)

            def up(e, j, m, first=False):
                if m == 0:
                    if j == 0:
                        pe.wait_ge(s("emptied"), 2 if first else uses_before(e))
                    if not first:
                        if j == 0:
                            pe.wait_ge(s("wT"), e)
                        else:
                            pe.wait_ge(s("act"), 2 * e)
                for c in range(4):
                    chunk(e, 8 * j + 4 * m + c, ps[:, j, 512 * m:512 * m + 512], xs_high, xs_low, 2 * c, c == 0, c == 3)

            def turn(e, j, out_):
                pe.wait_ge(s("act"), 2 * e + j + 1)
                for k in range(4):
                    ins = T.transpose(out_[:, k * P:(k + 1) * P], e_act[:, j, k * P:(k + 1) * P], ident)
                ins.then_inc(s("used"), 1)

            def add(e_next, c, out_):
                if c == 0:
                    pe.wait_ge(s("y"), e_next)
                    pe.wait_ge(s("wT"), e_next)
                part = slice((c % 2) * 512, (c % 2) * 512 + 512)
                T.matmul(out_, onehotT[:, c // 2, :], y_high[:, part], start=True, stop=False)
                T.matmul(out_, onehotT[:, c // 2, :], y_low[:, part], start=False, stop=True).then_inc(s("used"), 1)

            def gather(e, c, out_):
                if c == 0:
                    pe.wait_ge(s("onehot"), e + 1)
                for k in range(4):
                    for t in range(TILES):
                        at = (4 * c + k) * P
                        ins = T.matmul(out_[:, k * P:(k + 1) * P], pre[:, t, at:at + P], onehot[:, t, :],
                                       start=(t == 0), stop=(t == 1))
                ins.then_inc(s("used"), 1)

            def turn_onehot(e):
                pe.wait_ge(s("onehot_add"), e + 1)
                for t in range(TILES):
                    ins = T.transpose(ps[:, 0, t * P:(t + 1) * P], onehot_add[:, t, :], ident)
                ins.then_inc(s("wT_psum"), 1)

            def down(e, j, turned, first=False):
                pe.wait_ge(s("emptied"), turned)
                if j == 0 and not first:
                    pe.wait_ge(s("y"), e)
                for c in range(4):
                    half_, k0 = c // 2, 2 * (c % 2)
                    chunk(e, 16 + 4 * j + c, ps[:, 2, 512 * half_:512 * half_ + 512], actT_high[:, j], actT_low[:, j], k0,
                          j == 0 and k0 == 0, j == 1 and k0 == 2)

            def expert(e, first=False, last=False):
                b = 2 if first else uses_before(e)
                u = 0 if first else 2
                up(e, 0, 0, first)
                up(e, 0, 1, first)
                if not first:
                    add(e, 0, bank(0, b))
                    add(e, 1, bank(1, b))
                up(e, 1, 0, first)
                up(e, 1, 1, first)
                turn(e, 0, bank(u, b))
                if not first:
                    add(e, 2, bank(3, b))
                    add(e, 3, bank(4, b))
                turn_onehot(e)
                down(e, 0, b + u + 1, first)
                u = 1 if first else 5
                if not last:
                    gather(e + 1, 0, bank(u, b))
                    u += 1
                turn(e, 1, bank(u, b))
                if not last:
                    gather(e + 1, 1, bank(u + 1, b))
                down(e, 1, b + u + 1)

            if n == 0:
                pe.wait_ge(*flag("ple2_copied"))
                pe.wait_ge(*flag("router_x"))
            else:
                pe.wait_ge(sem("moe0_emptied"), USES)
            gather(0, 0, ps[:, 3, 0:512])
            gather(0, 1, ps[:, 3, 512:1024])
            expert(0, first=True)
            with pe.Fori(1, EXPERTS - 1) as e:
                expert(e)
            expert(EXPERTS - 1, last=True)
            for c in range(4):
                add(EXPERTS, c, bank(6 + c, uses_before(EXPERTS - 1)))

        def v_experts(v, n):
            s = lambda k: sem(f"moe{n}_{k}")
            def bank(u, base=0):
                v.wait_ge(s("used"), base + u + 1)
                return ps[:, 3, 512 * (u % 2):512 * (u % 2) + 512]

            def low(e, *chunks):
                for c in chunks:
                    v.wait_ge(s("high"), CHUNKS * e + c + 1)
                    high, low_ = split_buffer(c)
                    V.tensor_tensor(low_, raw_chunk(c), high, ALU.subtract).then_inc(s("low"), 1)

            slot_numbers = table("slot_no" if n == 0 else "slot_no2")

            def one_hot(e):
                for t in range(TILES):
                    ins = V.tensor_scalar(onehot[:, t, :], slot_numbers, rank[:, t, bass.ds(e, 1)], None, ALU.is_equal)
                ins.then_inc(s("onehot"), 1)

            def biased(e, j):
                v.wait_ge(s("product"), CHUNKS * e + 8 * j + 8)
                v.wait_ge(s(f"bias{j}"), 16 * e + 16)
                V.tensor_tensor(e_up[:, j].rearrange("p m f -> p (m f)"), ps[:, j, :],
                                up_bias[:, j].rearrange("p m f -> p (m f)"), ALU.add).then_inc(s("biased"), 1)

            def clip(e, j):
                gate, lin = e_up[:, j, 0, :], e_up[:, j, 1, :]
                v.wait_ge(s("biased"), 2 * e + j + 1)
                V.tensor_scalar(gate, gate, LIMIT, None, ALU.min).then_inc(s("gate"), 1)
                V.tensor_scalar(lin, lin, LIMIT, -LIMIT, ALU.min, ALU.max).then_inc(s("lin"), 1)

            def keep_low(low_, src, high, kept):
                v.wait_ge(s("kept"), kept)
                V.tensor_tensor(low_, view(src, (4, P)), high, ALU.subtract).then_inc(s("emptied"), 1)

            def add(e, c, src):
                part = x[:, c // 2, (c % 2) * 512:(c % 2) * 512 + 512]
                V.scalar_tensor_tensor(out=part, in0=src, scalar=weight[:, c // 2, bass.ds(e, 1)], in1=part,
                                       op0=ALU.mult, op1=ALU.add).then_inc(s("emptied"), 1)

            def keep_onehot(e):
                v.wait_ge(s("wT_psum"), e + 1)
                V.tensor_copy(onehotT, view(ps[:, 0, 0:256], (2, P))).then_inc(s("wT"), 1)

            def results_low(e):
                v.wait_ge(s("y_high"), e + 1)
                V.tensor_tensor(y_low, ps[:, 2, :], y_high, ALU.subtract).then_inc(s("y"), 1)

            def expert(e, first=False, last=False):
                b = 2 if first else uses_before(e)
                kept = 4 * e + 2
                v.wait_ge(s("emptied"), b)
                if not first:
                    results_low(e - 1)
                low(e, 5, 6, 7, 8, 9, 10, 11)
                biased(e, 0)
                if not first:
                    add(e - 1, 0, bank(0, b))
                    add(e - 1, 1, bank(1, b))
                clip(e, 0)
                low(e, 12, 13)
                V.tensor_copy(onehot_add, onehot).then_inc(s("onehot_add"), 1)
                if not last:
                    v.wait_ge(s("onehot_add"), e + 1)
                    one_hot(e + 1)
                low(e, 14, 15, 16, 17, 18)
                biased(e, 1)
                u = 0 if first else 2
                keep_low(actT_low[:, 0], bank(u, b), actT_high[:, 0], kept + 1)
                clip(e, 1)
                if not first:
                    add(e - 1, 2, bank(3, b))
                    add(e - 1, 3, bank(4, b))
                low(e, 19, 20, 21)
                keep_onehot(e)
                low(e, 22, 23)
                u = 1 if first else 5
                if not last:
                    keep_low(xs_low[:, 0:4], bank(u, b), xs_high[:, 0:4], kept + 2)
                    low(e, 24)
                    u += 1
                keep_low(actT_low[:, 1], bank(u, b), actT_high[:, 1], kept + (2 if last else 3))
                if not last:
                    keep_low(xs_low[:, 4:8], bank(u + 1, b), xs_high[:, 4:8], kept + 4)
                    low(e, 25, 26, 27, 28)

            one_hot(0)
            keep_low(xs_low[:, 0:4], bank(0), xs_high[:, 0:4], 1)
            keep_low(xs_low[:, 4:8], bank(1), xs_high[:, 4:8], 2)
            low(0, 0, 1, 2, 3, 4)
            expert(0, first=True)
            with v.Fori(1, EXPERTS - 1) as e:
                expert(e)
            expert(EXPERTS - 1, last=True)
            results_low(EXPERTS - 1)
            v.wait_ge(s("emptied"), uses_before(EXPERTS - 1) + 6)
            for c in range(4):
                add(EXPERTS - 1, c, bank(6 + c, uses_before(EXPERTS - 1)))
            v.wait_ge(s("emptied"), USES)

        def pool_experts(pool, n):
            s = lambda k: sem(f"moe{n}_{k}")

            def act(e, j):
                gate, lin = e_up[:, j, 0, :], e_up[:, j, 1, :]
                pool.wait_ge(s("lin"), 2 * e + j + 1)
                G.tensor_tensor(view(lin, (4, P)), view(lin, (4, P)), repeat(ones, 4), ALU.add).then_inc(s("lin_plus"), 1)
                pool.wait_ge(s("lin_plus"), 2 * e + j + 1)
                pool.wait_ge(s("gate"), 2 * e + j + 1)
                G.tensor_tensor(lin, lin, gate, ALU.mult).then_inc(s("lin_gate"), 1)
                pool.wait_ge(s("lin_gate"), 2 * e + j + 1)
                pool.wait_ge(s("sigmoid"), 2 * e + j + 1)
                G.tensor_tensor(e_act[:, j, :], e_act[:, j, :], lin, ALU.mult).then_inc(s("act"), 1)

            act(0, 0)
            act(0, 1)
            with pool.Fori(1, EXPERTS) as e:
                act(e, 0)
                act(e, 1)

        def a_experts(a, n):
            s = lambda k: sem(f"moe{n}_{k}")

            def high(e, *chunks, first=False):
                for c in chunks:
                    if c % 2 == 0:
                        h = c // 2
                        a.wait_ge(s(f"full{h % HALF_SLOTS}"), 16 * (2 * e + h // HALF_SLOTS + 1))
                    if c >= BUFFERS or (c == BUFFERS - 1 and not first):
                        a.wait_ge(s("product"), CHUNKS * e + c - BUFFERS + 1)
                    A.copy(split_buffer(c)[0], raw_chunk(c)).then_inc(s("high"), 1)

            def sigmoid(e, j):
                a.wait_ge(s("gate"), 2 * e + j + 1)
                A.activation(e_act[:, j, :], e_up[:, j, 0, :], ACT.Sigmoid, scale=1.702).then_inc(s("sigmoid"), 1)

            def keep_high(dst, u, base):
                a.wait_ge(s("used"), base + u + 1)
                A.copy(dst, view(ps[:, 3, 512 * (u % 2):512 * (u % 2) + 512], (4, P))).then_inc(s("kept"), 1)

            def results_high(e, first=False):
                a.wait_ge(s("product"), CHUNKS * e + CHUNKS)
                if not first:
                    a.wait_ge(s("used"), uses_before(e) + 5)
                A.copy(y_high, ps[:, 2, :]).then_inc(s("y_high"), 1)

            def expert(e, first=False, last=False, second=False):
                b = 2 if first else uses_before(e)
                if not first:
                    results_high(e - 1, first=second)
                high(e, 5, 6, 7, 8, 9, 10, 11, 12, 13, first=first)
                sigmoid(e, 0)
                high(e, 14, 15, 16, 17, 18, 19, 20, 21)
                keep_high(actT_high[:, 0], 0 if first else 2, b)
                sigmoid(e, 1)
                high(e, 22, 23)
                u = 1 if first else 5
                if not last:
                    high(e, 24, 25)
                    keep_high(xs_high[:, 0:4], u, b)
                    u += 1
                keep_high(actT_high[:, 1], u, b)
                if not last:
                    keep_high(xs_high[:, 4:8], u + 1, b)
                    high(e, 26, 27, 28)

            if n == 0:
                a.wait_ge(*flag("ple2_psum"))
            else:
                a.wait_ge(sem("moe0_emptied"), USES)
            keep_high(xs_high[:, 0:4], 0, 0)
            keep_high(xs_high[:, 4:8], 1, 0)
            high(0, 0, 1, 2, 3, 4)
            expert(0, first=True)
            expert(1, second=True)
            with a.Fori(2, EXPERTS - 1) as e:
                expert(e)
            expert(EXPERTS - 1, last=True)
            results_high(EXPERTS - 1)

        def second_pass(eng, program):
            eng.wait_ge(*flag("router_count"))
            most = eng.value_load(count_i[0:1, 0:1])
            with eng.If(most > P):
                program(eng, 1)

        def v_final(v):
            b = TILES * 2
            v_rms_norm(v, "rnp", "ln_ple")
            v_transpose(v, "rnp")
            for t in range(TILES):
                v.wait_ge(sem("ple_gate"), b + t + 1)
                link(v, V.tensor_tensor(side[:, t, :], side[:, t, :], pre[:, t, :], ALU.mult))
                V.tensor_tensor(x[:, t, :], x[:, t, :], side[:, t, :], ALU.add).then_inc(sem("last_x"), 1)
            v_rms_norm(v, "rnf", "ln_f")

        def a_final(a):
            a.wait_ge(*flag("moe_end"))
            A.copy(side[:], ple2.rearrange("p (t c) -> p t c", t=TILES)).then_inc(flag_up("ple2_side"), 1)
            a_rms_norm(a, "rnp", None, 0)
            a.wait_ge(*flag("ple2_side"))
            a_transpose(a, "rnp")
            for t in range(TILES):
                a.wait_ge(sem("ple_gate_psum"), TILES * 2 + t + 1)
                A.activation(pre[:, t, :], ps[:, 2 + t, :], ACT.Sigmoid).then_inc(sem("ple_gate"), 1)
            a_rms_norm(a, "rnf", "last_x", 0)
            for t in range(TILES):
                a.wait_ge(sem("norm_x"), before(NORMS, "rnf") + t + 1)
                a.dma_start(out[:, t, :], pre[:, t, :]).then_inc(sem("out_stored"), 16)
            a.wait_ge(sem("out_stored"), 16 * TILES)

        block = ctx.enter_context(nc.Block())

        @block.sync
        def _(sp):
            sp_constants(sp)
            fill(sp, "mlp0_up0", 0)
            fill(sp, "mlp0_down0", 1)
            fill(sp, "mlp0_up1", 2)
            fill(sp, "mlp0_down1", 3, "ple_gate_psum", 2)
            fill(sp, "gdn_in0", 4, "ple_proj_psum", 2)
            fill(sp, "gdn_in1", 5, "ple_gate_psum", 2)
            sp_mlp(sp, 0)
            for n in range(2, 6):
                fill(sp, f"gdn_in{n}", n - 2, "mlp_down", MLP_STEPS)
            for n in range(6, 8):
                fill(sp, f"gdn_in{n}", n - 2, "gdn_in_psum", n - 5)
            fill(sp, "gdn_out0", 4, "gdn_z_psum", 1)
            fill(sp, "gdn_out1", 5, "gdn_z_psum", 2)
            fill(sp, "mlp1_up0", 0, "gdn_y", 2)
            fill(sp, "mlp1_down0", 1)
            fill(sp, "mlp1_up1", 2)
            fill(sp, "gate10", 4, "gdn_out_psum", 2)
            fill(sp, "gate11", 5)
            fill(sp, "proj1", 3, width=2048)
            fill(sp, "mlp1_down1", 3, "ple_proj_psum", 4)
            fill(sp, "att_in0", 4, "ple_gate_psum", 4)
            fill(sp, "att_in1", 5)
            sp_mlp(sp, 1)
            for n in range(2, 6):
                fill(sp, f"att_in{n}", n - 2, "mlp_down", 2 * MLP_STEPS)
            fill(sp, "cmp", 4, "att_qn_psum", 1)
            fill(sp, "att_out0", 2, "att_kf_psum", 1)
            fill(sp, "att_out1", 3, "att_vf_psum", 1)
            fill(sp, "ple2", 5, "att_in1_read", 1, width=2048)
            sp.wait_ge(sem("att_y"), TILES)
            sp.dma_start(b_down_sb, b_down).then_inc(sem("b_down_loaded"), 16)
            sp_experts(sp, 0)
            second_pass(sp, sp_experts)
            sp.wait_ge(*flag("moe_end"))
            fill(sp, "gate20", 0)
            fill(sp, "gate21", 1)

        @block.gpsimd
        def _(pool):
            pool_rows(pool, 0, len(places["row"]))
            pool_experts(pool, 0)
            second_pass(pool, pool_experts)

        @block.tensor
        def _(pe):
            pe.wait_ge(sem("tables_loaded"), 16)
            pe_pool(pe)
            pe_transpose(pe, "ln00", x, "norm_x", before(NORMS, "ln00"))
            pe.wait_ge(sem("ple_loaded"), 16)
            pe_ple(pe, "ln00", 0, (5, 3), 4, 2048, proj_taken=True)
            pe_mlp(pe, 0)
            pe_transpose(pe, "ln01", x, "norm_x", before(NORMS, "ln01"))
            pe_gdn_in(pe)
            pe_gdn_sums(pe)
            pe_gdn_scores(pe)
            pe_gdn_inverse(pe)
            pe_gdn_out(pe)
            pe_transpose(pe, "gdny", pre, "gdn_y")
            pe.wait_ge(sem("T"), before(TURNS, "gdny") + 2)
            pe_dense(pe, "gdn_out_psum", (2, 3), (4, 5))
            pe_transpose(pe, "ln10", x, "norm_x", before(NORMS, "ln10"))
            pe_ple(pe, "ln10", 1, (4, 5), 3, 0)
            pe_mlp(pe, 1)
            pe_transpose(pe, "rn1", pre, "norm_x", before(NORMS, "rn1"))
            pe_att_in(pe)
            pe_fox_bias(pe)
            pe_compress(pe)
            pe_attention(pe)
            pe_transpose(pe, "att", mix, "att_y")
            pe.wait_ge(sem("T"), before(TURNS, "att") + 2)
            pe_dense(pe, "att_out_psum", (2, 3), (2, 3))
            pe_transpose(pe, "rn2", pre, "norm_x", before(NORMS, "rn2"))
            pe_router(pe)
            pe_ple2(pe)
            pe_experts(pe, 0)
            second_pass(pe, pe_experts)
            pe_transpose(pe, "rnp", pre, "norm_x", before(NORMS, "rnp"))
            pe.wait_ge(sem("T"), before(TURNS, "rnp") + 2)
            pe_dense(pe, "ple_gate_psum", (2, 3), (0, 1))

        @block.vector
        def _(v):
            v.wait_ge(sem("pool_T_psum"), 1)
            V.tensor_copy(xT[:, 0:4, :], view(ps[:, 0, :], (4, SEQ))).then_inc(sem("pool_T"), 1)
            v_pool(v)
            v_layer_norm(v, "ln00", pre, "gain00", "bias00")
            v_transpose(v, "ln00")
            v_ple(v, 0)
            v_mlp(v, 0)
            v_layer_norm(v, "ln01", pre, "gain01", "bias01")
            v_transpose(v, "ln01")
            v_gdn_in(v)
            v_gdn_scores(v)
            v_gdn_inverse(v)
            v_gdn_out(v)
            v_transpose(v, "gdny")
            v_residual(v, "gdn_out_psum", (2, 3), ALPHA)
            v_layer_norm(v, "ln10", pre, "gain10", "bias10")
            v_transpose(v, "ln10")
            v_ple(v, 1)
            v_mlp(v, 1)
            v_layer_norm(v, "ln11", pre, "gain11", "bias11")
            v_rms_norm(v, "rn1", "ln1")
            v_transpose(v, "rn1")
            v_att_in(v)
            v_fox_bias(v)
            v_compress(v)
            v_attention(v)
            v_att_mix(v)
            v_transpose(v, "att")
            v_add_product(v, "att_out", "att_out_psum", (2, 3))
            v_rms_norm(v, "rn2", "ln2")
            v_transpose(v, "rn2")
            v_router(v)
            v_ple2(v)
            v_experts(v, 0)
            second_pass(v, v_experts)
            v.sem_inc(flag_up("moe_end"), 1)
            v_final(v)

        @block.scalar
        def _(a):
            a.wait_ge(sem("tables_loaded"), 16)
            a.wait_ge(sem("pool_T_psum"), 2)
            A.copy(xT[:, 4:8, :], view(ps[:, 1, :], (4, SEQ))).then_inc(sem("pool_T"), 1)
            a_layer_norm(a, "ln00")
            a_transpose(a, "ln00")
            a_ple(a, 0)
            a_mlp(a, 0)
            a_layer_norm(a, "ln01")
            a_transpose(a, "ln01")
            a_gdn_in(a)
            a_gdn_scores(a)
            a_gdn_inverse(a)
            a_gdn_out(a)
            a_transpose(a, "gdny")
            a_layer_norm(a, "ln10")
            a_transpose(a, "ln10")
            a_ple(a, 1)
            a_mlp(a, 1)
            a_layer_norm(a, "ln11")
            a_rms_norm(a, "rn1", "norm_x", before(NORMS, "ln11"))
            a_transpose(a, "rn1")
            a_att_in(a)
            a_compress(a)
            a_attention(a)
            a_att_mix(a)
            a_transpose(a, "att")
            a_rms_norm(a, "rn2", "att_out_x", 0)
            a_transpose(a, "rn2")
            a_router(a)
            a_experts(a, 0)
            second_pass(a, a_experts)
            a_final(a)


def kernel(**inputs):
    import concourse.bacc as bacc
    from concourse.bass_utils import run_bass_kernel_spmd

    arrays, places = lay_out(inputs)
    nc = bacc.Bacc("TRN2", target_bir_lowering=False, num_devices=1)
    args = {n: nc.dram_tensor(f"{n}_dram", a.shape, F32, kind="ExternalInput").ap() for n, a in arrays.items()}
    out = nc.dram_tensor("out_dram", (P, TILES, D), F32, kind="ExternalOutput").ap()
    build(nc, places, out=out, **args)
    r = run_bass_kernel_spmd(nc, [{f"{n}_dram": a for n, a in arrays.items()}], core_ids=[0])
    return r.results[0]["out_dram"].transpose(1, 0, 2).reshape(1, SEQ, D)
```

```python
from contextlib import ExitStack

import numpy as np

import concourse.bass as bass
from concourse import mybir

F32 = mybir.dt.float32
F32R = mybir.dt.float32r
I32 = mybir.dt.int32
ALU = mybir.AluOpType
ACT = mybir.ActivationFunctionType
AX = mybir.AxisListType

P = 128
SEQ = 256
TILES = SEQ // P
D = 1024
KT = D // P
HEADS = 8
DFF = 4096
STEP = 512
MLP_STEPS = DFF // STEP
UNIT = 4096
SLOTS = 6
ALPHA = 4.0 ** 0.25
WINDOWS = (2, 4, 8, 16)
NCMP = (SEQ - 32) // 16 + 1
EXPERTS = 32
TOP_K = 4
BIG = 1e30
LIMIT = 7.0

FLAGS = {
    "tensor": (
        "gdn_ba_psum", "gdn_rows_psum", "gdn_KK_psum", "gdn_QK_psum", "gdn_k_psum", "gdn_v_psum",
        "gdn_u0_psum", "gdn_wT_psum", "gdn_state_psum", "gdn_o0_psum", "gdn_vnew_psum", "gdn_os_psum",
        "gdn_o1_psum", "att_kv_psum", "att_nat_psum", "att_qf_psum", "fox_cum_psum", "fox_rows_psum",
        "cmp_hid_psum", "cmp_kv_psum", "cmp_score_psum", "cmp_pT_psum", "cmp_o_psum", "router_psum",
        "router_rank_psum", "router_wT_psum", "router_bias_psum", "ple2_psum",
    ),
    "vector": (
        "gdn_ba", "gdn_g_in", "gdn_g", "gdn_diff", "gdn_DB", "gdn_LT", "gdn_QKT", "gdn_k_ready",
        "gdn_v_ready", "gdn_wT", "att_kv", "att_nat", "cmp_in", "fox_f", "att_kf", "fox_lf",
        "fox_bias", "cmp_clear", "cmp_hv4", "cmp_kcc", "cmp_vblk", "cmp_diff", "cmp_prob", "cmp_pT", "cmp_o",
        "router_top", "router_chosen", "router_weight", "router_rank", "router_count", "router_wT",
        "router_x", "moe_end",
    ),
    "scalar": (
        "gdn_beta", "gdn_log", "gdn_exp_gc", "gdn_z", "gdn_exp", "gdn_u0", "gdn_state", "gdn_vnew",
        "att_qn", "att_gates", "fox_log", "att_qf", "att_vf", "cmp_exp", "att_rms",
        "ple2_side",
    ),
}


def shape_tables():
    p = np.arange(P)[:, None]
    c = np.arange(P)[None, :]
    t = {}
    t["ident"] = (p == c)
    t["upto"] = (p <= c)
    t["ones"] = np.ones((P, P))
    t["strict"] = (p < c)
    for level in range(7):
        b = 1 << level
        t[f"level{level}"] = (c // (2 * b) == p // (2 * b)) & ((c // b) % 2 == 1) & ((p // b) % 2 == 0)
    sel = np.zeros((P, HEADS, P))
    for h in range(HEADS):
        sel[h, h] = 1
    t["pick_head"] = sel.reshape(P, -1)
    t["head_col"] = np.tile(np.eye(HEADS).reshape(1, -1), (P, 1))
    dist = np.concatenate([p - c, p + P - np.arange(SEQ)[None, :]], 1).astype(np.float64)
    t["neg_dist"] = np.where(dist >= 0, -dist, -1e32)
    t["mask_neg"] = np.where(dist >= 0, 0.0, -BIG)
    j = np.arange(16)[None, :]
    d = np.concatenate([p - (16 * j + 31), p + P - (16 * j + 31)], 1).astype(np.float64)
    ok = (d >= 0) & (np.tile(j, (1, 2)) < NCMP)
    slopes = 2.0 ** -(np.arange(HEADS) + 1.0)
    bias = np.where(ok, -d, 0.0).reshape(P, 1, 2, 1, 16) * slopes.reshape(1, 2, 1, 4, 1)
    valid = np.broadcast_to(ok.reshape(P, 1, 2, 1, 16), bias.shape)
    t["cmp_bias"] = np.where(valid, bias, -BIG).reshape(P, -1)
    t["cmp_mask"] = valid.reshape(P, -1)
    t["slopes"] = np.broadcast_to(slopes.reshape(2, 4).T.reshape(1, 4, 2, 1), (P, 4, 2, 2)).reshape(P, -1)
    t["own_row"] = (p // 32 == np.arange(4)[None, :])
    t["slot_no"] = np.broadcast_to(np.arange(P)[None, :], (P, P))
    t["slot_no2"] = t["slot_no"] + P
    t["eps"] = np.broadcast_to(np.array([1e-5, 1e-6, 128e-6, 1.0, 4.0])[None, :], (P, 5))
    return {k: np.asarray(v, np.float32) for k, v in t.items()}


def band_tables():
    s = np.arange(SEQ)[:, None]
    t = np.arange(SEQ)[None, :]
    bands = []
    for w in WINDOWS:
        mean = ((s <= t) & (s > t - w)) / np.minimum(t + 1.0, w)
        bands.append(mean - (s == t))
    b = np.stack(bands, 1).astype(np.float32)
    return np.concatenate([b[:P].reshape(P, -1), b[P:, :, P:].reshape(P, -1)], 1)


def column_layout(parts):
    at, where = 0, {}
    for name, a in parts.items():
        where[name] = (at, a.shape[1])
        at += a.shape[1]
    return where, at


def unit(w, k0, kn, c0, cn):
    return w[k0 * P:(k0 + kn) * P, c0:c0 + cn].reshape(kn, P, cn).transpose(1, 0, 2).reshape(P, kn * cn)


def unit_halves(w, k0):
    return w[k0 * P:(k0 + 4) * P].reshape(4, P, 2, STEP).transpose(1, 2, 0, 3).reshape(P, UNIT)


def padded(a, n):
    return np.concatenate([a, np.zeros((a.shape[0], n - a.shape[1]), a.dtype)], 1)


def weight_units(i):
    u = {}
    pool = np.concatenate([unit(i["pool_w"][0, g], 0, 2, 0, 256) for g in range(4)], 1)
    u["pool_proj0"] = np.concatenate([pool, unit(i["ple_proj"][0], 0, 2, 0, D)], 1)
    for l in range(2):
        for h in range(2):
            u[f"gate{l}{h}"] = unit(i["ple_gate_w"][l], 4 * h, 4, 0, D)
        for s in range(MLP_STEPS):
            u[f"mlp{l}_up{s}"] = unit(i["mlp_w1"][l], 0, KT, s * STEP, STEP)
            u[f"mlp{l}_down{s}"] = unit_halves(i["mlp_w2"][l], 4 * s)
    for n in range(8):
        u[f"gdn_in{n}"] = unit(i["gdn_w_in"][0], 0, KT, n * STEP, STEP)
    for h in range(2):
        u[f"gdn_out{h}"] = unit(i["gdn_w_out"][0], 4 * h, 4, 0, D)
    u["proj1"] = padded(unit(i["ple_proj"][1], 0, 2, 0, D), UNIT)
    w = i["w_in_2"][0]
    w = np.concatenate([w[:, 0:512].reshape(D, 2, 4, 64).transpose(0, 2, 1, 3).reshape(D, 512),
                        w[:, 512:768].reshape(D, 2, 2, 64).transpose(0, 2, 1, 3).reshape(D, 256), w[:, 768:]], 1)
    for n, (c0, cn) in enumerate(ATT_COLS):
        u[f"att_in{n}"] = padded(unit(w, 0, KT, c0, cn), UNIT)
    cmp = [i[k][0].reshape(32, 64, 128).transpose(1, 0, 2).reshape(64, UNIT) for k in ("w_cmp1_k_2", "w_cmp1_v_2")]
    u["cmp"] = np.concatenate(cmp, 0)
    for h in range(2):
        u[f"att_out{h}"] = unit(i["w_out_2"][0], 4 * h, 4, 0, D)
    u["ple2"] = padded(unit(i["w_ple_2"][0], 0, 2, 0, D), UNIT)
    for h in range(2):
        u[f"gate2{h}"] = unit(i["w_ple_gate_2"][0], 4 * h, 4, 0, D)
    return u


ATT_COLS = ((0, 512), (512, 512), (1024, 280), (1304, 512), (1816, 512), (2328, 512))


def row_vectors(i):
    r = {"pool_b": i["pool_b"][0].reshape(-1), "pool_scale": i["pool_scale"][0]}
    for l in range(2):
        r[f"gain{l}0"] = i["ln_gain"][l, 0]
        if l > 0:
            r[f"bias{l}0"], r[f"gate_b{l}"] = i["ln_bias"][l, 0], i["ple_gate_b"][l]
        r[f"gain{l}1"], r[f"bias{l}1"] = i["ln_gain"][l, 1], i["ln_bias"][l, 1]
    r["ln1"] = i["ln1_2"][0]
    r["gn"] = np.concatenate([i["gn_nsa_2"][0], i["gn_fox_2"][0]])
    r["ln2"] = i["ln2_2"][0]
    r["ln_ple"] = i["ln_ple_2"][0]
    r["ln_f"] = i["ln_f_2"]
    r["bias00"], r["gate_b0"] = i["ln_bias"][0, 0], i["ple_gate_b"][0]
    return r


def small_params(i):
    s = {}

    def every(a):
        return np.broadcast_to(a.reshape(1, -1), (P, a.size))

    s["conv"] = i["gdn_conv"][0].reshape(4, 24, P).transpose(2, 1, 0).reshape(P, 96)
    s["a_log"] = every(i["gdn_a_log"])
    s["dt_bias"] = every(i["gdn_dt_bias"])
    s["norm_w"] = every(i["gdn_norm_w"])
    s["w_ba"] = unit(i["gdn_w_in"][0], 0, KT, 4096, 16)
    s["b_fg"] = every(i["b_fg_2"])
    s["w_fg"] = unit(i["w_in_2"][0], 0, KT, 2840, 8)
    s["w_router"] = unit(i["w_router_2"][0], 0, KT, 0, EXPERTS)
    s["b_router"] = every(i["b_router_2"])
    s["pe"] = np.concatenate([i["pe_cmp_k_2"][0].T, i["pe_cmp_v_2"][0].T], 0)
    s["cmp2_k"] = i["w_cmp2_k_2"][0]
    s["cmp2_v"] = i["w_cmp2_v_2"][0]
    return s


def lay_out(inputs):
    i = {k: np.asarray(v) for k, v in inputs.items()}
    units = weight_units(i)
    rows = row_vectors(i)
    tables, small = shape_tables(), small_params(i)
    table_at, table_n = column_layout(tables)
    small_at, small_n = column_layout(small)
    up = i["w_up_2"][0].reshape(EXPERTS, KT, P, 2, 2, STEP)
    up = up.transpose(0, 4, 3, 2, 1, 5).reshape(EXPERTS, 4, P, UNIT)
    down = i["w_down_2"][0].reshape(EXPERTS, 2, 4, P, 2, STEP)
    down = down.transpose(0, 1, 3, 4, 2, 5).reshape(EXPERTS, 2, P, UNIT)
    p_all = np.concatenate([i["p"][:, 0], i["p_2"][:, 0]], 0)
    arrays = {
        "tokens": i["x"][0].reshape(TILES, P, D).transpose(1, 0, 2),
        "weights": np.stack(list(units.values()), 0),
        "experts": np.concatenate([up, down], 1),
        "rows": np.stack(list(rows.values()), 0),
        "expert_b": i["b_up_2"][0],
        "b_down": i["b_down_2"][0],
        "ple_in": p_all.transpose(0, 2, 1).reshape(3, 2, P, SEQ).transpose(2, 0, 1, 3),
        "small": np.concatenate(list(small.values()), 1),
        "tables": np.concatenate(list(tables.values()), 1),
        "bands": band_tables(),
    }
    places = {"unit": {n: k for k, n in enumerate(units)}, "row": {n: k for k, n in enumerate(rows)},
              "table": table_at, "small": small_at}
    return {k: np.ascontiguousarray(v) for k, v in arrays.items()}, places


def build(nc, places, tokens, weights, experts, rows, expert_b, b_down, ple_in, small, tables, bands, out):
    with ExitStack() as ctx:
        def sb(name, shape, dt=F32):
            return ctx.enter_context(nc.sbuf_tensor(name, shape, dt))

        sems = {}

        def sem(name):
            if name not in sems:
                sems[name] = ctx.enter_context(nc.semaphore(name))
            return sems[name]

        def shared(name, shape):
            with nc.sbuf_tensor(name, shape, F32) as plain:
                pass
            return plain, sb(name + "_split", shape, F32R)

        ring, ring_split = shared("ring", [P, SLOTS, UNIT])
        x = sb("x", [P, TILES, D])
        xT = sb("xT", [P, KT, SEQ])
        pre = sb("pre", [P, TILES, D])
        side, side_split = shared("side", [P, TILES, D])
        row_buf, row_split = shared("row_buf", [P, 3, D])
        tab = sb("tab", [P, tables.shape[1]])
        par = sb("par", [P, small.shape[1]])
        pleT = sb("pleT", [P, 3, 2, SEQ])
        stats = sb("stats", [P, TILES, 2, 6])
        mv = sb("mv", [P, TILES, 2])
        std = sb("std", [P, TILES])
        rstd = sb("rstd", [P, TILES])
        arena, arena_split = shared("arena", [P, 9728])
        ps = ctx.enter_context(nc.psum_tensor("ps", [P, 4, 1024], F32))

        def table(name):
            at, n = places["table"][name]
            return tab[:, at:at + n]

        def param(name):
            at, n = places["small"][name]
            return par[:, at:at + n]

        ident, ones, upto = table("ident"), table("ones"), table("upto")

        def eps(k):
            return table("eps")[:, k:k + 1]

        EPS5, EPS6, EPS6_128, ONE = 0, 1, 2, 3

        def scratch(at, *shape):
            n = int(np.prod(shape))
            return view(arena[:, at:at + n], shape)

        def split_scratch(at, *shape):
            n = int(np.prod(shape))
            return view(arena_split[:, at:at + n], shape)

        def view(flat, shape):
            if len(shape) == 1:
                return flat
            names = "abcd"[:len(shape)]
            return flat.rearrange(f"p ({' '.join(names)}) -> p {' '.join(names)}", **{n: s for n, s in zip(names, shape)})

        def spread(ap, n):
            return ap[:, :, None].to_broadcast((*ap.shape, n))

        def repeat(ap, n):
            return ap[:, None, :].to_broadcast((ap.shape[0], n, ap.shape[1]))

        CHUNK, HALF = UNIT // 4, UNIT // 2

        unit_full = [sem(f"unit_full{s}") for s in range(SLOTS)]
        taken = [0] * SLOTS

        def fill(sp, name, slot, after=None, count=0, width=UNIT):
            if after is not None:
                sp.wait_ge(sem(after), count)
            sp.dma_start(ring[:, slot, 0:width], weights[places["unit"][name], :, 0:width]).then_inc(unit_full[slot], 16)

        def take(pe, slot):
            taken[slot] += 1
            pe.wait_ge(unit_full[slot], 16 * taken[slot])
            return ring[:, slot, :]

        row_full = [sem(f"row_full{s}") for s in range(3)]
        rows_taken = [0]

        EARLY = {"bias00": 4096, "gate_b0": 5120}

        def row(dve, name):
            if name in EARLY:
                dve.wait_ge(sem(f"{name}_loaded"), 16)
                return scratch(EARLY[name], D)
            n = places["row"][name]
            assert n == rows_taken[0], name
            rows_taken[0] += 1
            dve.wait_ge(row_full[n % 3], 16 * (n // 3 + 1))
            return row_buf[:, n % 3, :]

        def row_done(dve, ins):
            ins.then_inc(sem("row_used"), 1)
            dve.wait_ge(sem("row_used"), rows_taken[0])

        NORMS = ("ln00", "ln01", "ln10", "ln11", "rn1", "rn2", "rnp", "rnf")
        LAYER_NORMS = NORMS[:4]
        TURNS = ("ln00", "ln01", "gdny", "ln10", "rn1", "att", "rn2", "rnp")

        def before(stages_, tag):
            return TILES * stages_.index(tag)

        flags_up = {e: 0 for e in FLAGS}

        def flag_up(name):
            e = next(e for e in FLAGS if name in FLAGS[e])
            assert FLAGS[e][flags_up[e]] == name, (name, FLAGS[e][flags_up[e]])
            flags_up[e] += 1
            return sem(f"{e}_flags")

        def flag(name):
            e = next(e for e in FLAGS if name in FLAGS[e])
            return sem(f"{e}_flags"), FLAGS[e].index(name) + 1

        chained = {"v": 0, "a": 0}

        def link(eng, ins, which="v"):
            chained[which] += 1
            ins.then_inc(sem("chain_" + which), 1)
            eng.wait_ge(sem("chain_" + which), chained[which])

        V, A, G, T = nc.vector, nc.scalar, nc.gpsimd, nc.tensor

        def sp_constants(sp):
            sp.dma_start(x[:], tokens).then_inc(sem("x_loaded"), 16)
            sp.dma_start(arena[:, 0:1536], bands).then_inc(sem("bands_loaded"), 16)
            both = weights[places["unit"]["pool_proj0"]]
            sp.dma_start(ring[:, 5, 0:HALF], both[:, 0:HALF]).then_inc(unit_full[5], 16)
            sp.dma_start(tab[:], tables).then_inc(sem("tables_loaded"), 16)
            for name, at in EARLY.items():
                n = places["row"][name]
                sp.dma_start(scratch(at, D), rows[n:n + 1, :].to_broadcast((P, D))).then_inc(sem(f"{name}_loaded"), 16)
            fill(sp, "gate00", 2)
            fill(sp, "gate01", 3)
            sp.dma_start(ring[:, 5, HALF:UNIT], both[:, HALF:UNIT]).then_inc(sem("proj0_loaded"), 16)
            sp.dma_start(pleT[:], ple_in).then_inc(sem("ple_loaded"), 16)
            sp.dma_start(par[:], small).then_inc(sem("small_loaded"), 16)

        def pool_rows(pool, first, last):
            for n in range(first, last):
                if n >= 3:
                    pool.wait_ge(sem("row_used"), n - 2)
                pool.dma_start(row_buf[:, n % 3, :], rows[n:n + 1, :].to_broadcast((P, D))).then_inc(row_full[n % 3], 16)

        def v_layer_norm(v, tag, src, gain, bias):
            for t in range(TILES):
                V.bn_stats(stats[:, t, 0, :], src[:, t, 0:512])
                link(v, V.bn_stats(stats[:, t, 1, :], src[:, t, 512:1024]))
                V.bn_aggr(mv[:, t, :], stats[:, t].rearrange("p a b -> p (a b)")).then_inc(sem("norm_var"), 1)
            g, b = row(v, gain), row(v, bias)
            for t in range(TILES):
                if t == 0:
                    v.wait_ge(sem("norm_var"), before(LAYER_NORMS, tag) + TILES)
                V.scalar_tensor_tensor(out=src[:, t, :], in0=src[:, t, :], scalar=mv[:, t, 0:1], in1=g,
                                       op0=ALU.subtract, op1=ALU.mult)
                v.wait_ge(sem("norm_std"), before(NORMS, tag) + t + 1)
                link(v, V.reciprocal(rstd[:, t:t + 1], std[:, t:t + 1]))
                V.scalar_tensor_tensor(out=x[:, t, :], in0=src[:, t, :], scalar=rstd[:, t:t + 1], in1=b,
                                       op0=ALU.mult, op1=ALU.add).then_inc(sem("norm_x"), 1)
            v.wait_ge(sem("norm_x"), before(NORMS, tag) + TILES)
            v.sem_inc(sem("row_used"), 1 if bias in EARLY else 2)

        def a_layer_norm(a, tag):
            for t in range(TILES):
                a.wait_ge(sem("norm_var"), before(LAYER_NORMS, tag) + t + 1)
                A.activation(std[:, t:t + 1], mv[:, t, 1:2], ACT.Sqrt, bias=eps(EPS5)).then_inc(sem("norm_std"), 1)

        def v_rms_norm(v, tag, gain, halves=1):
            g = row(v, gain)
            for t in range(TILES):
                v.wait_ge(sem("norm_std"), before(NORMS, tag) + t + 1)
                link(v, V.reciprocal(rstd[:, t:t + 1], std[:, t:t + 1]))
                last = V.scalar_tensor_tensor(out=pre[:, t, :], in0=x[:, t, :], scalar=rstd[:, t:t + 1], in1=g,
                                              op0=ALU.mult, op1=ALU.mult)
                last.then_inc(sem("norm_x"), 1)
            v.wait_ge(sem("norm_x"), before(NORMS, tag) + TILES)
            v.sem_inc(sem("row_used"), 1)

        def a_rms_norm(a, tag, ready, count):
            for t in range(TILES):
                if ready is not None:
                    a.wait_ge(sem(ready), count + t + 1)
                link(a, A.activation(pre[:, t, :], x[:, t, :], ACT.Square, accum_out=mv[:, t, 1:2]), "a")
                A.activation(std[:, t:t + 1], mv[:, t, 1:2], ACT.Sqrt, bias=eps(EPS6), scale=1.0 / D).then_inc(sem("norm_std"), 1)

        def pe_transpose(pe, tag, src, ready, count=0):
            for t in range(TILES):
                pe.wait_ge(sem(ready), count + t + 1)
                for c in range(KT):
                    at = (c % 4) * SEQ + t * P
                    m = T.transpose(ps[:, c // 4, at:at + P], src[:, t, c * P:(c + 1) * P], ident)
                    if t == TILES - 1 and c % 4 == 3:
                        m.then_inc(sem("T_psum"), 1)

        def v_transpose(v, tag):
            v.wait_ge(sem("T_psum"), before(TURNS, tag) + 1)
            V.tensor_copy(xT[:, 0:4, :], view(ps[:, 0, :], (4, SEQ))).then_inc(sem("T"), 1)

        def a_transpose(a, tag):
            a.wait_ge(sem("T_psum"), before(TURNS, tag) + 2)
            A.copy(xT[:, 4:8, :], view(ps[:, 1, :], (4, SEQ))).then_inc(sem("T"), 1)

        def pe_dense(pe, done, pair_of, slots):
            for t in range(TILES):
                for half in range(2):
                    for k in range(KT):
                        slot = slots[k // 4]
                        if t == 0 and half == 0 and k % 4 == 0:
                            take(pe, slot)
                        at = (k % 4) * D + half * 512
                        m = T.matmul(ps[:, pair_of[t], half * 512:half * 512 + 512], xT[:, k, t * P:(t + 1) * P],
                                     ring[:, slot, at:at + 512], start=(k == 0), stop=(k == KT - 1))
                m.then_inc(sem(done), 1)

        def pe_pool(pe):
            pe.wait_ge(sem("x_loaded"), 16)
            pe.wait_ge(sem("bands_loaded"), 16)
            for c in range(KT):
                g, at = c // 2, (c % 4) * SEQ
                band0, band1 = arena[:, g * SEQ:(g + 1) * SEQ], arena[:, 1024 + g * P:1024 + (g + 1) * P]
                T.matmul(ps[:, c // 4, at:at + SEQ], x[:, 0, c * P:(c + 1) * P], band0, start=True, stop=False)
                m = T.matmul(ps[:, c // 4, at + P:at + SEQ], x[:, 1, c * P:(c + 1) * P], band1, start=False, stop=True)
                if c % 4 == 3:
                    m.then_inc(sem("pool_T_psum"), 1)
            w = take(pe, 5)
            pe.wait_ge(sem("pool_T"), 2)
            for t in range(TILES):
                for g in range(4):
                    for k in range(2):
                        m = T.matmul(ps[:, 2 + t, g * 256:(g + 1) * 256], xT[:, 2 * g + k, t * P:(t + 1) * P],
                                     w[:, (2 * g + k) * 256:(2 * g + k + 1) * 256], start=(k == 0), stop=(k == 1))
                m.then_inc(sem("pool_psum"), 1)

        def v_pool(v):
            b = row(v, "pool_b")
            for t in range(TILES):
                v.wait_ge(sem("pool_psum"), t + 1)
                last = V.tensor_tensor(pre[:, t, :], ps[:, 2 + t, :], b, ALU.add)
            row_done(v, last)
            s = row(v, "pool_scale")
            for t in range(TILES):
                last = V.tensor_tensor(pre[:, t, :], pre[:, t, :], s, ALU.mult)
            row_done(v, last)
            for t in range(TILES):
                last = V.scalar_tensor_tensor(out=pre[:, t, :], in0=x[:, t, :], scalar=ALPHA, in1=pre[:, t, :],
                                              op0=ALU.mult, op1=ALU.add)
            link(v, last)

        def pe_ple(pe, tag, layer, gate_slots, proj_slot, proj_at, proj_taken=False):
            pe.wait_ge(sem("T"), before(TURNS, tag) + 2)
            pe_dense(pe, "ple_gate_psum", (0, 1), gate_slots)
            if not proj_taken:
                take(pe, proj_slot)
            for t in range(TILES):
                for half in range(2):
                    for k in range(2):
                        at = proj_at + k * D + half * 512
                        m = T.matmul(ps[:, 2 + t, half * 512:half * 512 + 512], pleT[:, layer, k, t * P:(t + 1) * P],
                                     ring[:, proj_slot, at:at + 512], start=(k == 0), stop=(k == 1))
                m.then_inc(sem("ple_proj_psum"), 1)

        def v_ple(v, layer):
            b = row(v, f"gate_b{layer}")
            for t in range(TILES):
                v.wait_ge(sem("ple_gate_psum"), TILES * layer + t + 1)
                last = V.tensor_tensor(side[:, t, :], ps[:, t, :], b, ALU.add).then_inc(sem("ple_logit"), 1)
            if f"gate_b{layer}" not in EARLY:
                v.wait_ge(sem("ple_logit"), TILES * layer + 2)
                v.sem_inc(sem("row_used"), 1)
            for t in range(TILES):
                v.wait_ge(sem("ple_proj_psum"), TILES * layer + t + 1)
                v.wait_ge(sem("ple_gate"), TILES * layer + t + 1)
                V.tensor_tensor(side[:, t, :], side[:, t, :], ps[:, 2 + t, :], ALU.mult).then_inc(sem("ple_side"), 1)

        def a_ple(a, layer):
            for t in range(TILES):
                a.wait_ge(sem("ple_logit"), TILES * layer + t + 1)
                A.activation(side[:, t, :], side[:, t, :], ACT.Sigmoid).then_inc(sem("ple_gate"), 1)

        ring_flat = ring[:].rearrange("p s n -> p (s n)")
        ring_split_flat = ring_split[:].rearrange("p s n -> p (s n)")

        def split_buffer(first_slot, b):
            at = first_slot * UNIT + b * 2 * CHUNK
            return ring_split_flat[:, at:at + CHUNK], ring_split_flat[:, at + CHUNK:at + 2 * CHUNK]

        def split_product(out_, high, low, weights_, k, start, stop):
            w_high, w_low = (w[:, k * STEP:(k + 1) * STEP] for w in weights_)
            T.matmul(out_, high, w_high, start=start, stop=False, skip_group_check=True)
            T.matmul(out_, high, w_low, start=False, stop=False, skip_group_check=True)
            return T.matmul(out_, low, w_high, start=False, stop=stop, skip_group_check=True)

        x_high, x_low = split_scratch(0, KT, SEQ), split_scratch(2048, KT, SEQ)
        hid_high, hid_low = split_scratch(4096, 2, 4, SEQ), split_scratch(6144, 2, 4, SEQ)
        relu = view(xT[:].rearrange("p k t -> p (k t)"), (2, TILES, STEP))
        MLP_CHUNKS, MLP_BUFFERS, MLP_SPLIT_SLOT = 8 * MLP_STEPS, 4, 4
        mlp_base = {}

        def up_chunk(s, c):
            return 8 * s - 4 + c

        def down_chunk(s, c):
            return 8 * s + 8 + c

        def raw_up(par, c):
            return ring[:, 2 * par, c * CHUNK:(c + 1) * CHUNK]

        def raw_down(par, c):
            return ring[:, 2 * par + 1, c * CHUNK:(c + 1) * CHUNK]

        def sp_mlp(sp, layer):
            ups = weights[places["unit"][f"mlp{layer}_up0"]:places["unit"][f"mlp{layer}_up0"] + 2 * MLP_STEPS]
            ups = ups.rearrange("(i j m) p n -> i j m p n", j=2, m=2)
            with sp.Fori(0, MLP_STEPS // 2 - 1) as i:
                for j in range(2):
                    sp.wait_ge(sem("mlp_low"), MLP_CHUNKS * layer + 16 * i + 8 * j + 4)
                    sp.dma_start(ring[:, 2 * j, :], ups[i + 1, j, 0]).then_inc(unit_full[2 * j], 16)
                    sp.wait_ge(sem("mlp_low"), MLP_CHUNKS * layer + 16 * i + 8 * j + 12)
                    sp.dma_start(ring[:, 2 * j + 1, :], ups[i + 1, j, 1]).then_inc(unit_full[2 * j + 1], 16)

        def sp_after_mlp(sp, layer, names):
            at = MLP_CHUNKS * layer
            fill(sp, names[0], 0, "mlp_low", at + 52)
            fill(sp, names[1], 1, "mlp_low", at + 60)
            fill(sp, names[2], 2, "mlp_low", at + 60)
            fill(sp, names[3], 3, "mlp_low", at + 64)
            fill(sp, names[4], 4, "mlp_product", at + MLP_CHUNKS)
            fill(sp, names[5], 5)

        def pe_mlp(pe, layer):
            mlp_base[layer] = taken[:4]
            base = MLP_CHUNKS * layer

            def weights_of(g, buffer):
                pe.wait_ge(sem("mlp_low"), base + g + 1)
                return split_buffer(MLP_SPLIT_SLOT, buffer)

            def up(s, chunks, first=False):
                for c in chunks:
                    if c == 0 and not first:
                        pe.wait_ge(sem("mlp_relu"), 16 * layer + 2 * s)
                    w = weights_of(c if first else up_chunk(s, c), c)
                    for t in range(TILES):
                        for k in range(2):
                            m = split_product(ps[:, 0, t * 512:t * 512 + 512], x_high[:, 2 * c + k, t * P:(t + 1) * P],
                                              x_low[:, 2 * c + k, t * P:(t + 1) * P], w, k,
                                              c == 0 and k == 0, c == 3 and k == 1)
                    m.then_inc(sem("mlp_product"), 1)

            def turn(s, par, first=False):
                pe.wait_ge(sem("mlp_square"), 16 * layer + 2 * s + 2)
                if not first:
                    pe.wait_ge(sem("mlp_hid_low"), 8 * layer + s)
                for t in range(TILES):
                    for k in range(4):
                        m = T.transpose(ps[:, 1, k * SEQ + t * P:k * SEQ + (t + 1) * P],
                                        relu[:, par, t, k * P:(k + 1) * P], ident)
                m.then_inc(sem("mlp_hid_psum"), 1)

            def down(s, par, first=False, last=False):
                pe.wait_ge(sem("mlp_hid_low"), 8 * layer + s + 1)
                for c in range(4):
                    half_, k0 = c // 2, 2 * (c % 2)
                    w = weights_of(down_chunk(s, c) - (4 if last else 0), c)
                    for t in range(TILES):
                        for k in range(2):
                            m = split_product(ps[:, 2 + t, half_ * 512:half_ * 512 + 512],
                                              hid_high[:, par, k0 + k, t * P:(t + 1) * P],
                                              hid_low[:, par, k0 + k, t * P:(t + 1) * P], w, k,
                                              first and k0 + k == 0, last and k0 + k == 3)
                    m.then_inc(sem("mlp_product"), 1)

            def step(s, par, first=False):
                up(s + 1, (0,))
                turn(s, par, first)
                up(s + 1, (1, 2, 3))
                down(s, par, first)

            pe.wait_ge(sem("ple_side"), TILES * layer + 2)
            up(0, (0, 1, 2, 3), first=True)
            step(0, 0, first=True)
            step(1, 1)
            with pe.Fori(1, MLP_STEPS // 2 - 1) as i:
                step(2 * i, 0)
                step(2 * i + 1, 1)
            step(MLP_STEPS - 2, 0)
            turn(MLP_STEPS - 1, 1)
            down(MLP_STEPS - 1, 1, last=True)
            for slot in range(4):
                taken[slot] += 4

        def v_mlp_low(v, layer, g, raw, buffer):
            v.wait_ge(sem("mlp_high"), MLP_CHUNKS * layer + g + 1)
            high, low = split_buffer(MLP_SPLIT_SLOT, buffer)
            V.tensor_tensor(low, raw, high, ALU.subtract).then_inc(sem("mlp_low"), 1)

        def v_mlp_x(v, layer):
            v.wait_ge(sem("mlp_x_high"), layer + 1)
            V.tensor_tensor(x_low, xT[:], x_high, ALU.subtract)
            for c in range(2):
                v_mlp_low(v, layer, c, raw_up(0, c), c)

        def v_mlp(v, layer):
            def step(s, par, first=False, early=False, last=False):
                for t in range(TILES):
                    if t == 0:
                        v.wait_ge(sem("mlp_product"), MLP_CHUNKS * layer + (4 if first else 8 * s))
                        if not early:
                            v.wait_ge(sem("mlp_hid_psum"), 8 * layer + s - 1)
                    V.tensor_scalar(relu[:, par, t, :], ps[:, 0, t * 512:t * 512 + 512], 0.0, None, ALU.max)\
                     .then_inc(sem("mlp_relu"), 1)
                if not last:
                    for c in range(4):
                        v_mlp_low(v, layer, up_chunk(s + 1, c), raw_up(1 - par, c), c)
                v.wait_ge(sem("mlp_hid_high"), 8 * layer + s + 1)
                V.tensor_tensor(hid_low[:, par], view(ps[:, 1, :], (4, SEQ)), hid_high[:, par], ALU.subtract)\
                 .then_inc(sem("mlp_hid_low"), 1)
                for c in range(4):
                    v_mlp_low(v, layer, down_chunk(s, c) - (4 if last else 0), raw_down(par, c), c)

            for c in (2, 3):
                v_mlp_low(v, layer, c, raw_up(0, c), c)
            v.wait_ge(sem("ple_side"), TILES * (layer + 1))
            V.scalar_tensor_tensor(out=side[:], in0=x[:], scalar=ALPHA, in1=side[:], op0=ALU.mult, op1=ALU.add)\
             .then_inc(sem("mlp_side"), 1)
            step(0, 0, first=True, early=True)
            step(1, 1, early=True)
            with v.Fori(1, MLP_STEPS // 2 - 1) as i:
                step(2 * i, 0)
                step(2 * i + 1, 1)
            step(MLP_STEPS - 2, 0)
            step(MLP_STEPS - 1, 1, last=True)
            v.wait_ge(sem("mlp_product"), MLP_CHUNKS * (layer + 1))
            v.wait_ge(sem("mlp_side"), layer + 1)
            for t in range(TILES):
                m = V.tensor_tensor(pre[:, t, :], ps[:, 2 + t, :], side[:, t, :], ALU.add)
            link(v, m)

        def a_mlp_high(a, layer, g, raw, buffer, reused=True):
            if reused:
                a.wait_ge(sem("mlp_product"), MLP_CHUNKS * layer + g - MLP_BUFFERS + 1)
            A.copy(split_buffer(MLP_SPLIT_SLOT, buffer)[0], raw).then_inc(sem("mlp_high"), 1)

        def a_mlp_x(a, tag, layer):
            a.wait_ge(sem("T"), before(TURNS, tag) + 2)
            A.copy(x_high, xT[:]).then_inc(sem("mlp_x_high"), 1)
            a.wait_ge(unit_full[0], 16 * (mlp_base[layer][0] + 1))
            if layer == 1:
                a.wait_ge(sem("gdn_out_psum"), TILES)
            for c in range(2):
                a_mlp_high(a, layer, c, raw_up(0, c), c, reused=False)

        def a_mlp(a, layer):
            base = mlp_base[layer]

            def step(s, par, round_, early=False, last=False):
                for t in range(TILES):
                    a.wait_ge(sem("mlp_relu"), 16 * layer + 2 * s + t + 1)
                    A.activation(relu[:, par, t, :], relu[:, par, t, :], ACT.Square).then_inc(sem("mlp_square"), 1)
                if not last:
                    slot = 2 * (1 - par)
                    a.wait_ge(unit_full[slot], 16 * round_ + 16 * (base[slot] + 1 + par))
                    for c in range(4):
                        a_mlp_high(a, layer, up_chunk(s + 1, c), raw_up(1 - par, c), c)
                a.wait_ge(sem("mlp_hid_psum"), 8 * layer + s + 1)
                if not early:
                    a.wait_ge(sem("mlp_product"), MLP_CHUNKS * layer + 8 * s - 4)
                A.copy(hid_high[:, par], view(ps[:, 1, :], (4, SEQ))).then_inc(sem("mlp_hid_high"), 1)
                slot = 2 * par + 1
                a.wait_ge(unit_full[slot], 16 * round_ + 16 * (base[slot] + 1))
                for c in range(4):
                    a_mlp_high(a, layer, down_chunk(s, c) - (4 if last else 0), raw_down(par, c), c)

            a.wait_ge(sem("ple_proj_psum"), TILES * layer + 2)
            for c in (2, 3):
                a_mlp_high(a, layer, c, raw_up(0, c), c, reused=False)
            step(0, 0, 0, early=True)
            step(1, 1, 0, early=True)
            with a.Fori(1, MLP_STEPS // 2 - 1) as i:
                step(2 * i, 0, i)
                step(2 * i + 1, 1, i)
            step(MLP_STEPS - 2, 0, 3)
            step(MLP_STEPS - 1, 1, 3, last=True)

        qkvT = scratch(0, 24, SEQ)
        z_silu = scratch(6144, TILES, D)
        g_small = arena[:, 8192:9728]
        logits2 = view(g_small[:, 0:32], (16, TILES))
        beta, g_in, g_log, g_abs, g_dec, gc, exp_gc, bg, g_ea = (
            view(g_small[:, 32 + 16 * n:48 + 16 * n], (HEADS, TILES)) for n in range(9))
        rms16 = g_small[:, 192:208]
        rowsT = view(g_small[0:8, 256:768], (2, TILES, P))
        root8 = view(g_small[0:8, 768:1280], (2, SEQ))
        slot01 = ring[:, 0:2, :].rearrange("p a b -> p (a b)")
        slot23 = ring[:, 2:4, :].rearrange("p a b -> p (a b)")

        def heads16(flat):
            return flat.rearrange("p (h t c) -> p h t c", h=HEADS, t=TILES)

        LT, TI, TT, PR = (slot01[:, 2048 * n:2048 * (n + 1)] for n in range(4))
        DEC, QKT, VB = (slot23[:, 2048 * n:2048 * (n + 1)] for n in range(3))
        KBG, KD = slot23[:, 6144:7168], slot23[:, 7168:8192]
        MT = pre[:].rearrange("p a b -> p (a b)")
        U0, VNEW = side[:, 0, :], side[:, 1, :]
        WTN, STATE = TI[:, 0:1024], TI[:, 1024:2048]
        O = view(PR, (TILES, D))
        pair01 = ps[:, 0:2, :].rearrange("p a b -> p (a b)")
        pair23 = ps[:, 2:4, :].rearrange("p a b -> p (a b)")
        LEVELS = 7

        def half(flat, g):
            return flat[:, 1024 * g:1024 * (g + 1)]

        def system(flat, h, t):
            return flat[:, (2 * h + t) * P:(2 * h + t + 1) * P]

        def pe_gdn_in(pe):
            pe.wait_ge(sem("T"), before(TURNS, "ln01") + 2)
            pe.wait_ge(sem("small_loaded"), 16)
            w_ba = view(param("w_ba"), (KT, 16))
            for t in range(TILES):
                for k in range(KT):
                    m = T.matmul(ps[:, 3, 512 + 16 * t:528 + 16 * t], xT[:, k, t * P:(t + 1) * P], w_ba[:, k, :],
                                 start=(k == 0), stop=(k == KT - 1))
            m.then_inc(flag_up("gdn_ba_psum"), 1)
            for n in range(6):
                w = take(pe, GDN_IN_SLOTS[n])
                if n == 3:
                    pe.wait_ge(*flag("gdn_g"))
                    pe.wait_ge(*flag("gdn_beta"))
                    for t in range(TILES):
                        T.matmul(ps[:, 3, 8 * t:8 * t + 8], upto, g_dec[:, :, t], start=True, stop=True)
                        T.matmul(ps[0:8, 3, 512 + P * t:512 + P * (t + 1)], g_dec[:, :, t], upto, start=True, stop=True)
                        m = T.transpose(ps[0:8, 3, 768 + P * t:768 + P * (t + 1)], beta[:, :, t], ident)
                    m.then_inc(flag_up("gdn_rows_psum"), 1)
                    pe.wait_ge(sem("gdn_rows"), 2)
                if n >= 4:
                    pe.wait_ge(sem("gdn_conv"), n - 3)
                for b in range(4):
                    for k in range(KT):
                        m = T.matmul(ps[:, n % 4, b * SEQ:(b + 1) * SEQ], w[:, k * STEP + b * P:k * STEP + (b + 1) * P],
                                     xT[:, k, :], start=(k == 0), stop=(k == KT - 1))
                m.then_inc(sem("gdn_in_psum"), 1)
            pe.wait_ge(sem("gdn_conv"), 4)
            for half_ in range(2):
                w = take(pe, GDN_IN_SLOTS[6 + half_])
                for t in range(TILES):
                    for k in range(KT):
                        m = T.matmul(ps[:, 2 + t, half_ * 512:half_ * 512 + 512], xT[:, k, t * P:(t + 1) * P],
                                     w[:, k * STEP:(k + 1) * STEP], start=(k == 0), stop=(k == KT - 1))
                m.then_inc(sem("gdn_z_psum"), 1)
                if half_ == 0:
                    pe.wait_ge(sem("gdn_conv"), 5)
                    head_col = table("head_col")
                    for n, src in enumerate((pre, side)):
                        pe.wait_ge(sem("gdn_sq"), n + 1)
                        for h in range(HEADS):
                            m = T.matmul(ps[0:8, 0, 512 * n:512 * n + SEQ], head_col[:, HEADS * h:HEADS * (h + 1)],
                                         src[:, h // 4, (h % 4) * SEQ:(h % 4 + 1) * SEQ], start=(h == 0), stop=(h == HEADS - 1))
                        m.then_inc(sem("gdn_sum_psum"), 1)

        GDN_IN_SLOTS = (0, 1, 2, 3, 4, 5, 4, 5)
        conv_w = view(param("conv"), (24, 4))

        def a_gdn_in(a):
            a.wait_ge(sem("small_loaded"), 16)
            a.wait_ge(*flag("gdn_ba"))
            A.activation(beta, logits2[:, 0:8, :], ACT.Sigmoid).then_inc(flag_up("gdn_beta"), 1)
            a.wait_ge(*flag("gdn_g_in"))
            link(a, A.activation(g_abs, g_in, ACT.Abs), "a")
            link(a, A.activation(g_abs, g_abs, ACT.Exp, scale=-1.0), "a")
            A.activation(g_ea, spread(param("a_log"), TILES), ACT.Exp)
            A.activation(g_log, g_abs, ACT.Ln, bias=eps(ONE)).then_inc(flag_up("gdn_log"), 1)

            def taps(n):
                a.wait_ge(sem("gdn_in_psum"), n + 1)
                for b in range(4):
                    m = A.activation(qkvT[:, 4 * n + b, :], ps[:, n % 4, b * SEQ:(b + 1) * SEQ], ACT.Copy,
                                     scale=conv_w[:, 4 * n + b, 3:4])
                m.then_inc(sem("gdn_tap"), 1)

            def silu(n):
                a.wait_ge(sem("gdn_conv"), n + 1)
                A.activation(qkvT[:, 4 * n:4 * n + 4, :], qkvT[:, 4 * n:4 * n + 4, :], ACT.Silu).then_inc(sem("gdn_qkv"), 1)

            for n in range(6):
                taps(n)
                if n == 2:
                    a.wait_ge(sem("gdn_rows"), 1)
                    A.activation(exp_gc, gc, ACT.Exp).then_inc(flag_up("gdn_exp_gc"), 1)
                silu(n)
                if n in (3, 4):
                    a.wait_ge(sem("gdn_qkv"), 4)
                    q_or_k = qkvT[:, 8 * (n - 3):8 * (n - 2), :].rearrange("p a b -> p (a b)")
                    A.activation((pre, side)[n - 3][:], view(q_or_k, (TILES, D)), ACT.Square).then_inc(sem("gdn_sq"), 1)
            for n in range(2):
                a.wait_ge(sem("gdn_sum_psum"), n + 1)
                A.activation(root8[:, n, :], ps[0:8, 0, 512 * n:512 * n + SEQ], ACT.Sqrt, bias=eps(EPS6 if n else EPS6_128)[0:8],
                             scale=1.0 if n else float(P)).then_inc(sem("gdn_root"), 1)
            a.wait_ge(sem("gdn_z_psum"), 2)
            A.activation(z_silu, ps[:, 2:4, :], ACT.Silu).then_inc(flag_up("gdn_z"), 1)

        def v_gdn_in(v):
            v.wait_ge(sem("small_loaded"), 16)
            v.wait_ge(*flag("gdn_ba_psum"))
            for t in range(TILES):
                m = V.tensor_copy(logits2[:, :, t], ps[:, 3, 512 + 16 * t:528 + 16 * t])
            m.then_inc(flag_up("gdn_ba"), 1)
            v.wait_ge(*flag("gdn_ba"))
            V.tensor_tensor(g_in, logits2[:, 8:16, :], spread(param("dt_bias"), TILES), ALU.add).then_inc(flag_up("gdn_g_in"), 1)
            v.wait_ge(*flag("gdn_log"))
            v.wait_ge(*flag("gdn_g_in"))
            link(v, V.scalar_tensor_tensor(out=g_log, in0=g_in, scalar=0.0, in1=g_log, op0=ALU.max, op1=ALU.add))
            V.scalar_tensor_tensor(out=g_dec, in0=g_log, scalar=-1.0, in1=g_ea, op0=ALU.mult, op1=ALU.mult)\
             .then_inc(flag_up("gdn_g"), 1)
            for n in range(6):
                v.wait_ge(sem("gdn_tap"), n + 1)
                for tap in (2, 1, 0):
                    s = 3 - tap
                    for b in range(4):
                        m = V.scalar_tensor_tensor(out=qkvT[:, 4 * n + b, s:SEQ], in0=ps[:, n % 4, b * SEQ:(b + 1) * SEQ - s],
                                                   scalar=conv_w[:, 4 * n + b, tap:tap + 1], in1=qkvT[:, 4 * n + b, s:SEQ],
                                                   op0=ALU.mult, op1=ALU.add)
                    if tap:
                        link(v, m)
                m.then_inc(sem("gdn_conv"), 1)
                if n == 1:
                    v.wait_ge(*flag("gdn_rows_psum"))
                    V.tensor_copy(gc, ps[:, 3, 0:16].rearrange("p (t h) -> p h t", t=TILES)).then_inc(sem("gdn_rows"), 1)
                    V.tensor_copy(rowsT.rearrange("p a t c -> p (a t c)"), ps[0:8, 3, 512:1024]).then_inc(sem("gdn_rows"), 1)
            v.wait_ge(*flag("gdn_exp_gc"))
            link(v, V.tensor_tensor(bg, beta, exp_gc, ALU.mult))
            for n in range(2):
                v.wait_ge(sem("gdn_root"), n + 1)
                V.reciprocal(root8[:, n, :], root8[:, n, :]).then_inc(sem("gdn_rnorm"), 1)
            for n, pair in enumerate((pair01, pair23)):
                v.wait_ge(sem("gdn_rnorm_psum"), n + 1)
                blocks = qkvT[:, 8 * n:8 * n + 8, :].rearrange("p a b -> p (a b)")
                V.tensor_tensor(blocks, blocks, pair, ALU.mult).then_inc(sem("gdn_unit"), 1)

        def pe_gdn_norms(pe):
            pick = table("pick_head")
            for n, pair in enumerate((pair01, pair23)):
                if n == 0:
                    pe.wait_ge(sem("gdn_rnorm"), 2)
                    pe.wait_ge(sem("gdn_conv"), 6)
                else:
                    pe.wait_ge(*flag("gdn_z"))
                for h in range(HEADS):
                    m = T.matmul(pair[:, h * SEQ:(h + 1) * SEQ], pick[0:8, h * P:(h + 1) * P], root8[:, n, :],
                                 start=True, stop=True)
                m.then_inc(sem("gdn_rnorm_psum"), 1)

        def pe_gdn_scores(pe):
            pick = table("pick_head")

            def rows_out(which, out_, done):
                for h in range(HEADS):
                    m = T.matmul(out_[:, h * SEQ:(h + 1) * SEQ], pick[0:8, h * P:(h + 1) * P],
                                 rowsT[:, which].rearrange("p t c -> p (t c)"), start=True, stop=True)
                m.then_inc(sem(done), 1)

            pe.wait_ge(sem("gdn_unit"), 1)
            rows_out(0, pair01, "gdn_G_psum")
            pe.wait_ge(sem("gdn_unit"), 2)
            rows_out(1, pair23, "gdn_B_psum")
            pe.wait_ge(*flag("gdn_diff"))
            for h in range(HEADS):
                for t in range(TILES):
                    k = qkvT[:, 8 + h, t * P:(t + 1) * P]
                    m = T.matmul(system(pair01, h, t), k, k, start=True, stop=True)
            m.then_inc(flag_up("gdn_KK_psum"), 1)
            pe.wait_ge(*flag("gdn_DB"))
            for h in range(HEADS):
                for t in range(TILES):
                    m = T.matmul(system(pair23, h, t), qkvT[:, 8 + h, t * P:(t + 1) * P], qkvT[:, h, t * P:(t + 1) * P],
                                 start=True, stop=True)
            m.then_inc(flag_up("gdn_QK_psum"), 1)
            pe.wait_ge(*flag("gdn_LT"))
            for h in range(HEADS):
                for t in range(TILES):
                    m = T.transpose(system(pair01, h, t), qkvT[:, 8 + h, t * P:(t + 1) * P], ident)
            m.then_inc(flag_up("gdn_k_psum"), 1)
            pe.wait_ge(*flag("gdn_QKT"))
            for h in range(HEADS):
                for t in range(TILES):
                    m = T.transpose(system(pair23, h, t), qkvT[:, 16 + h, t * P:(t + 1) * P], ident)
            m.then_inc(flag_up("gdn_v_psum"), 1)

        def a_gdn_scores(a):
            a.wait_ge(*flag("gdn_diff"))
            A.activation(DEC, DEC, ACT.Exp).then_inc(flag_up("gdn_exp"), 1)

        def v_gdn_scores(v):
            g3 = lambda flat: flat.rearrange("p (s c) -> p s c", c=P)
            v.wait_ge(sem("gdn_G_psum"), 1)
            for h in range(HEADS):
                for t in range(TILES):
                    m = V.tensor_scalar(system(DEC, h, t), system(pair01, h, t), gc[:, h, t:t + 1], 0.0,
                                        ALU.subtract, ALU.min)
            m.then_inc(flag_up("gdn_diff"), 1)
            v.wait_ge(*flag("gdn_exp"))
            link(v, V.tensor_tensor(g3(DEC), g3(DEC), repeat(upto, 16), ALU.mult))
            v.wait_ge(sem("gdn_B_psum"), 1)
            V.tensor_tensor(LT, DEC, pair23, ALU.mult).then_inc(flag_up("gdn_DB"), 1)
            v.wait_ge(*flag("gdn_DB"))
            v.wait_ge(*flag("gdn_KK_psum"))
            V.tensor_tensor(LT, LT, pair01, ALU.mult).then_inc(flag_up("gdn_LT"), 1)
            v.wait_ge(*flag("gdn_QK_psum"))
            V.tensor_tensor(QKT, DEC, pair23, ALU.mult).then_inc(flag_up("gdn_QKT"), 1)
            v.wait_ge(*flag("gdn_LT"))
            for g in range(2):
                V.tensor_tensor(g3(half(MT, g)), g3(half(LT, g)), repeat(table("level0"), 8), ALU.mult)\
                 .then_inc(sem("gdn_MT"), 1)
            v.wait_ge(sem("gdn_MT"), 2)
            for g in range(2):
                V.tensor_tensor(g3(half(TT, g)), repeat(ident, 8), g3(half(MT, g)), ALU.subtract).then_inc(sem("gdn_TT"), 1)
            v.wait_ge(*flag("gdn_k_psum"))
            last_col = heads16(DEC)[:, :, 0, P - 1:P].to_broadcast((P, HEADS, P))
            V.tensor_tensor(g3(KD), heads16(pair01)[:, :, 0, :], last_col, ALU.mult)
            V.tensor_tensor(g3(KBG), heads16(pair01)[:, :, 1, :], bg[:, :, 1:2].to_broadcast((P, HEADS, P)), ALU.mult)\
             .then_inc(flag_up("gdn_k_ready"), 1)
            v.wait_ge(*flag("gdn_v_psum"))
            V.tensor_tensor(g3(VB), g3(pair23), spread(beta.rearrange("p h t -> p (h t)"), P), ALU.mult)\
             .then_inc(flag_up("gdn_v_ready"), 1)

        def pe_gdn_inverse(pe):
            s_MT, s_T, s_TT, s_P = sem("gdn_MT"), sem("gdn_T"), sem("gdn_TT"), sem("gdn_P")
            P_psum, T_psum, TT_psum = sem("gdn_P_psum"), sem("gdn_T_psum"), sem("gdn_TT_psum")

            def systems(out_, lhsT, rhs, g, done):
                for q in range(8):
                    a_, b_ = 1024 * g + P * q, 1024 * g + P * (q + 1)
                    m = T.matmul(out_[:, P * q:P * (q + 1)], lhsT[:, a_:b_], rhs[:, a_:b_] if rhs is not None else ident,
                                 start=True, stop=True)
                m.then_inc(done, 1)

            def level(l, update_T=True):
                for g in range(2):
                    pe.wait_ge(s_MT, 2 * l + g + 1)
                    pe.wait_ge(s_T, 2 * l + g - 1)
                    pe.wait_ge(s_TT, 2 * l + g - 1)
                    systems(ps[:, g, :], MT, TI, g, P_psum)
                for g in range(2):
                    pe.wait_ge(s_P, 2 * l + g - 1)
                    if update_T:
                        systems(ps[:, 2 + g, :], TT, PR, g, T_psum)
                    systems(ps[:, g, :], PR, TT, g, TT_psum)

            pe.wait_ge(*flag("gdn_k_ready"))
            for g in range(2):
                pe.wait_ge(s_MT, g + 1)
                systems(ps[:, g, :], MT, None, g, P_psum)
            pe.wait_ge(*flag("gdn_v_ready"))
            with pe.Fori(1, LEVELS - 1) as l:
                level(l)
            level(LEVELS - 1, update_T=False)

        def a_gdn_inverse(a):
            def level(l):
                for g in range(2):
                    a.wait_ge(sem("gdn_P_psum"), 2 * l + g + 1)
                    A.copy(half(PR, g), ps[:, g, :]).then_inc(sem("gdn_P"), 1)

            with a.Fori(1, LEVELS) as l:
                level(l)

        def v_gdn_inverse(v):
            g3 = lambda flat: flat.rearrange("p (s c) -> p s c", c=P)
            masks_at, _ = places["table"]["level0"]

            def mask(l):
                return tab[:, masks_at:masks_at + LEVELS * P].rearrange("p (l c) -> p l c", c=P)[:, l, :]

            def next_M(l):
                for g in range(2):
                    v.wait_ge(sem("gdn_P_psum"), 2 * l + g - 1)
                    V.tensor_tensor(g3(half(MT, g)), g3(half(LT, g)), repeat(mask(l), 8), ALU.mult)\
                     .then_inc(sem("gdn_MT"), 1)

            def update_TT(l, g):
                v.wait_ge(sem("gdn_TT_psum"), 2 * l + g - 1)
                V.tensor_tensor(half(TT, g), half(TT, g), ps[:, g, :], ALU.subtract).then_inc(sem("gdn_TT"), 1)

            for g in range(2):
                v.wait_ge(sem("gdn_P_psum"), g + 1)
                V.tensor_tensor(g3(half(TI, g)), repeat(ident, 8), g3(ps[:, g, :]), ALU.subtract).then_inc(sem("gdn_T"), 1)
            next_M(1)
            with v.Fori(1, LEVELS - 1) as l:
                next_M(l + 1)
                for g in range(2):
                    v.wait_ge(sem("gdn_T_psum"), 2 * l + g - 1)
                    V.tensor_tensor(half(TI, g), half(TI, g), ps[:, 2 + g, :], ALU.subtract).then_inc(sem("gdn_T"), 1)
                    update_TT(l, g)
            for g in range(2):
                update_TT(LEVELS - 1, g)

        def pe_gdn_out(pe):
            head = lambda flat, h: flat[:, h * P:(h + 1) * P]
            pe.wait_ge(sem("gdn_TT"), 2 * LEVELS)
            for h in range(HEADS):
                m = T.matmul(head(ps[:, 0, :], h), system(TT, h, 0), system(VB, h, 0), start=True, stop=True)
            m.then_inc(flag_up("gdn_u0_psum"), 1)
            for h in range(HEADS):
                m = T.matmul(head(ps[:, 1, :], h), head(KBG, h), system(TT, h, 1), start=True, stop=True)
            m.then_inc(flag_up("gdn_wT_psum"), 1)
            pe.wait_ge(*flag("gdn_u0"))
            for h in range(HEADS):
                m = T.matmul(head(ps[:, 2, :], h), head(KD, h), head(U0, h), start=True, stop=True)
            m.then_inc(flag_up("gdn_state_psum"), 1)
            for h in range(HEADS):
                m = T.matmul(head(ps[:, 0, :], h), system(QKT, h, 0), head(U0, h), start=True, stop=True)
            m.then_inc(flag_up("gdn_o0_psum"), 1)
            pe.wait_ge(*flag("gdn_wT"))
            pe.wait_ge(*flag("gdn_state"))
            for h in range(HEADS):
                T.matmul(head(ps[:, 3, :], h), system(TT, h, 1), system(VB, h, 1), start=True, stop=False)
                m = T.matmul(head(ps[:, 3, :], h), head(WTN, h), head(STATE, h), start=False, stop=True)
            m.then_inc(flag_up("gdn_vnew_psum"), 1)
            for h in range(HEADS):
                m = T.matmul(head(ps[:, 1, :], h), qkvT[:, h, P:SEQ], head(STATE, h), start=True, stop=True)
            m.then_inc(flag_up("gdn_os_psum"), 1)
            pe.wait_ge(*flag("gdn_vnew"))
            for h in range(HEADS):
                m = T.matmul(head(ps[:, 2, :], h), system(QKT, h, 1), head(VNEW, h), start=True, stop=True)
            m.then_inc(flag_up("gdn_o1_psum"), 1)

        def a_gdn_out(a):
            a.wait_ge(*flag("gdn_u0_psum"))
            A.copy(U0, ps[:, 0, :]).then_inc(flag_up("gdn_u0"), 1)
            a.wait_ge(*flag("gdn_state_psum"))
            A.copy(STATE, ps[:, 2, :]).then_inc(flag_up("gdn_state"), 1)

            def root(t):
                a.wait_ge(sem("gdn_o_sum"), t + 1)
                part = rms16[:, HEADS * t:HEADS * (t + 1)]
                A.activation(part, part, ACT.Sqrt, bias=eps(EPS6), scale=1.0 / P).then_inc(sem("gdn_o_root"), 1)

            a.wait_ge(sem("gdn_o"), 1)
            A.activation(pre[:, 0, :], O[:, 0, :], ACT.Square).then_inc(sem("gdn_o_square"), 1)
            a.wait_ge(*flag("gdn_vnew_psum"))
            A.copy(VNEW, ps[:, 3, :]).then_inc(flag_up("gdn_vnew"), 1)
            root(0)
            a.wait_ge(sem("gdn_o"), 2)
            A.activation(pre[:, 1, :], O[:, 1, :], ACT.Square).then_inc(sem("gdn_o_square"), 1)
            root(1)

        def v_gdn_out(v):
            g3 = lambda flat: flat.rearrange("p (s c) -> p s c", c=P)
            v.wait_ge(*flag("gdn_wT_psum"))
            V.tensor_scalar(WTN, ps[:, 1, :], -1.0, None, ALU.mult).then_inc(flag_up("gdn_wT"), 1)
            v.wait_ge(*flag("gdn_o0_psum"))
            V.tensor_copy(O[:, 0, :], ps[:, 0, :]).then_inc(sem("gdn_o"), 1)

            def square_sum(t):
                v.wait_ge(sem("gdn_o_square"), t + 1)
                V.tensor_reduce(rms16[:, HEADS * t:HEADS * (t + 1)], pre[:, t, :].rearrange("p (h c) -> p h c", c=P), AX.X, ALU.add)\
                 .then_inc(sem("gdn_o_sum"), 1)

            def normed(t):
                v.wait_ge(sem("gdn_o_root"), t + 1)
                part = rms16[:, HEADS * t:HEADS * (t + 1)]
                link(v, V.reciprocal(part, part))
                o = O[:, t, :].rearrange("p (h c) -> p h c", c=P)
                link(v, V.tensor_tensor(o, o, spread(part, P), ALU.mult))
                V.tensor_tensor(pre[:, t, :], O[:, t, :], z_silu[:, t, :], ALU.mult).then_inc(sem("gdn_y"), 1)

            square_sum(0)
            v.wait_ge(*flag("gdn_os_psum"))
            link(v, V.tensor_tensor(g3(O[:, 1, :]), g3(ps[:, 1, :]), exp_gc[:, :, 1:2].to_broadcast((P, HEADS, P)), ALU.mult))
            v.wait_ge(*flag("gdn_o1_psum"))
            V.tensor_tensor(O[:, 1, :], O[:, 1, :], ps[:, 2, :], ALU.add).then_inc(sem("gdn_o"), 1)
            v.wait_ge(sem("gdn_zw"), 1)
            normed(0)
            square_sum(1)
            normed(1)

        def pool_gdn_z(pool):
            pool.wait_ge(*flag("gdn_z"))
            pool.wait_ge(sem("small_loaded"), 16)
            z16 = z_silu.rearrange("p t (h c) -> p (t h) c", c=P)
            G.tensor_tensor(z16, z16, repeat(param("norm_w"), 16), ALU.mult).then_inc(sem("gdn_zw"), 1)

        def v_residual(v, done, pairs, scale):
            for t in range(TILES):
                v.wait_ge(sem(done), t + 1)
                m = V.scalar_tensor_tensor(out=pre[:, t, :], in0=x[:, t, :], scalar=scale, in1=ps[:, pairs[t], :],
                                           op0=ALU.mult, op1=ALU.add)
            link(v, m)

        SEL, WIN, FOX = range(3)
        HD = 64
        COLS = P + SEQ
        projT = scratch(0, 16, SEQ)
        qnT, kvcT, ksT, kwT, qfT, kfT = projT[:, 0:4], projT[:, 4:6], projT[:, 6], projT[:, 7], projT[:, 8:12], projT[:, 12:16]
        nat = scratch(4096, TILES, 288)
        vf = scratch(4672, TILES, 512)
        cmp_in = scratch(5696, 32, 30)
        fox_bias = scratch(6656, HEADS, COLS)
        prob = view(slot01[:, 0:1536], (2, 2, COLS))
        probT = view(slot01[:, 1536:3072], (2, 6, P))
        o_att = view(slot01[:, 3072:6144], (3, TILES, 512))
        v_blk = view(slot01[:, 6144:6656], (2, 4, HD))
        pc32 = view(slot01[:, 6656:7168], (16, 32))
        pcT = view(slot01[:, 7168:7680], (4, P))
        m_small = side[:, 1, 0:512]
        raw_c = view(m_small[:, 0:256], (16, 16))
        c16 = m_small[:, 256:272]
        hid = view(m_small[:, 272:336], (2, 2, 16))
        kcc = m_small[:, 336:352]
        mx = view(m_small[:, 352:368], (2, 8))
        f_c, f_abs, f_log = (view(m_small[:, 368 + 16 * n:384 + 16 * n], (HEADS, TILES)) for n in range(3))
        sums = view(m_small[:, 416:464], (3, TILES, HEADS))
        att4, att4b = m_small[:, 464:468], m_small[:, 468:472]
        f_cum = view(m_small[:, 472:488], (HEADS, TILES))
        gate48 = side[:, 0, 0:48]
        hv4 = view(side[:, 0, 64:320], (2, 4, 32))
        cumT = side[0:8, 0, 512:768]
        mix = pre
        STEPS = [(b, r) for b in (SEL, WIN, FOX) for r in range(4)]

        def pe_att_in(pe):
            pe.wait_ge(sem("T"), before(TURNS, "rn1") + 2)

            def turned(out_, w, width, cols):
                for k in range(KT):
                    m = T.matmul(out_, cols(w[:, k * width:(k + 1) * width]), xT[:, k, :], start=(k == 0), stop=(k == KT - 1))
                return m

            def plain(out_, t, w, width, c0, cn):
                for k in range(KT):
                    m = T.matmul(out_, xT[:, k, t * P:(t + 1) * P], w[:, k * width + c0:k * width + c0 + cn],
                                 start=(k == 0), stop=(k == KT - 1))
                return m

            w = take(pe, 0)
            for r in range(4):
                m = turned(ps[:, 0, r * SEQ:(r + 1) * SEQ], w, 512,
                           lambda a: a[:, r * P:(r + 1) * P])
            m.then_inc(sem("att_qn_psum"), 1)
            w = take(pe, 1)
            for g in range(2):
                turned(ps[:, 1, g * SEQ:(g + 1) * SEQ], w, 512,
                       lambda a: a[:, g * P:(g + 1) * P])
            turned(ps[:, 1, 512:768], w, 512, lambda a: a[:, 256:384])
            for t in range(TILES):
                m = plain(ps[:, 3, 512 * t:512 * t + 128], t, w, 512, 384, 128)
            m.then_inc(sem("att_in1_read"), 1)
            w = take(pe, 2)
            turned(ps[:, 1, 768:1024], w, 280, lambda a: a[:, 0:128]).then_inc(flag_up("att_kv_psum"), 1)
            w_fg = param("w_fg")
            for t in range(TILES):
                plain(ps[:, 3, 512 * t + 128:512 * t + 280], t, w, 280, 128, 152)
                m = plain(ps[:, 3, 512 * t + 280:512 * t + 288], t, w_fg, 8, 0, 8)
            m.then_inc(flag_up("att_nat_psum"), 1)
            w = take(pe, 3)
            for r in range(4):
                m = turned(ps[:, 2, r * SEQ:(r + 1) * SEQ], w, 512, lambda a: a[:, r * P:(r + 1) * P])
            m.then_inc(flag_up("att_qf_psum"), 1)
            w = take(pe, 4)
            pe.wait_ge(*flag("att_qn"))
            for r in range(4):
                m = turned(ps[:, 0, r * SEQ:(r + 1) * SEQ], w, 512, lambda a: a[:, r * P:(r + 1) * P])
            m.then_inc(sem("att_kf_psum"), 1)
            w = take(pe, 5)
            pe.wait_ge(*flag("att_kv"))
            for t in range(TILES):
                m = plain(ps[:, 1, 512 * t:512 * t + 512], t, w, 512, 0, 512)
            m.then_inc(sem("att_vf_psum"), 1)

        def v_att_in(v):
            v.wait_ge(*flag("att_kv_psum"))
            V.tensor_copy(projT[:, 4:8, :], view(ps[:, 1, :], (4, SEQ))).then_inc(flag_up("att_kv"), 1)
            v.wait_ge(*flag("att_nat_psum"))
            V.tensor_copy(nat, view(ps[:, 3, :], (TILES, 512))[:, :, 0:288]).then_inc(flag_up("att_nat"), 1)
            v.wait_ge(*flag("att_kv"))
            pe_cols = param("pe")
            for g in range(2):
                for q in range(2):
                    tokens_ = kvcT[:, g, 16 * q:16 * q + 240].rearrange("p (j i) -> p i j", i=16)
                    m = V.tensor_tensor(cmp_in[:, 16 * q:16 * q + 16, 15 * g:15 * g + 15], tokens_,
                                        spread(pe_cols[:, 16 * q:16 * q + 16], 15), ALU.add)
            m.then_inc(flag_up("cmp_in"), 1)
            v.wait_ge(*flag("att_nat"))
            b_fg = param("b_fg")[:, None, :].to_broadcast((P, TILES, HEADS))
            V.tensor_tensor(f_c.rearrange("p h t -> p t h"), nat[:, :, 280:288], b_fg, ALU.add).then_inc(flag_up("fox_f"), 1)
            v.wait_ge(sem("att_kf_psum"), 1)
            V.tensor_copy(projT[:, 12:16, :], view(ps[:, 0, :], (4, SEQ))).then_inc(flag_up("att_kf"), 1)
            v.wait_ge(*flag("fox_log"))
            V.scalar_tensor_tensor(out=f_log, in0=f_c, scalar=0.0, in1=f_log, op0=ALU.min, op1=ALU.subtract)\
             .then_inc(flag_up("fox_lf"), 1)

        def a_att_in(a):
            a.wait_ge(sem("att_qn_psum"), 1)
            A.copy(projT[:, 0:4, :], view(ps[:, 0, :], (4, SEQ))).then_inc(flag_up("att_qn"), 1)
            a.wait_ge(*flag("att_nat"))
            A.activation(view(gate48, (TILES, 24)), nat[:, :, 256:280], ACT.Sigmoid).then_inc(flag_up("att_gates"), 1)
            a.wait_ge(*flag("fox_f"))
            link(a, A.activation(f_abs, f_c, ACT.Abs), "a")
            link(a, A.activation(f_abs, f_abs, ACT.Exp, scale=-1.0), "a")
            A.activation(f_log, f_abs, ACT.Ln, bias=eps(ONE)).then_inc(flag_up("fox_log"), 1)
            a.wait_ge(*flag("att_qf_psum"))
            A.copy(projT[:, 8:12, :], view(ps[:, 2, :], (4, SEQ))).then_inc(flag_up("att_qf"), 1)
            a.wait_ge(sem("att_vf_psum"), 1)
            A.copy(vf, view(ps[:, 1, :], (TILES, 512))).then_inc(flag_up("att_vf"), 1)

        def pe_fox_bias(pe):
            lf = f_log
            pe.wait_ge(*flag("fox_lf"))
            pe.wait_ge(*flag("att_qf"))
            both = tab[:, places["table"]["upto"][0]:places["table"]["upto"][0] + 2 * P]
            T.matmul(ps[:, 2, 0:8], upto, lf[:, :, 0], start=True, stop=True)
            T.matmul(ps[:, 2, 8:16], ones, lf[:, :, 0], start=True, stop=False)
            T.matmul(ps[:, 2, 8:16], upto, lf[:, :, 1], start=False, stop=True)
            T.matmul(ps[0:8, 2, 512:768], lf[:, :, 0], both, start=True, stop=False)
            T.matmul(ps[0:8, 2, 640:768], lf[:, :, 1], upto, start=False, stop=True).then_inc(flag_up("fox_cum_psum"), 1)
            pe.wait_ge(sem("fox_cum"), 2)
            pe.wait_ge(*flag("att_kf"))
            pe.wait_ge(*flag("att_vf"))
            pick = table("pick_head")
            for h in range(HEADS):
                m = T.matmul(pair01[:, h * SEQ:(h + 1) * SEQ], pick[0:8, h * P:(h + 1) * P], cumT, start=True, stop=True)
            m.then_inc(flag_up("fox_rows_psum"), 1)

        def v_fox_bias(v):
            v.wait_ge(*flag("fox_cum_psum"))
            V.tensor_copy(f_cum.rearrange("p h t -> p t h"), view(ps[:, 2, 0:16], (TILES, HEADS))).then_inc(sem("fox_cum"), 1)
            V.tensor_copy(cumT, ps[0:8, 2, 512:768]).then_inc(sem("fox_cum"), 1)
            v.wait_ge(sem("fox_cum"), 2)
            v.wait_ge(*flag("fox_rows_psum"))
            masks = table("mask_neg")
            for h in range(HEADS):
                for t, (c0, c1) in enumerate(((0, P), (P, COLS))):
                    m = V.scalar_tensor_tensor(out=fox_bias[:, h, c0:c1], in0=pair01[:, h * SEQ:h * SEQ + c1 - c0],
                                               scalar=f_cum[:, h, t:t + 1], in1=masks[:, c0:c1],
                                               op0=ALU.subtract, op1=ALU.subtract)
            m.then_inc(flag_up("fox_bias"), 1)

        def pe_compress(pe):
            w = take(pe, 2)
            pe.wait_ge(*flag("cmp_in"))
            pe.wait_ge(sem("fox_cum"), 2)
            for i in range(32):
                for kv in range(2):
                    rows_ = slice(64 * kv, 64 * kv + 64)
                    m = T.matmul(ps[:, 2, 512 * kv:512 * kv + 30], w[rows_, i * P:(i + 1) * P], cmp_in[rows_, i, :],
                                 start=(i == 0), stop=(i == 31))
            m.then_inc(flag_up("cmp_hid_psum"), 1)
            pe.wait_ge(sem("cmp_hid"), 2)
            pe.wait_ge(*flag("cmp_hv4"))
            pe.wait_ge(*flag("att_nat"))
            for g in range(2):
                T.matmul(ps[HD * g:HD * g + HD, 3, 0:15], param("cmp2_k"), hid[:, 0, g, 0:15], start=True, stop=True)
            for g in range(2):
                m = T.matmul(ps[:, 3, 512 + HD * g:512 + HD * g + HD], hv4[:, g].rearrange("p r j -> p (r j)"), param("cmp2_v"),
                             start=True, stop=True)
            m.then_inc(flag_up("cmp_kv_psum"), 1)
            pe.wait_ge(*flag("cmp_kcc"))
            for g in range(2):
                rows_ = slice(HD * g, HD * g + HD)
                for t in range(TILES):
                    for r in range(4):
                        at = 512 * g + (4 * t + r) * 16
                        m = T.matmul(ps[:, 2, at:at + 16], qnT[rows_, r, t * P:(t + 1) * P], kcc[rows_, :], start=True, stop=True)
            m.then_inc(flag_up("cmp_score_psum"), 1)
            pe.wait_ge(*flag("cmp_prob"))
            pe.wait_ge(*flag("cmp_vblk"))
            for q in range(4):
                m = T.transpose(ps[:, 2, q * P:(q + 1) * P], pc32[:, 4 * q:4 * q + 4, :].rearrange("p r j -> p (r j)"), ident)
            m.then_inc(flag_up("cmp_pT_psum"), 1)
            pe.wait_ge(*flag("cmp_pT"))
            for t in range(TILES):
                for g in range(2):
                    m = T.matmul(ps[:, 3, 512 * t + 256 * g:512 * t + 256 * g + 256], pcT[:, 2 * g + t, :],
                                 v_blk[:, g].rearrange("p r d -> p (r d)"), start=True, stop=True)
            m.then_inc(flag_up("cmp_o_psum"), 1)

        def a_compress(a):
            a.wait_ge(*flag("cmp_clear"))
            a.wait_ge(*flag("cmp_hid_psum"))
            for kv in range(2):
                A.activation(hid[:, kv, :, 0:15], view(ps[:, 2, 512 * kv:512 * kv + 30], (2, 15)), ACT.Gelu_apprx_tanh)\
                 .then_inc(sem("cmp_hid"), 1)
            a.wait_ge(*flag("cmp_diff"))
            A.activation(raw_c, raw_c, ACT.Exp).then_inc(flag_up("cmp_exp"), 1)

        def v_compress(v):
            V.memset(m_small[:, 272:352], 0.0).then_inc(flag_up("cmp_clear"), 1)
            V.memset(pc32, 0.0).then_inc(sem("cmp_clear2"), 1)
            V.memset(hv4, 0.0).then_inc(sem("cmp_clear2"), 1)
            v.wait_ge(sem("cmp_clear2"), 2)
            v.wait_ge(*flag("cmp_clear"))
            v.wait_ge(sem("cmp_hid"), 2)
            for g in range(2):
                m = V.tensor_copy(hv4[:, g, :, 0:16], hid[:, 1, g, None, :].to_broadcast((P, 4, 16)))
            m.then_inc(flag_up("cmp_hv4"), 1)
            v.wait_ge(*flag("cmp_kv_psum"))
            V.tensor_copy(kcc[:, 0:15], ps[:, 3, 0:15]).then_inc(flag_up("cmp_kcc"), 1)
            for g in range(2):
                m = V.tensor_tensor(v_blk[:, g], ps[:, 3, None, 512 + HD * g:512 + HD * g + HD].to_broadcast((P, 4, HD)),
                                    spread(table("own_row"), HD), ALU.mult)
            m.then_inc(flag_up("cmp_vblk"), 1)
            v.wait_ge(*flag("cmp_score_psum"))
            bias, mask = view(table("cmp_bias"), (16, 16)), view(table("cmp_mask"), (16, 16))
            for g in range(2):
                m = V.scalar_tensor_tensor(out=raw_c[:, 8 * g:8 * g + 8, :], in0=view(ps[:, 2, 512 * g:512 * g + 128], (8, 16)),
                                           scalar=HD ** -0.5, in1=bias[:, 8 * g:8 * g + 8, :], op0=ALU.mult, op1=ALU.add)
            link(v, m)
            link(v, V.tensor_reduce(c16, raw_c, AX.X, ALU.max))
            V.tensor_tensor(raw_c, raw_c, spread(c16, 16), ALU.subtract).then_inc(flag_up("cmp_diff"), 1)
            v.wait_ge(*flag("cmp_exp"))
            link(v, V.tensor_tensor(raw_c, raw_c, mask, ALU.mult))
            link(v, V.tensor_reduce(c16, raw_c, AX.X, ALU.add))
            link(v, V.tensor_scalar(c16, c16, 1e-30, None, ALU.max))
            link(v, V.reciprocal(c16, c16))
            V.tensor_tensor(pc32[:, :, 0:16], raw_c, spread(c16, 16), ALU.mult).then_inc(flag_up("cmp_prob"), 1)
            v.wait_ge(*flag("cmp_pT_psum"))
            V.tensor_copy(pcT, view(ps[:, 2, 0:512], (4, P))).then_inc(flag_up("cmp_pT"), 1)
            v.wait_ge(*flag("cmp_o_psum"))
            v.wait_ge(*flag("att_gates"))
            V.tensor_tensor(mix[:, :, 0:512].rearrange("p t (h d) -> p t h d", d=HD),
                            ps[:, 3, :].rearrange("p (t h d) -> p t h d", t=TILES, d=HD),
                            gate48.rearrange("p (t h b) -> p t h b", t=TILES, b=3)[:, :, :, 0:1].to_broadcast((P, TILES, HEADS, HD)),
                            ALU.mult).then_inc(flag_up("cmp_o"), 1)

        def head_of(branch, r, half_):
            return 2 * r + half_ if branch == FOX else 4 * half_ + r

        def pe_attention(pe):
            def scores(n):
                branch, r = STEPS[n]
                if n == 0:
                    pe.wait_ge(*flag("fox_bias"))
                if n >= 2:
                    pe.wait_ge(sem("att_raw"), n - 1)
                for half_ in range(2):
                    rows_ = slice(HD * half_, HD * half_ + HD)
                    q = (qfT if branch == FOX else qnT)[rows_, r, :]
                    k = {SEL: ksT, WIN: kwT, FOX: kfT[:, r, :]}[branch][rows_, :]
                    out_ = ps[:, n % 2, 512 * half_:512 * half_ + COLS]
                    T.matmul(out_[:, 0:P], q[:, 0:P], k[:, 0:P], start=True, stop=True)
                    m = T.matmul(out_[:, P:COLS], q[:, P:SEQ], k, start=True, stop=True)
                m.then_inc(sem("att_score_psum"), 1)

            def turn(n):
                pe.wait_ge(sem("att_prob"), n + 1)
                if n >= 1:
                    pe.wait_ge(sem("att_probT"), n)
                else:
                    pe.wait_ge(*flag("cmp_pT"))
                for half_ in range(2):
                    for b in range(3):
                        at = (3 * half_ + b) * P
                        m = T.transpose(ps[:, 2, at:at + P], prob[:, n % 2, half_, b * P:(b + 1) * P], ident)
                m.then_inc(sem("att_probT_psum"), 1)

            def values(n):
                branch, r = STEPS[n]
                pe.wait_ge(sem("att_probT"), n + 1)
                if r == 0:
                    if branch == SEL:
                        pe.wait_ge(*flag("cmp_o"))
                    else:
                        pe.wait_ge(sem("att_o"), branch)
                for half_ in range(2):
                    h = head_of(branch, r, half_)

                    def val(t):
                        return vf[:, t, HD * h:HD * h + HD] if branch == FOX else \
                            nat[:, t, 128 * branch + HD * half_:128 * branch + HD * half_ + HD]

                    o0, o1 = ps[:, 3, HD * h:HD * h + HD], ps[:, 3, 512 + HD * h:512 + HD * h + HD]
                    T.matmul(o0, probT[:, n % 2, 3 * half_, :], val(0), start=True, stop=True)
                    T.matmul(o1, probT[:, n % 2, 3 * half_ + 1, :], val(0), start=True, stop=False)
                    m = T.matmul(o1, probT[:, n % 2, 3 * half_ + 2, :], val(1), start=False, stop=True)
                m.then_inc(sem("att_value_psum"), 1)

            scores(0)
            scores(1)
            for n in range(len(STEPS)):
                turn(n)
                if n + 2 < len(STEPS):
                    scores(n + 2)
                values(n)

        def v_attention(v):
            for n, (branch, r) in enumerate(STEPS):
                v.wait_ge(sem("att_score_psum"), n + 1)
                if n >= 2:
                    v.wait_ge(sem("att_probT_psum"), n - 1)
                for half_ in range(2):
                    h = head_of(branch, r, half_)
                    raw, src = prob[:, n % 2, half_, :], ps[:, n % 2, 512 * half_:512 * half_ + COLS]
                    if branch == FOX:
                        m = V.scalar_tensor_tensor(out=raw, in0=src, scalar=HD ** -0.5, in1=fox_bias[:, h, :],
                                                   op0=ALU.mult, op1=ALU.subtract)
                    else:
                        m = V.scalar_tensor_tensor(out=raw, in0=src, scalar=HD ** -0.5 * 2.0 ** (h + 1),
                                                   in1=table("neg_dist"), op0=ALU.mult, op1=ALU.add)
                m.then_inc(sem("att_raw"), 1)
                v.wait_ge(sem("att_raw"), n + 1)
                top = view(mx[:, n % 2, 0:4], (2, TILES))
                V.tensor_reduce(top[:, :, 0:1], prob[:, n % 2, :, 0:P], AX.X, ALU.max, negate=True)
                link(v, V.tensor_reduce(top[:, :, 1:2], prob[:, n % 2, :, P:COLS], AX.X, ALU.max, negate=True))
                scale = ones[:, 0:4] if branch == FOX else table("slopes")[:, 4 * r:4 * r + 4]
                V.tensor_tensor(mx[:, n % 2, 4:8], mx[:, n % 2, 0:4], scale, ALU.mult).then_inc(sem("att_top"), 1)
                if r == 2 and branch > SEL:
                    v_att_branch(v, branch - 1)
            v_att_branch(v, FOX)

        def v_att_branch(v, b):
            v.wait_ge(sem("att_prob"), 4 * b + 4)
            v.wait_ge(sem("att_o"), b + 1)
            link(v, V.reciprocal(sums[:, b], sums[:, b]))
            if b != FOX:
                gates = gate48.rearrange("p (t h b) -> p t h b", t=TILES, b=3)
                link(v, V.tensor_tensor(sums[:, b], sums[:, b], gates[:, :, :, 1 + b], ALU.mult))
            o = o_att[:, b].rearrange("p t (h d) -> p t h d", d=HD)
            dst = mix[:, :, 512:1024].rearrange("p t (h d) -> p t h d", d=HD) if b == FOX else o
            link(v, V.tensor_tensor(dst, o, sums[:, b, :, :, None].to_broadcast((P, TILES, HEADS, HD)), ALU.mult))
            if b != FOX:
                link(v, V.tensor_tensor(mix[:, :, 0:512], mix[:, :, 0:512], o_att[:, b], ALU.add))
            if b != SEL:
                v.sem_inc(sem("att_mix"), 1)

        def a_attention(a):
            def turn(n):
                a.wait_ge(sem("att_probT_psum"), n + 1)
                if n >= 2:
                    a.wait_ge(sem("att_value_psum"), n - 1)
                A.copy(probT[:, n % 2], view(ps[:, 2, 0:768], (6, P))).then_inc(sem("att_probT"), 1)

            def out_of(branch):
                a.wait_ge(sem("att_value_psum"), 4 * branch + 4)
                A.copy(o_att[:, branch], view(ps[:, 3, :], (TILES, 512))).then_inc(sem("att_o"), 1)

            for n, (branch, r) in enumerate(STEPS):
                if r == 1 and branch > SEL:
                    out_of(branch - 1)
                a.wait_ge(sem("att_top"), n + 1)
                for half_ in range(2):
                    h = head_of(branch, r, half_)
                    for t, (c0, c1) in enumerate(((0, P), (P, COLS))):
                        m = A.activation(prob[:, n % 2, half_, c0:c1], prob[:, n % 2, half_, c0:c1], ACT.Exp,
                                         bias=mx[:, n % 2, 4 + 2 * half_ + t:5 + 2 * half_ + t],
                                         scale=1.0 if branch == FOX else 2.0 ** -(h + 1),
                                         accum_out=sums[:, branch, t, h:h + 1])
                m.then_inc(sem("att_prob"), 1)
                if n >= 1:
                    turn(n - 1)
            turn(len(STEPS) - 1)
            out_of(FOX)

        def v_att_mix(v):
            v.wait_ge(*flag("att_rms"))
            link(v, V.reciprocal(att4b, att4))
            g = row(v, "gn")
            for t in range(TILES):
                for q in range(2):
                    part = mix[:, t, 512 * q:512 * q + 512]
                    m = V.scalar_tensor_tensor(out=part, in0=part, scalar=att4b[:, 2 * t + q:2 * t + q + 1],
                                               in1=g[:, 512 * q:512 * q + 512], op0=ALU.mult, op1=ALU.mult)
                m.then_inc(sem("att_y"), 1)
            v.wait_ge(sem("att_y"), TILES)
            v.sem_inc(sem("row_used"), 1)

        def a_att_mix(a):
            for q in range(2):
                a.wait_ge(sem("att_mix"), q + 1)
                for t in range(TILES):
                    m = A.activation(o_att[:, q, t, :], mix[:, t, 512 * q:512 * q + 512], ACT.Square,
                                     accum_out=att4[:, 2 * t + q:2 * t + q + 1])
            link(a, m, "a")
            A.activation(att4, att4, ACT.Sqrt, bias=eps(EPS6), scale=1.0 / 512).then_inc(flag_up("att_rms"), 1)

        def v_add_product(v, tag, done, pairs):
            for t in range(TILES):
                v.wait_ge(sem(done), t + 1)
                V.tensor_tensor(x[:, t, :], x[:, t, :], ps[:, pairs[t], :], ALU.add).then_inc(sem(f"{tag}_x"), 1)
            v.wait_ge(sem(f"{tag}_x"), TILES)

        R = side[:, 1, :]
        logit = view(R[:, 0:64], (TILES, EXPERTS))
        chosen = view(R[:, 64:128], (TILES, EXPERTS))
        weight = view(R[:, 128:192], (TILES, EXPERTS))
        rank = view(R[:, 192:256], (TILES, EXPERTS))
        top8 = view(R[:, 256:272], (TILES, 8))
        neg_top = R[:, 272:274]
        wsum = R[:, 274:276]
        count_f = R[:, 276:277]
        b_down_sb = arena[0:EXPERTS, 7168:8192]
        w_ple2 = xT[:].rearrange("p k t -> p (k t)")
        weightT = side[0:EXPERTS, 0, 0:SEQ]
        count_i = sb("count_i", [P, 2], I32)

        def pe_router(pe):
            w = view(param("w_router"), (KT, EXPERTS))
            pe.wait_ge(sem("T"), before(TURNS, "rn2") + 2)
            for t in range(TILES):
                for k in range(KT):
                    m = T.matmul(ps[:, 2, EXPERTS * t:EXPERTS * (t + 1)], xT[:, k, t * P:(t + 1) * P], w[:, k, :],
                                 start=(k == 0), stop=(k == KT - 1))
            m.then_inc(flag_up("router_psum"), 1)
            pe.wait_ge(*flag("router_chosen"))
            strict = table("strict")
            T.matmul(ps[:, 2, 512:544], strict, chosen[:, 0, :], start=True, stop=True)
            T.matmul(ps[:, 2, 544:576], ones, chosen[:, 0, :], start=True, stop=False)
            T.matmul(ps[:, 2, 544:576], strict, chosen[:, 1, :], start=False, stop=True)
            T.matmul(ps[:, 2, 576:608], ones, chosen[:, 0, :], start=True, stop=False)
            T.matmul(ps[:, 2, 576:608], ones, chosen[:, 1, :], start=False, stop=True).then_inc(flag_up("router_rank_psum"), 1)
            pe.wait_ge(*flag("router_weight"))
            for t in range(TILES):
                m = T.transpose(ps[0:EXPERTS, 3, t * P:(t + 1) * P], weight[:, t, :], ident)
            m.then_inc(flag_up("router_wT_psum"), 1)

        def pe_down_bias(pe):
            pe.wait_ge(*flag("router_wT"))
            pe.wait_ge(sem("b_down_loaded"), 16)
            for t in range(TILES):
                for half_ in range(2):
                    m = T.matmul(pair01[:, t * D + half_ * 512:t * D + half_ * 512 + 512], weightT[:, t * P:(t + 1) * P],
                                 b_down_sb[:, half_ * 512:half_ * 512 + 512], start=True, stop=True)
            m.then_inc(flag_up("router_bias_psum"), 1)

        def v_router(v):
            v.wait_ge(*flag("router_psum"))
            for t in range(TILES):
                m = V.tensor_tensor(logit[:, t, :], ps[:, 2, EXPERTS * t:EXPERTS * (t + 1)], param("b_router"), ALU.add)
            link(v, m)
            for t in range(TILES):
                m = V.max(top8[:, t, :], logit[:, t, :])
            link(v, m)
            V.tensor_scalar(neg_top, top8[:, :, 0], -1.0, None, ALU.mult).then_inc(flag_up("router_top"), 1)
            v.wait_ge(*flag("router_top"))
            link(v, V.memset(top8[:, :, TOP_K:8], 3e38))
            for t in range(TILES):
                m = V.match_replace(chosen[:, t, :], top8[:, t, :], logit[:, t, :], -3e38)
            link(v, m)
            V.tensor_tensor(chosen, chosen, logit, ALU.not_equal).then_inc(flag_up("router_chosen"), 1)
            v.wait_ge(*flag("router_chosen"))
            v.wait_ge(sem("router_exp"), TILES)
            link(v, V.tensor_tensor(weight, weight, chosen, ALU.mult))
            link(v, V.tensor_reduce(wsum, weight, AX.X, ALU.add))
            link(v, V.reciprocal(wsum, wsum))
            V.tensor_tensor(weight, weight, spread(wsum, EXPERTS), ALU.mult).then_inc(flag_up("router_weight"), 1)
            v.wait_ge(*flag("router_rank_psum"))
            link(v, V.scalar_tensor_tensor(out=rank, in0=view(ps[:, 2, 512:576], (TILES, EXPERTS)), scalar=1.0, in1=chosen,
                                           op0=ALU.add, op1=ALU.mult))
            V.tensor_scalar(rank, rank, -1.0, None, ALU.add).then_inc(flag_up("router_rank"), 1)
            link(v, V.tensor_reduce(count_f, ps[:, 2, 576:608], AX.X, ALU.max))
            V.tensor_copy(count_i[:, 0:1], count_f).then_inc(flag_up("router_count"), 1)
            v.wait_ge(*flag("router_wT_psum"))
            V.tensor_copy(weightT, ps[0:EXPERTS, 3, 0:SEQ]).then_inc(flag_up("router_wT"), 1)
            v.wait_ge(*flag("router_rank"))

        def v_down_bias(v):
            v.wait_ge(*flag("router_bias_psum"))
            V.tensor_tensor(x[:], x[:], ps[:, 0:2, :], ALU.add).then_inc(flag_up("router_x"), 1)
            v.wait_ge(*flag("router_x"))

        def a_router(a):
            a.wait_ge(*flag("router_top"))
            for t in range(TILES):
                A.activation(weight[:, t, :], logit[:, t, :], ACT.Exp, bias=neg_top[:, t:t + 1]).then_inc(sem("router_exp"), 1)

        def pe_ple2(pe):
            pe.wait_ge(*flag("moe_end"))
            pe.wait_ge(sem("ple2_loaded"), 16)
            for t in range(TILES):
                for half_ in range(2):
                    for k in range(2):
                        at = k * D + half_ * 512
                        m = T.matmul(ps[:, 2 + t, half_ * 512:half_ * 512 + 512], pleT[:, 2, k, t * P:(t + 1) * P],
                                     w_ple2[:, at:at + 512], start=(k == 0), stop=(k == 1))
            m.then_inc(flag_up("ple2_psum"), 1)

        up_bias = scratch(0, 2, 2, STEP)
        xs_high, xs_low = split_scratch(2048, KT, P), split_scratch(3072, KT, P)
        e_up, e_act = scratch(4096, 2, 2, STEP), scratch(6144, 2, STEP)
        actT_high, actT_low = split_scratch(7168, 2, 4, P), split_scratch(8192, 2, 4, P)
        onehotT = split_scratch(9472, TILES, P)
        y_high, y_low = row_split[:, places["row"]["ln2"] % 3, :], side_split[:, 0, :]
        onehot = view(R[:, 512:768], (TILES, P))
        onehot_add = view(R[:, 768:1024], (TILES, P))
        bias_rows = expert_b.rearrange("e (m j f) -> e j m f", m=2, j=2)

        CHUNKS, BUFFERS = 24, 6
        HALVES, HALF_SLOTS = 12, 6
        USES = 8 * (EXPERTS - 1) - 2 + 6 + 4
        POOL_CHUNKS = (5, 11, 18, 24)
        SPLIT_SLOT = 3

        def raw_chunk(c):
            at = (c // 2) % HALF_SLOTS * HALF + (c % 2) * CHUNK
            return ring_flat[:, at:at + CHUNK]

        def uses_before(e):
            return 8 * e - 2

        def sp_expert(sp, n, e, first=False):
            for h in range(HALVES):
                slot = h % HALF_SLOTS
                if not first or h >= HALF_SLOTS:
                    sp.wait_ge(sem(f"moe{n}_low"), CHUNKS * e + 2 * (h + 1 - HALF_SLOTS))
                elif n == 1:
                    sp.wait_ge(sem("moe0_low"), CHUNKS * EXPERTS)
                elif h == 0:
                    sp.wait_ge(sem("att_y"), TILES)
                sp.dma_start(ring_flat[:, slot * HALF:(slot + 1) * HALF], experts[e, h // 2, :, (h % 2) * HALF:(h % 2 + 1) * HALF])\
                  .then_inc(sem(f"moe{n}_full{slot}"), 16)
                if h in (3, 7):
                    j = h // 4
                    if not first:
                        sp.wait_ge(sem(f"moe{n}_biased"), 2 * e + j - 1)
                    elif n == 1:
                        sp.wait_ge(sem("moe0_biased"), 2 * EXPERTS)
                    sp.dma_start(up_bias[:, j], bias_rows[e, j].partition_broadcast(P))\
                      .then_inc(sem(f"moe{n}_bias{j}"), 16)

        def sp_experts(sp, n):
            sp_expert(sp, n, 0, first=True)
            with sp.Fori(1, EXPERTS) as e:
                sp_expert(sp, n, e)

        def pe_experts(pe, n):
            s = lambda k: sem(f"moe{n}_{k}")

            def bank(u, base=0):
                pe.wait_ge(s("emptied"), base + u - 1)
                return ps[:, 3, 512 * (u % 2):512 * (u % 2) + 512]

            def chunk(e, c, out_, high, low, k0, start, stop):
                pe.wait_ge(s("low"), CHUNKS * e + c + 1)
                for k in range(2):
                    ins = split_product(out_, high[:, k0 + k, :], low[:, k0 + k, :], split_buffer(SPLIT_SLOT, c % BUFFERS), k,
                                        start and k == 0, stop and k == 1)
                ins.then_inc(s("product"), 1)

            def up(e, j, m, first=False, chunks=(0, 1, 2, 3)):
                if m == 0 and chunks[0] == 0:
                    if j == 0:
                        pe.wait_ge(s("emptied"), 2 if first else uses_before(e))
                    if not first:
                        if j == 0:
                            pe.wait_ge(s("wT"), e)
                        else:
                            pe.wait_ge(s("act"), 2 * e)
                for c in chunks:
                    chunk(e, 8 * j + 4 * m + c, ps[:, j, 512 * m:512 * m + 512], xs_high, xs_low, 2 * c, c == 0, c == 3)

            def turn(e, j, out_):
                pe.wait_ge(s("act"), 2 * e + j + 1)
                for k in range(4):
                    ins = T.transpose(out_[:, k * P:(k + 1) * P], e_act[:, j, k * P:(k + 1) * P], ident)
                ins.then_inc(s("used"), 1)

            def add(e_next, c, out_):
                if c == 0:
                    pe.wait_ge(s("y"), e_next)
                    pe.wait_ge(s("wT"), e_next)
                part = slice((c % 2) * 512, (c % 2) * 512 + 512)
                T.matmul(out_, onehotT[:, c // 2, :], y_high[:, part], start=True, stop=False)
                T.matmul(out_, onehotT[:, c // 2, :], y_low[:, part], start=False, stop=True).then_inc(s("used"), 1)

            def gather(e, c, out_):
                if c == 0:
                    pe.wait_ge(s("onehot"), e + 1)
                for k in range(4):
                    for t in range(TILES):
                        at = (4 * c + k) * P
                        ins = T.matmul(out_[:, k * P:(k + 1) * P], pre[:, t, at:at + P], onehot[:, t, :],
                                       start=(t == 0), stop=(t == 1))
                ins.then_inc(s("used"), 1)

            def turn_onehot(e):
                pe.wait_ge(s("onehot_add"), e + 1)
                for t in range(TILES):
                    ins = T.transpose(ps[:, 0, t * P:(t + 1) * P], onehot_add[:, t, :], ident)
                ins.then_inc(s("wT_psum"), 1)

            def down(e, j, turned, first=False, chunks=(0, 1, 2, 3)):
                pe.wait_ge(s("emptied"), turned)
                if j == 0 and not first:
                    pe.wait_ge(s("y"), e)
                for c in chunks:
                    half_, k0 = c // 2, 2 * (c % 2)
                    chunk(e, 16 + 4 * j + c, ps[:, 2, 512 * half_:512 * half_ + 512], actT_high[:, j], actT_low[:, j], k0,
                          j == 0 and k0 == 0, j == 1 and k0 == 2)

            def expert(e, first=False, last=False):
                b = 2 if first else uses_before(e)
                u = 0 if first else 2
                up(e, 0, 0, first)
                up(e, 0, 1, first)
                if not first:
                    add(e, 0, bank(0, b))
                    add(e, 1, bank(1, b))
                up(e, 1, 0, first)
                up(e, 1, 1, first, (0, 1))
                turn(e, 0, bank(u, b))
                up(e, 1, 1, first, (2, 3))
                if not first:
                    add(e, 2, bank(3, b))
                    add(e, 3, bank(4, b))
                turn_onehot(e)
                turned = b + u + 1
                down(e, 0, turned, first, (0, 1))
                u = 1 if first else 5
                if not last:
                    gather(e + 1, 0, bank(u, b))
                    u += 1
                down(e, 0, turned, first, (2, 3))
                turn(e, 1, bank(u, b))
                if not last:
                    gather(e + 1, 1, bank(u + 1, b))
                down(e, 1, b + u + 1)

            if n == 0:
                pe.wait_ge(*flag("router_rank"))
                pe.wait_ge(*flag("router_count"))
                pe.wait_ge(*flag("router_wT"))
            else:
                pe.wait_ge(sem("moe0_emptied"), USES)
            gather(0, 0, ps[:, 3, 0:512])
            gather(0, 1, ps[:, 3, 512:1024])
            if n == 0:
                pe_down_bias(pe)
                pe.wait_ge(*flag("router_x"))
            expert(0, first=True)
            with pe.Fori(1, EXPERTS - 1) as e:
                expert(e)
            expert(EXPERTS - 1, last=True)
            for c in range(4):
                add(EXPERTS, c, bank(6 + c, uses_before(EXPERTS - 1)))

        def v_experts(v, n):
            s = lambda k: sem(f"moe{n}_{k}")
            def bank(u, base=0):
                v.wait_ge(s("used"), base + u + 1)
                return ps[:, 3, 512 * (u % 2):512 * (u % 2) + 512]

            def low(e, *chunks):
                for c in chunks:
                    v.wait_ge(s("high"), CHUNKS * e + c + 1)
                    after_pool = c - 1 in POOL_CHUNKS
                    if after_pool:
                        v.wait_ge(s("low_pool"), len(POOL_CHUNKS) * e + POOL_CHUNKS.index(c - 1) + 1)
                    high, low_ = split_buffer(SPLIT_SLOT, c % BUFFERS)
                    V.tensor_tensor(low_, raw_chunk(c), high, ALU.subtract).then_inc(s("low"), 2 if after_pool else 1)

            slot_numbers = table("slot_no" if n == 0 else "slot_no2")

            def one_hot(e):
                for t in range(TILES):
                    ins = V.tensor_scalar(onehot[:, t, :], slot_numbers, rank[:, t, bass.ds(e, 1)], None, ALU.is_equal)
                ins.then_inc(s("onehot"), 1)

            def biased(e, j):
                v.wait_ge(s("product"), CHUNKS * e + 8 * j + 8)
                v.wait_ge(s(f"bias{j}"), 16 * e + 16)
                V.tensor_tensor(e_up[:, j].rearrange("p m f -> p (m f)"), ps[:, j, :],
                                up_bias[:, j].rearrange("p m f -> p (m f)"), ALU.add).then_inc(s("biased"), 1)

            def clip(e, j):
                gate, lin = e_up[:, j, 0, :], e_up[:, j, 1, :]
                v.wait_ge(s("biased"), 2 * e + j + 1)
                V.tensor_scalar(gate, gate, LIMIT, None, ALU.min).then_inc(s("gate"), 1)
                V.tensor_scalar(lin, lin, LIMIT, -LIMIT, ALU.min, ALU.max).then_inc(s("lin"), 1)

            def keep_low(low_, src, high, kept):
                v.wait_ge(s("kept"), kept)
                V.tensor_tensor(low_, view(src, (4, P)), high, ALU.subtract).then_inc(s("emptied"), 1)

            def add(e, c, src):
                part = x[:, c // 2, (c % 2) * 512:(c % 2) * 512 + 512]
                V.scalar_tensor_tensor(out=part, in0=src, scalar=weight[:, c // 2, bass.ds(e, 1)], in1=part,
                                       op0=ALU.mult, op1=ALU.add).then_inc(s("emptied"), 1)

            def keep_onehot(e):
                v.wait_ge(s("wT_psum"), e + 1)
                V.tensor_copy(onehotT, view(ps[:, 0, 0:256], (2, P))).then_inc(s("wT"), 1)

            def results_low(e):
                v.wait_ge(s("y_high"), e + 1)
                V.tensor_tensor(y_low, ps[:, 2, :], y_high, ALU.subtract).then_inc(s("y"), 1)

            def expert(e, first=False, last=False):
                b = 2 if first else uses_before(e)
                kept = 4 * e + 2
                v.wait_ge(s("emptied"), b)
                if not first:
                    results_low(e - 1)
                low(e, 6, 7, 8, 9, 10)
                biased(e, 0)
                if not first:
                    add(e - 1, 0, bank(0, b))
                    add(e - 1, 1, bank(1, b))
                clip(e, 0)
                low(e, 12, 13)
                V.tensor_copy(onehot_add, onehot).then_inc(s("onehot_add"), 1)
                if not last:
                    v.wait_ge(s("onehot_add"), e + 1)
                    one_hot(e + 1)
                low(e, 14, 15, 16)
                u = 0 if first else 2
                keep_low(actT_low[:, 0], bank(u, b), actT_high[:, 0], kept + 1)
                low(e, 17, 19)
                biased(e, 1)
                clip(e, 1)
                if not first:
                    add(e - 1, 2, bank(3, b))
                    add(e - 1, 3, bank(4, b))
                low(e, 20, 21)
                keep_onehot(e)
                low(e, 22)
                u = 1 if first else 5
                if not last:
                    keep_low(xs_low[:, 0:4], bank(u, b), xs_high[:, 0:4], kept + 2)
                    u += 1
                low(e, 23)
                keep_low(actT_low[:, 1], bank(u, b), actT_high[:, 1], kept + (2 if last else 3))
                if not last:
                    keep_low(xs_low[:, 4:8], bank(u + 1, b), xs_high[:, 4:8], kept + 4)
                    low(e, 25, 26, 27, 28)

            one_hot(0)
            keep_low(xs_low[:, 0:4], bank(0), xs_high[:, 0:4], 1)
            keep_low(xs_low[:, 4:8], bank(1), xs_high[:, 4:8], 2)
            low(0, 0)
            if n == 0:
                v_down_bias(v)
            low(0, 1, 2, 3, 4)
            expert(0, first=True)
            with v.Fori(1, EXPERTS - 1) as e:
                expert(e)
            expert(EXPERTS - 1, last=True)
            results_low(EXPERTS - 1)
            v.wait_ge(s("emptied"), uses_before(EXPERTS - 1) + 6)
            for c in range(4):
                add(EXPERTS - 1, c, bank(6 + c, uses_before(EXPERTS - 1)))
            v.wait_ge(s("emptied"), USES)

        def pool_experts(pool, n):
            s = lambda k: sem(f"moe{n}_{k}")

            def act(e, j):
                gate, lin = e_up[:, j, 0, :], e_up[:, j, 1, :]
                pool.wait_ge(s("lin"), 2 * e + j + 1)
                G.tensor_tensor(view(lin, (4, P)), view(lin, (4, P)), repeat(ones, 4), ALU.add).then_inc(s("lin_plus"), 1)
                pool.wait_ge(s("lin_plus"), 2 * e + j + 1)
                pool.wait_ge(s("gate"), 2 * e + j + 1)
                G.tensor_tensor(lin, lin, gate, ALU.mult).then_inc(s("lin_gate"), 1)
                pool.wait_ge(s("lin_gate"), 2 * e + j + 1)
                pool.wait_ge(s("sigmoid"), 2 * e + j + 1)
                G.tensor_tensor(e_act[:, j, :], e_act[:, j, :], lin, ALU.mult).then_inc(s("act"), 1)

            def low(e, c):
                pool.wait_ge(s("high"), CHUNKS * e + c + 1)
                high, low_ = split_buffer(SPLIT_SLOT, c % BUFFERS)
                G.tensor_tensor(low_, raw_chunk(c), high, ALU.subtract).then_inc(s("low_pool"), 1)

            def expert(e, last=False):
                low(e, 5)
                low(e, 11)
                act(e, 0)
                low(e, 18)
                act(e, 1)
                if not last:
                    low(e, 24)

            expert(0)
            with pool.Fori(1, EXPERTS - 1) as e:
                expert(e)
            expert(EXPERTS - 1, last=True)

        def a_experts(a, n):
            s = lambda k: sem(f"moe{n}_{k}")

            def high(e, *chunks, first=False):
                for c in chunks:
                    if c % 2 == 0:
                        h = c // 2
                        a.wait_ge(s(f"full{h % HALF_SLOTS}"), 16 * (2 * e + h // HALF_SLOTS + 1))
                    if c >= BUFFERS or (c == BUFFERS - 1 and not first):
                        a.wait_ge(s("product"), CHUNKS * e + c - BUFFERS + 1)
                    A.copy(split_buffer(SPLIT_SLOT, c % BUFFERS)[0], raw_chunk(c)).then_inc(s("high"), 1)

            def sigmoid(e, j):
                a.wait_ge(s("gate"), 2 * e + j + 1)
                A.activation(e_act[:, j, :], e_up[:, j, 0, :], ACT.Sigmoid, scale=1.702).then_inc(s("sigmoid"), 1)

            def keep_high(dst, u, base):
                a.wait_ge(s("used"), base + u + 1)
                A.copy(dst, view(ps[:, 3, 512 * (u % 2):512 * (u % 2) + 512], (4, P))).then_inc(s("kept"), 1)

            def results_high(e, first=False):
                a.wait_ge(s("product"), CHUNKS * e + CHUNKS)
                if not first:
                    a.wait_ge(s("used"), uses_before(e) + 5)
                A.copy(y_high, ps[:, 2, :]).then_inc(s("y_high"), 1)

            def expert(e, first=False, last=False, second=False):
                b = 2 if first else uses_before(e)
                if not first:
                    results_high(e - 1, first=second)
                high(e, 5, 6, 7, 8, 9, 10, 11, 12, 13, first=first)
                sigmoid(e, 0)
                high(e, 14, 15, 16, 17, 18, 19)
                keep_high(actT_high[:, 0], 0 if first else 2, b)
                high(e, 20, 21)
                sigmoid(e, 1)
                high(e, 22, 23)
                u = 1 if first else 5
                if not last:
                    keep_high(xs_high[:, 0:4], u, b)
                    high(e, 24, 25)
                    u += 1
                keep_high(actT_high[:, 1], u, b)
                if not last:
                    keep_high(xs_high[:, 4:8], u + 1, b)
                    high(e, 26, 27, 28)

            if n == 0:
                a.wait_ge(sem("att_out_psum"), TILES)
            else:
                a.wait_ge(sem("moe0_emptied"), USES)
            keep_high(xs_high[:, 0:4], 0, 0)
            keep_high(xs_high[:, 4:8], 1, 0)
            high(0, 0, 1, 2, 3, 4)
            expert(0, first=True)
            expert(1, second=True)
            with a.Fori(2, EXPERTS - 1) as e:
                expert(e)
            expert(EXPERTS - 1, last=True)
            results_high(EXPERTS - 1)

        def second_pass(eng, program):
            eng.wait_ge(*flag("router_count"))
            most = eng.value_load(count_i[0:1, 0:1])
            with eng.If(most > P):
                program(eng, 1)

        def v_final(v):
            b = TILES * 2
            v_rms_norm(v, "rnp", "ln_ple")
            v_transpose(v, "rnp")
            for t in range(TILES):
                v.wait_ge(sem("ple_gate"), b + t + 1)
                link(v, V.tensor_tensor(side[:, t, :], side[:, t, :], pre[:, t, :], ALU.mult))
                V.tensor_tensor(x[:, t, :], x[:, t, :], side[:, t, :], ALU.add).then_inc(sem("last_x"), 1)
            v_rms_norm(v, "rnf", "ln_f")

        def a_final(a):
            a.wait_ge(*flag("moe_end"))
            a_rms_norm(a, "rnp", None, 0)
            a.wait_ge(*flag("ple2_psum"))
            A.copy(side[:], ps[:, 2:4, :]).then_inc(flag_up("ple2_side"), 1)
            a_transpose(a, "rnp")
            for t in range(TILES):
                a.wait_ge(sem("ple_gate_psum"), TILES * 2 + t + 1)
                A.activation(pre[:, t, :], ps[:, 2 + t, :], ACT.Sigmoid).then_inc(sem("ple_gate"), 1)
            a_rms_norm(a, "rnf", "last_x", 0)
            for t in range(TILES):
                a.wait_ge(sem("norm_x"), before(NORMS, "rnf") + t + 1)
                a.dma_start(out[:, t, :], pre[:, t, :]).then_inc(sem("out_stored"), 16)
            a.wait_ge(sem("out_stored"), 16 * TILES)

        block = ctx.enter_context(nc.Block())

        @block.sync
        def _(sp):
            sp_constants(sp)
            fill(sp, "mlp0_up0", 0)
            fill(sp, "mlp0_down0", 1)
            fill(sp, "mlp0_up1", 2, "ple_gate_psum", 2)
            fill(sp, "mlp0_down1", 3)
            sp_mlp(sp, 0)
            sp_after_mlp(sp, 0, [f"gdn_in{n}" for n in range(6)])
            for n in range(6, 8):
                fill(sp, f"gdn_in{n}", n - 2, "gdn_in_psum", n - 1)
            fill(sp, "gdn_out0", 4, "gdn_z_psum", 1)
            fill(sp, "gdn_out1", 5, "gdn_z_psum", 2)
            fill(sp, "gate10", 2, "gdn_y", 2)
            fill(sp, "gate11", 3)
            fill(sp, "mlp1_up0", 0)
            fill(sp, "mlp1_down0", 1)
            fill(sp, "proj1", 5, "gdn_out_psum", 2, width=2048)
            fill(sp, "mlp1_up1", 2, "ple_gate_psum", 4)
            fill(sp, "mlp1_down1", 3)
            sp_mlp(sp, 1)
            sp_after_mlp(sp, 1, [f"att_in{n}" for n in range(6)])
            sp.wait_ge(*flag("att_nat_psum"))
            fill(sp, "cmp", 2)
            fill(sp, "att_out0", 4, "att_kf_psum", 1)
            fill(sp, "att_out1", 5, "att_vf_psum", 1)
            sp.wait_ge(sem("att_y"), TILES)
            sp.dma_start(b_down_sb, b_down).then_inc(sem("b_down_loaded"), 16)
            sp_experts(sp, 0)
            sp.wait_ge(*flag("router_psum"))
            sp.dma_start(w_ple2, weights[places["unit"]["ple2"], :, 0:2048]).then_inc(sem("ple2_loaded"), 16)
            second_pass(sp, sp_experts)
            sp.wait_ge(*flag("moe_end"))
            fill(sp, "gate20", 0)
            fill(sp, "gate21", 1)

        @block.gpsimd
        def _(pool):
            before_z = places["row"]["gate_b1"] + 1
            pool_rows(pool, 0, before_z)
            pool_gdn_z(pool)
            pool_rows(pool, before_z, len(places["row"]) - len(EARLY))
            pool_experts(pool, 0)
            second_pass(pool, pool_experts)

        @block.tensor
        def _(pe):
            pe_pool(pe)
            pe.wait_ge(sem("tables_loaded"), 16)
            pe_transpose(pe, "ln00", x, "norm_x", before(NORMS, "ln00"))
            pe.wait_ge(sem("ple_loaded"), 16)
            pe.wait_ge(sem("proj0_loaded"), 16)
            pe_ple(pe, "ln00", 0, (2, 3), 5, 2048, proj_taken=True)
            pe_mlp(pe, 0)
            pe_transpose(pe, "ln01", x, "norm_x", before(NORMS, "ln01"))
            pe_gdn_in(pe)
            pe_gdn_norms(pe)
            pe_gdn_scores(pe)
            pe_gdn_inverse(pe)
            pe_gdn_out(pe)
            pe_transpose(pe, "gdny", pre, "gdn_y")
            pe.wait_ge(sem("T"), before(TURNS, "gdny") + 2)
            pe_dense(pe, "gdn_out_psum", (2, 3), (4, 5))
            pe_transpose(pe, "ln10", x, "norm_x", before(NORMS, "ln10"))
            pe_ple(pe, "ln10", 1, (2, 3), 5, 0)
            pe_mlp(pe, 1)
            pe_transpose(pe, "rn1", pre, "norm_x", before(NORMS, "rn1"))
            pe_att_in(pe)
            pe_fox_bias(pe)
            pe_compress(pe)
            pe_attention(pe)
            pe_transpose(pe, "att", mix, "att_y")
            pe.wait_ge(sem("T"), before(TURNS, "att") + 2)
            pe_dense(pe, "att_out_psum", (2, 3), (4, 5))
            pe_transpose(pe, "rn2", pre, "norm_x", before(NORMS, "rn2"))
            pe_router(pe)
            pe_experts(pe, 0)
            second_pass(pe, pe_experts)
            pe_ple2(pe)
            pe_transpose(pe, "rnp", pre, "norm_x", before(NORMS, "rnp"))
            pe.wait_ge(sem("T"), before(TURNS, "rnp") + 2)
            pe.wait_ge(*flag("ple2_side"))
            pe_dense(pe, "ple_gate_psum", (2, 3), (0, 1))

        @block.vector
        def _(v):
            v.wait_ge(sem("pool_T_psum"), 1)
            V.tensor_copy(xT[:, 0:4, :], view(ps[:, 0, :], (4, SEQ))).then_inc(sem("pool_T"), 1)
            v_pool(v)
            v_layer_norm(v, "ln00", pre, "gain00", "bias00")
            v_transpose(v, "ln00")
            v_mlp_x(v, 0)
            v_ple(v, 0)
            v_mlp(v, 0)
            v_layer_norm(v, "ln01", pre, "gain01", "bias01")
            v_transpose(v, "ln01")
            v_gdn_in(v)
            v_gdn_scores(v)
            v_gdn_inverse(v)
            v_gdn_out(v)
            v_transpose(v, "gdny")
            v_residual(v, "gdn_out_psum", (2, 3), ALPHA)
            v_layer_norm(v, "ln10", pre, "gain10", "bias10")
            v_transpose(v, "ln10")
            v_mlp_x(v, 1)
            v_ple(v, 1)
            v_mlp(v, 1)
            v_layer_norm(v, "ln11", pre, "gain11", "bias11")
            v_rms_norm(v, "rn1", "ln1")
            v_transpose(v, "rn1")
            v_att_in(v)
            v_fox_bias(v)
            v_compress(v)
            v_attention(v)
            v_att_mix(v)
            v_transpose(v, "att")
            v_add_product(v, "att_out", "att_out_psum", (2, 3))
            v_rms_norm(v, "rn2", "ln2")
            v_transpose(v, "rn2")
            v_router(v)
            v_experts(v, 0)
            second_pass(v, v_experts)
            v.sem_inc(flag_up("moe_end"), 1)
            v_final(v)

        @block.scalar
        def _(a):
            a.wait_ge(sem("pool_T_psum"), 2)
            A.copy(xT[:, 4:8, :], view(ps[:, 1, :], (4, SEQ))).then_inc(sem("pool_T"), 1)
            a.wait_ge(sem("tables_loaded"), 16)
            a_layer_norm(a, "ln00")
            a_transpose(a, "ln00")
            a_mlp_x(a, "ln00", 0)
            a_ple(a, 0)
            a_mlp(a, 0)
            a_layer_norm(a, "ln01")
            a_transpose(a, "ln01")
            a_gdn_in(a)
            a_gdn_scores(a)
            a_gdn_inverse(a)
            a_gdn_out(a)
            a_transpose(a, "gdny")
            a_layer_norm(a, "ln10")
            a_transpose(a, "ln10")
            a_mlp_x(a, "ln10", 1)
            a_ple(a, 1)
            a_mlp(a, 1)
            a_layer_norm(a, "ln11")
            a_rms_norm(a, "rn1", "norm_x", before(NORMS, "ln11"))
            a_transpose(a, "rn1")
            a_att_in(a)
            a_compress(a)
            a_attention(a)
            a_att_mix(a)
            a_transpose(a, "att")
            a_rms_norm(a, "rn2", "att_out_x", 0)
            a_transpose(a, "rn2")
            a_router(a)
            a_experts(a, 0)
            second_pass(a, a_experts)
            a_final(a)


def kernel(**inputs):
    import concourse.bacc as bacc
    from concourse.bass_utils import run_bass_kernel_spmd

    arrays, places = lay_out(inputs)
    nc = bacc.Bacc("TRN2", target_bir_lowering=False, num_devices=1)
    args = {n: nc.dram_tensor(f"{n}_dram", a.shape, F32, kind="ExternalInput").ap() for n, a in arrays.items()}
    out = nc.dram_tensor("out_dram", (P, TILES, D), F32, kind="ExternalOutput").ap()
    build(nc, places, out=out, **args)
    r = run_bass_kernel_spmd(nc, [{f"{n}_dram": a for n, a in arrays.items()}], core_ids=[0])
    return r.results[0]["out_dram"].transpose(1, 0, 2).reshape(1, SEQ, D)
```
